# Optimizing a Trainium2 kernel written in Bass

```python
import jax, jax.numpy as jnp
from jax import lax
import numpy as np

D_MODEL = 1024
BATCH = 1
SEQ = 512
DEPTH = 1

GRID_W = 64
CTX_LEN = 256
D_MIX = D_MODEL
ML_HEADS = 4
ML_HEAD_DIM = 128
ML_WIDTH = ML_HEADS * ML_HEAD_DIM
HG_HEADS = 4
HG_HEAD_DIM = 128
HG_WIDTH = HG_HEADS * HG_HEAD_DIM
ML_COLS = 4 * ML_WIDTH + 4 * ML_HEADS
HG_COLS = 5 * HG_WIDTH
IN_COLS = ML_COLS + HG_COLS
CONV_W = 3
D_FF = 2816
ML_CHUNK = 64
HG_CHUNK = 32
N_MOD = 6
EPS = 1e-6


F32 = jnp.float32

def _rmsnorm(x, w):
    xf = x.astype(F32)
    y = xf * lax.rsqrt(jnp.mean(xf * xf, axis=-1, keepdims=True) + EPS)
    return (y * w.astype(F32)).astype(x.dtype)

def _modulate(h, shift, scale):
    return h * (1 + scale) + shift

def _head_rmsnorm(h, w):
    B, H, T, d = h.shape
    y = h * lax.rsqrt(jnp.mean(h * h, axis=-1, keepdims=True) + EPS)
    y = jnp.transpose(y, (0, 2, 1, 3)).reshape(B, T, H * d)
    return y * w.astype(F32)

def _to_heads(a, n_heads):
    B, T, C = a.shape
    return jnp.transpose(a.reshape(B, T, n_heads, C // n_heads), (0, 2, 1, 3)).astype(F32)

def _dwconv2d(x, w, rows, cols):
    B, T, C = x.shape
    img = x.reshape(B, rows, cols, C)
    out = lax.conv_general_dilated(img, w[:, :, None, :].astype(x.dtype), (1, 1), 'SAME',
                                   dimension_numbers=('NHWC', 'HWIO', 'NHWC'), feature_group_count=C)
    return out.reshape(B, T, C)

def _chunks(a, L):
    B, H, T = a.shape[:3]
    a = a.reshape(B, H, T // L, L, *a.shape[3:])
    return jnp.moveaxis(a, 2, 0)

def _unchunks(a):
    nc, B, H, L, d = a.shape
    return jnp.moveaxis(a, 0, 2).reshape(B, H, nc * L, d)

def _mlstm_scan(q, k, v, ig, lf, state):
    L = ML_CHUNK
    causal = jnp.tril(jnp.ones((L, L), bool))

    def step(carry, inp):
        C, n, m = carry
        qc, kc, vc, ic, fc = inp
        b = jnp.cumsum(fc, axis=-1)
        dlog = jnp.where(causal, b[..., :, None] - b[..., None, :] + ic[..., None, :], -jnp.inf)
        inter = b + m[..., None]
        mt = jnp.maximum(inter, jnp.max(dlog, axis=-1))
        w_intra = jnp.exp(dlog - mt[..., None])
        w_inter = jnp.exp(inter - mt)
        s = jnp.einsum('bhtd,bhsd->bhts', qc, kc) * w_intra
        num = jnp.einsum('bhts,bhsv->bhtv', s, vc) + w_inter[..., None] * jnp.einsum('bhtd,bhdv->bhtv', qc, C)
        den = jnp.sum(s, axis=-1) + w_inter * jnp.einsum('bhtd,bhd->bht', qc, n)
        h = num / jnp.maximum(jnp.abs(den), jnp.exp(-mt))[..., None]
        bL = b[..., -1]
        wlog = bL[..., None] - b + ic
        m_new = jnp.maximum(bL + m, jnp.max(wlog, axis=-1))
        decay = jnp.exp(bL + m - m_new)
        ws = jnp.exp(wlog - m_new[..., None])
        C_new = decay[..., None, None] * C + jnp.einsum('bhs,bhsd,bhsv->bhdv', ws, kc, vc)
        n_new = decay[..., None] * n + jnp.einsum('bhs,bhsd->bhd', ws, kc)
        return (C_new, n_new, m_new), h

    state, hs = lax.scan(step, state, tuple(_chunks(a, L) for a in (q, k, v, ig, lf)))
    return _unchunks(hs), state

def _hgrn_scan(q, k, v, lf, S):
    L = HG_CHUNK
    causal = jnp.tril(jnp.ones((L, L), bool))[:, :, None]

    def step(S, inp):
        qc, kc, vc, fc = inp
        b = jnp.cumsum(fc, axis=2)
        rel = jnp.where(causal, b[:, :, :, None, :] - b[:, :, None, :, :], -jnp.inf)
        a = jnp.einsum('bhtk,bhtsk,bhsk->bhts', qc, jnp.exp(rel), kc)
        o = jnp.einsum('bhts,bhsv->bhtv', a, vc) + jnp.einsum('bhtk,bhkv->bhtv', qc * jnp.exp(b), S)
        bL = b[:, :, -1]
        S_new = jnp.exp(bL)[..., None] * S + jnp.einsum('bhsk,bhsv->bhkv', kc * jnp.exp(bL[:, :, None] - b), vc)
        return S_new, o

    S, os_ = lax.scan(step, S, tuple(_chunks(a, L) for a in (q, k, v, lf)))
    return _unchunks(os_), S

def _bidir(scan_fn, ctx_f, ctx_b, lat_f, lat_b, init):
    flip = lambda a: jnp.flip(a, axis=2)
    hc_f, st_f = scan_fn(*ctx_f, init)
    hl_f, _ = scan_fn(*lat_f, st_f)
    hc_b, st_b = scan_fn(*(flip(a) for a in ctx_b), init)
    hl_b, _ = scan_fn(*(flip(a) for a in lat_b), st_b)
    return hl_f + flip(hl_b), hc_f + flip(hc_b)

def _mlstm_prep(p, conv_w, gate_b, rows, cols):
    W, H = ML_WIDTH, ML_HEADS
    qk = jax.nn.silu(_dwconv2d(p[..., :2 * W], conv_w, rows, cols))
    q = _to_heads(qk[..., :W], H) * (ML_HEAD_DIM ** -0.5)
    k = _to_heads(qk[..., W:], H)
    v = _to_heads(p[..., 2 * W:3 * W], H)
    o = p[..., 3 * W:4 * W]
    g = jnp.transpose(p[..., 4 * W:].astype(F32) + gate_b.astype(F32), (0, 2, 1))
    i_f, f_f, i_b, f_b = jnp.split(g, 4, axis=1)
    return q, k, v, o, (i_f, jax.nn.log_sigmoid(f_f)), (i_b, jax.nn.log_sigmoid(f_b))

def _mlstm_mixer(pl, pc, conv_w, gate_b, norm_w, rows, need_ctx):
    ql, kl, vl, ol, gfl, gbl = _mlstm_prep(pl, conv_w, gate_b, rows, GRID_W)
    qc, kc, vc, oc, gfc, gbc = _mlstm_prep(pc, conv_w, gate_b, 1, pc.shape[1])
    B = pl.shape[0]
    init = (jnp.zeros((B, ML_HEADS, ML_HEAD_DIM, ML_HEAD_DIM), F32),
            jnp.zeros((B, ML_HEADS, ML_HEAD_DIM), F32),
            jnp.zeros((B, ML_HEADS), F32))
    hl, hc = _bidir(_mlstm_scan, (qc, kc, vc) + gfc, (qc, kc, vc) + gbc,
                    (ql, kl, vl) + gfl, (ql, kl, vl) + gbl, init)
    out = lambda h, o: (_head_rmsnorm(h, norm_w) * jax.nn.sigmoid(o.astype(F32))).astype(pl.dtype)
    return out(hl, ol), (out(hc, oc) if need_ctx else None)

def _hgrn_prep(p, lb):
    W, H = HG_WIDTH, HG_HEADS
    pf = p.astype(F32)
    q = _to_heads(jax.nn.silu(pf[..., :W]), H) * (HG_HEAD_DIM ** -0.5)
    v = _to_heads(pf[..., 3 * W:4 * W], H)
    g = p[..., 4 * W:5 * W]
    dirs = []
    for j in range(2):
        z = pf[..., (1 + j) * W:(2 + j) * W]
        lbj = lb[j]
        lf = jnp.logaddexp(jnp.log(lbj), jnp.log1p(-lbj) + jax.nn.log_sigmoid(z))
        k = (1 - lbj) * jax.nn.sigmoid(-z)
        dirs.append((q, _to_heads(k, H), v, _to_heads(lf, H)))
    return dirs[0], dirs[1], g

def _hgrn_mixer(pl, pc, lb, norm_w, need_ctx):
    lat_f, lat_b, gl = _hgrn_prep(pl, lb)
    ctx_f, ctx_b, gc = _hgrn_prep(pc, lb)
    B = pl.shape[0]
    init = jnp.zeros((B, HG_HEADS, HG_HEAD_DIM, HG_HEAD_DIM), F32)
    hl, hc = _bidir(_hgrn_scan, ctx_f, ctx_b, lat_f, lat_b, init)
    out = lambda h, g: (_head_rmsnorm(h, norm_w) * jax.nn.silu(g.astype(F32))).astype(pl.dtype)
    return out(hl, gl), (out(hc, gc) if need_ctx else None)

def _conv_ffn(h, w_up, conv_w, w_down, rows, cols):
    u = _dwconv2d(h @ w_up, conv_w, rows, cols)
    a, b = jnp.split(u, 2, axis=-1)
    return (jax.nn.silu(a) * b) @ w_down

def first_inputs(seed: int = 0) -> dict:
    key = jax.random.key(seed)
    ks = jax.random.split(key, 24)
    nrm = lambda k, shape, s: jax.random.normal(k, shape, F32) * s
    L, D = DEPTH, D_MODEL
    gate_b = jnp.concatenate([
        nrm(ks[8], (L, ML_HEADS), 0.1),
        jnp.linspace(3.0, 6.0, ML_HEADS, dtype=F32)[None] + nrm(ks[9], (L, ML_HEADS), 0.1),
        nrm(ks[10], (L, ML_HEADS), 0.1),
        jnp.linspace(3.0, 6.0, ML_HEADS, dtype=F32)[None] + nrm(ks[11], (L, ML_HEADS), 0.1)], axis=-1)
    return {
        "x": nrm(ks[0], (BATCH, SEQ, D), 1.0),
        "c": nrm(ks[1], (BATCH, D), 1.0),
        "ctx": nrm(ks[2], (BATCH, CTX_LEN, D), 1.0),
        "c_ctx": nrm(ks[3], (D,), 1.0),
        "w_mod": nrm(ks[4], (L, D, N_MOD * D), D ** -0.5),
        "b_mod": nrm(ks[5], (L, N_MOD * D), 0.02),
        "norm1_w": 1.0 + nrm(ks[6], (L, D), 0.05),
        "w_in": nrm(ks[7], (L, D, IN_COLS), D ** -0.5),
        "mlstm_gate_b": gate_b,
        "mlstm_conv_w": nrm(ks[12], (L, CONV_W, CONV_W, 2 * ML_WIDTH), 1.0 / CONV_W),
        "mlstm_norm_w": 1.0 + nrm(ks[13], (L, ML_WIDTH), 0.05),
        "hgrn_lb_logits": nrm(ks[14], (2, L + 1, HG_WIDTH), 0.1),
        "hgrn_norm_w": 1.0 + nrm(ks[15], (L, HG_WIDTH), 0.05),
        "w_out": nrm(ks[16], (L, D_MIX, D), D_MIX ** -0.5),
        "norm2_w": 1.0 + nrm(ks[17], (L, D), 0.05),
        "w_up": nrm(ks[18], (L, D, 2 * D_FF), D ** -0.5),
        "ffn_conv_w": nrm(ks[19], (L, CONV_W, CONV_W, 2 * D_FF), 1.0 / CONV_W),
        "w_down": nrm(ks[20], (L, D_FF, D), D_FF ** -0.5),
        "final_norm_w": 1.0 + nrm(ks[21], (D,), 0.05),
    }

def first_block(x, c, ctx, c_ctx, w_mod, b_mod, norm1_w, w_in, mlstm_gate_b, mlstm_conv_w, mlstm_norm_w,
              hgrn_lb_logits, hgrn_norm_w, w_out, norm2_w, w_up, ffn_conv_w, w_down, final_norm_w):
    rows = x.shape[1] // GRID_W
    ctx_len = ctx.shape[1]
    lower_bounds = jnp.cumsum(jax.nn.softmax(hgrn_lb_logits.astype(F32), axis=1), axis=1)
    xl, xc = x, ctx
    for l in range(DEPTH):
        last = l == DEPTH - 1
        mod_l = (jax.nn.silu(c) @ w_mod[l] + b_mod[l])[:, None, :]
        mod_c = (jax.nn.silu(c_ctx) @ w_mod[l] + b_mod[l])[None, None, :]
        sh1, sc1, g1, sh2, sc2, g2 = jnp.split(mod_l, N_MOD, axis=-1)
        sh1c, sc1c, g1c, sh2c, sc2c, g2c = jnp.split(mod_c, N_MOD, axis=-1)
        pl = _modulate(_rmsnorm(xl, norm1_w[l]), sh1, sc1) @ w_in[l]
        pc = _modulate(_rmsnorm(xc, norm1_w[l]), sh1c, sc1c) @ w_in[l]
        ml_l, ml_c = _mlstm_mixer(pl[..., :ML_COLS], pc[..., :ML_COLS], mlstm_conv_w[l], mlstm_gate_b[l],
                                  mlstm_norm_w[l], rows, not last)
        hg_l, hg_c = _hgrn_mixer(pl[..., ML_COLS:], pc[..., ML_COLS:], lower_bounds[:, l], hgrn_norm_w[l], not last)
        xl = xl + g1 * (jnp.concatenate([ml_l, hg_l], axis=-1) @ w_out[l])
        xl = xl + g2 * _conv_ffn(_modulate(_rmsnorm(xl, norm2_w[l]), sh2, sc2), w_up[l], ffn_conv_w[l],
                                 w_down[l], rows, GRID_W)
        if not last:
            xc = xc + g1c * (jnp.concatenate([ml_c, hg_c], axis=-1) @ w_out[l])
            xc = xc + g2c * _conv_ffn(_modulate(_rmsnorm(xc, norm2_w[l]), sh2c, sc2c), w_up[l], ffn_conv_w[l],
                                      w_down[l], 1, ctx_len)
    return _rmsnorm(xl, final_norm_w)


DEPTH_2 = 2

SB_HEADS = 4
SB_HEAD_DIM = 64
Q_BLOCK = 128
RET_HEADS = 4
RET_QK_DIM = 64
RET_V_DIM = 128
RET_CHUNK = 128
ROPE_BASE = 10000.0
POOL_GROUPS = 4
POOL_GROUP_DIM = 64
POOL_WINDOWS = (2, 4, 8, 16)
N_BRANCHES = 3

SB_W = SB_HEADS * SB_HEAD_DIM
RET_QK_W = RET_HEADS * RET_QK_DIM
RET_V_W = RET_HEADS * RET_V_DIM
POOL_W = POOL_GROUPS * POOL_GROUP_DIM
SPLITS = (SB_W, SB_W, SB_W, RET_QK_W, RET_QK_W, RET_V_W, RET_V_W, POOL_W, N_BRANCHES * D_MODEL)
D_IN = SB_W * 3 + RET_QK_W * 2 + RET_V_W * 2 + POOL_W + N_BRANCHES * D_MODEL


def rmsnorm(x, g):
    xf = x.astype(jnp.float32)
    y = xf * lax.rsqrt(jnp.mean(xf * xf, axis=-1, keepdims=True) + EPS)
    return (y * g.astype(jnp.float32)).astype(x.dtype)

def swiglu_half(h, w1, w3, w2):
    return 0.5 * ((jax.nn.silu(h @ w1) * (h @ w3)) @ w2)

def stick_breaking_attention(q, k, v):
    B, S, H, dh = q.shape
    qf = (q.astype(jnp.float32) * (dh ** -0.5)).transpose(0, 2, 1, 3)
    kf = k.astype(jnp.float32).transpose(0, 2, 1, 3)
    vf = v.astype(jnp.float32).transpose(0, 2, 1, 3)
    nb = S // Q_BLOCK
    q_blocks = qf.reshape(B, H, nb, Q_BLOCK, dh).transpose(2, 0, 1, 3, 4)
    key_pos = jnp.arange(S)

    def block(args):
        qb, start = args
        z = jnp.einsum('bhqd,bhkd->bhqk', qb, kf)
        q_pos = start + jnp.arange(Q_BLOCK)
        mask = key_pos[None, :] < q_pos[:, None]
        log_beta = jax.nn.log_sigmoid(z)
        log_fail = jnp.where(mask, log_beta - z, 0.0)
        after = lax.cumsum(log_fail, axis=3, reverse=True) - log_fail
        w = jnp.where(mask, jnp.exp(log_beta + after), 0.0)
        return jnp.einsum('bhqk,bhkd->bhqd', w, vf)

    out = lax.map(block, (q_blocks, jnp.arange(nb) * Q_BLOCK))
    return out.transpose(1, 0, 3, 2, 4).reshape(B, S, H * dh)

def rotary(x, cos, sin):
    half = x.shape[-1] // 2
    x1, x2 = x[..., :half], x[..., half:]
    c = cos[None, :, None, :]
    s = sin[None, :, None, :]
    return jnp.concatenate([x1 * c - x2 * s, x2 * c + x1 * s], axis=-1)

def retention(q, k, v, g):
    B, S, H, dk = q.shape
    dv = v.shape[-1]
    half = dk // 2
    pos = jnp.arange(S, dtype=jnp.float32)
    inv_freq = ROPE_BASE ** (-jnp.arange(half, dtype=jnp.float32) / half)
    ang = pos[:, None] * inv_freq[None, :]
    cos, sin = jnp.cos(ang), jnp.sin(ang)
    qf = rotary(q.astype(jnp.float32), cos, sin)
    kf = rotary(k.astype(jnp.float32), cos, sin) * (dk ** -0.5)
    vf = v.astype(jnp.float32)
    log_gamma = jnp.log(1.0 - 2.0 ** (-5.0 - jnp.arange(H, dtype=jnp.float32)))

    C = RET_CHUNK
    N = S // C
    qc = qf.reshape(B, N, C, H, dk)
    kc = kf.reshape(B, N, C, H, dk)
    vc = vf.reshape(B, N, C, H, dv)
    idx = jnp.arange(C, dtype=jnp.float32)
    diff = idx[:, None] - idx[None, :]
    causal = diff >= 0
    decay = jnp.where(causal[None], jnp.exp(jnp.where(causal, diff, 0.0)[None] * log_gamma[:, None, None]), 0.0)
    scores = jnp.einsum('bnihd,bnjhd->bnhij', qc, kc) * decay
    intra = jnp.einsum('bnhij,bnjhe->bnihe', scores, vc)

    k_decay = jnp.exp((C - 1 - idx)[:, None] * log_gamma[None, :])
    kv = jnp.einsum('bnjhd,bnjhe->nbhde', kc * k_decay[:, :, None], vc)
    chunk_decay = jnp.exp(C * log_gamma)[None, :, None, None]

    def step(state, kv_n):
        return chunk_decay * state + kv_n, state

    _, states = lax.scan(step, jnp.zeros((B, H, dk, dv), jnp.float32), kv)
    q_decay = jnp.exp((idx + 1)[:, None] * log_gamma[None, :])
    cross = jnp.einsum('bnihd,nbhde->bnihe', qc * q_decay[:, :, None], states)

    y = (intra + cross).reshape(B, S, H, dv)
    y = y * lax.rsqrt(jnp.mean(y * y, axis=-1, keepdims=True) + EPS)
    return y.reshape(B, S, H * dv) * jax.nn.silu(g.astype(jnp.float32))

def pool_mixer(u, w_pool, pool_scale):
    B, S, _ = u.shape
    uf = u.astype(jnp.float32).reshape(B, S, POOL_GROUPS, POOL_GROUP_DIM)
    cs = jnp.concatenate([jnp.zeros((B, 1, POOL_GROUPS, POOL_GROUP_DIM), jnp.float32),
                          jnp.cumsum(uf, axis=1)], axis=1)
    t = jnp.arange(S)
    win = jnp.array(POOL_WINDOWS)
    lo = jnp.maximum(t[:, None] + 1 - win[None, :], 0)
    count = (t[:, None] + 1 - lo).astype(jnp.float32)
    cs_lo = cs[:, lo, jnp.arange(POOL_GROUPS)[None, :], :]
    mean = (cs[:, 1:] - cs_lo) / count[None, :, :, None]
    y = jnp.einsum('bsgc,gce->bsge', mean - uf, w_pool.astype(jnp.float32))
    return y.reshape(B, S, POOL_W) * pool_scale.astype(jnp.float32)

def second_inputs(seed: int = 0) -> dict:
    key = jax.random.key(seed)
    ks = jax.random.split(key, 20)

    def w(k, shape, fan_in):
        return jax.random.normal(k, shape, jnp.float32) * (fan_in ** -0.5)

    def gain(k, shape):
        return 1.0 + 0.02 * jax.random.normal(k, shape, jnp.float32)

    return {
        "x": jax.random.normal(ks[0], (BATCH, SEQ, D_MODEL), jnp.float32),
        "g_ffn1": gain(ks[1], (DEPTH_2, D_MODEL)),
        "w1_ffn1": w(ks[2], (DEPTH_2, D_MODEL, D_FF), D_MODEL),
        "w3_ffn1": w(ks[3], (DEPTH_2, D_MODEL, D_FF), D_MODEL),
        "w2_ffn1": w(ks[4], (DEPTH_2, D_FF, D_MODEL), D_FF),
        "g_mix": gain(ks[5], (DEPTH_2, D_MODEL)),
        "w_in": w(ks[6], (DEPTH_2, D_MODEL, D_IN), D_MODEL),
        "w_branch_sb": w(ks[7], (DEPTH_2, SB_W, D_MODEL), SB_W),
        "w_branch_ret": w(ks[8], (DEPTH_2, RET_V_W, D_MODEL), RET_V_W),
        "w_branch_pool": w(ks[9], (DEPTH_2, POOL_W, D_MODEL), POOL_W),
        "w_pool": w(ks[10], (DEPTH_2, POOL_GROUPS, POOL_GROUP_DIM, POOL_GROUP_DIM), POOL_GROUP_DIM),
        "pool_scale": gain(ks[11], (DEPTH_2, POOL_W)),
        "w_out": w(ks[12], (DEPTH_2, D_MODEL, D_MODEL), D_MODEL),
        "g_ffn2": gain(ks[13], (DEPTH_2, D_MODEL)),
        "w1_ffn2": w(ks[14], (DEPTH_2, D_MODEL, D_FF), D_MODEL),
        "w3_ffn2": w(ks[15], (DEPTH_2, D_MODEL, D_FF), D_MODEL),
        "w2_ffn2": w(ks[16], (DEPTH_2, D_FF, D_MODEL), D_FF),
        "g_final": gain(ks[17], (D_MODEL,)),
    }

def second_block(x, g_ffn1, w1_ffn1, w3_ffn1, w2_ffn1, g_mix, w_in, w_branch_sb, w_branch_ret,
              w_branch_pool, w_pool, pool_scale, w_out, g_ffn2, w1_ffn2, w3_ffn2, w2_ffn2, g_final):
    B, S, D = x.shape
    split_points = [int(p) for p in np.cumsum(SPLITS)[:-1]]
    for l in range(DEPTH_2):
        x = x + swiglu_half(rmsnorm(x, g_ffn1[l]), w1_ffn1[l], w3_ffn1[l], w2_ffn1[l])

        h = rmsnorm(x, g_mix[l])
        proj = h @ w_in[l]
        q_sb, k_sb, v_sb, q_r, k_r, v_r, g_r, u_p, gate = jnp.split(proj, split_points, axis=-1)
        y_sb = stick_breaking_attention(q_sb.reshape(B, S, SB_HEADS, SB_HEAD_DIM),
                                        k_sb.reshape(B, S, SB_HEADS, SB_HEAD_DIM),
                                        v_sb.reshape(B, S, SB_HEADS, SB_HEAD_DIM))
        y_ret = retention(q_r.reshape(B, S, RET_HEADS, RET_QK_DIM),
                          k_r.reshape(B, S, RET_HEADS, RET_QK_DIM),
                          v_r.reshape(B, S, RET_HEADS, RET_V_DIM), g_r)
        y_pool = pool_mixer(u_p, w_pool[l], pool_scale[l])

        gates = jax.nn.sigmoid(gate.astype(jnp.float32)).reshape(B, S, N_BRANCHES, D)
        merged = (gates[:, :, 0] * (y_sb @ w_branch_sb[l].astype(jnp.float32))
                  + gates[:, :, 1] * (y_ret @ w_branch_ret[l].astype(jnp.float32))
                  + gates[:, :, 2] * (y_pool @ w_branch_pool[l].astype(jnp.float32)))
        x = x + merged.astype(x.dtype) @ w_out[l]

        x = x + swiglu_half(rmsnorm(x, g_ffn2[l]), w1_ffn2[l], w3_ffn2[l], w2_ffn2[l])
    return rmsnorm(x, g_final)


def setup_inputs(seed=0):
    out = dict(first_inputs(seed))
    for name, value in second_inputs(seed + 1).items():
        if name != "x":
            out[name + "_2"] = value
    return out


def reference(
    x, c, ctx, c_ctx, w_mod, b_mod, norm1_w, w_in, mlstm_gate_b, mlstm_conv_w, mlstm_norm_w,
    hgrn_lb_logits, hgrn_norm_w, w_out, norm2_w, w_up, ffn_conv_w, w_down, final_norm_w,
    g_ffn1_2, w1_ffn1_2, w3_ffn1_2, w2_ffn1_2, g_mix_2, w_in_2, w_branch_sb_2, w_branch_ret_2,
    w_branch_pool_2, w_pool_2, pool_scale_2, w_out_2, g_ffn2_2, w1_ffn2_2, w3_ffn2_2, w2_ffn2_2,
    g_final_2,
):
    x = first_block(
        x, c, ctx, c_ctx, w_mod, b_mod, norm1_w, w_in, mlstm_gate_b, mlstm_conv_w, mlstm_norm_w,
        hgrn_lb_logits, hgrn_norm_w, w_out, norm2_w, w_up, ffn_conv_w, w_down, final_norm_w,
    )
    return second_block(
        x, g_ffn1_2, w1_ffn1_2, w3_ffn1_2, w2_ffn1_2, g_mix_2, w_in_2, w_branch_sb_2,
        w_branch_ret_2, w_branch_pool_2, w_pool_2, pool_scale_2, w_out_2, g_ffn2_2, w1_ffn2_2,
        w3_ffn2_2, w2_ffn2_2, g_final_2,
    )


_drawn_inputs = setup_inputs


def setup_inputs(seed=0):
    import zlib

    import numpy as np

    out = dict(_drawn_inputs(seed))
    spreads = {}
    factors = {'mlstm_norm_w': 3.033,
     'hgrn_lb_logits': 8.0,
     'g_ffn1_2': 4.332,
     'pool_scale_2': 23.045,
     'g_ffn2_2': 38.364,
     'g_final_2': 22.72,
     'g_mix_2': 4.499}
    for name, (base, spread) in spreads.items():
        noise = np.random.default_rng([zlib.crc32(name.encode()), seed]).standard_normal(out[name].shape)
        drawn = base * np.exp(spread * noise) if base else spread * noise
        out[name] = __import__('jax').numpy.asarray(drawn.astype(out[name].dtype))
    for name, factor in factors.items():
        out[name] = (out[name] * factor).astype(out[name].dtype)
    return out
```

```python
from contextlib import ExitStack

import concourse.bass as bass
import numpy as np
from concourse import mybir

F32 = mybir.dt.float32
F32R = mybir.dt.float32r
U8 = mybir.dt.uint8
ALU = mybir.AluOpType
ACT = mybir.ActivationFunctionType

P = 128
D = 1024
KD = D // P
T = 512
FF = 2816
KF = FF // P
EPS = 1e-6
LAYERS = 2
SLAB = 256
SB_HEADS, SB_DIM = 4, 64
RET_HEADS, RET_DIM = 4, 64
TT = T // P
UP_STEPS = FF // SLAB
DOWN_K = KF // 2
COL = {"q_sb": 0, "k_sb": 256, "v_sb": 512, "q_r": 768, "k_r": 1024, "v_r": 1280, "g_r": 1792, "u": 2304, "gate": 2560}
POOL_WINDOWS = (2, 4, 8, 16)
PAD = 16
LIVE = [T - P * j for j in range(TT)]
LIVE_AT = [sum(LIVE[:j]) for j in range(TT)]
LIVE_ALL = sum(LIVE)

CT = 256
CTT = CT // P
TA = T + CT
TAT = TA // P
GRID = (T // 64, 64)
ML_HEADS, HG_HEADS = 4, 4
HEAD_DIM = 128
HEAD_SCALE = HEAD_DIM ** -0.5
ML_W = ML_HEADS * HEAD_DIM
HG_AT = 4 * ML_W + 4 * ML_HEADS
N_MOD = 6
MOD_TILES = N_MOD * KD
MOD_SLABS = N_MOD * D // SLAB
MOD_FIRST = 2 * D // SLAB
MOD_TILES1 = 2 * KD
LEVELS = 7
IN1 = ([("mq", 0), ("mq", SLAB), ("mk", ML_W), ("mk", ML_W + SLAB), ("mv", 2 * ML_W), ("mv", 2 * ML_W + SLAB), ("gate", 4 * ML_W),
        ("gate", 4 * ML_W), ("mo", 3 * ML_W), ("mo", 3 * ML_W + SLAB)]
       + [(n, HG_AT + o + e) for n, o in (("hq", 0), ("hv", 3 * ML_W), ("zf", ML_W), ("zb", 2 * ML_W), ("hg", 4 * ML_W)) for e in (0, SLAB)])
IN1_SLABS = len(IN1)
OUT1_SLABS = D // SLAB

COL_AT, n_col = {}, 0
for name_, width_ in (("g_ffn1", 16), ("g_mix", 16), ("g_ffn2", 16), ("g_final", 8), ("pool_scale", 4), ("norm1", 8), ("norm2", 8),
                      ("final_norm", 8), ("c", 16), ("ml_norm", 4), ("hg_norm", 4), ("lb_logits", 16), ("b_mod", MOD_TILES),
                      ("ml_conv", 72), ("ffn_conv", 9 * 2 * KF), ("gate_b", 4)):
    COL_AT[name_] = n_col
    n_col += width_
N_COL = n_col
HG_N = 2 * HG_HEADS
MOD_BEFORE, MOD_AFTER = 5, 3
MOD_WITHIN = (MOD_SLABS - MOD_FIRST - MOD_BEFORE - MOD_AFTER) * 2 * KD // HG_N
MOD_REST = [MOD_WITHIN * (m_ + 1) // LEVELS - MOD_WITHIN * m_ // LEVELS for m_ in range(LEVELS)]

IN1_P, IN1_USE, IN1_CTX = [], [], []
uses_, ctx_uses_ = [0, 1], [0, 0]
for i_, (name_, _) in enumerate(IN1):
    p_ = i_ % 2 if i_ < 6 else 0 if i_ < 8 else (i_ + 1) % 2
    IN1_P.append(p_)
    if i_ == 7:
        IN1_USE.append(IN1_USE[-1])
        IN1_CTX.append(IN1_CTX[-1])
        continue
    IN1_USE.append(uses_[p_])
    IN1_CTX.append(ctx_uses_[p_])
    uses_[p_] += 1
    ctx_uses_[p_] += name_ in ("mk", "mv", "gate", "hv", "zf", "zb")
    if i_ == 9:
        ML_USE = uses_[0]
        uses_ = [u_ + ML_HEADS for u_ in uses_]
HG_USE = uses_[0]
OUT1_USE = HG_USE + HG_HEADS
UP1_USE = OUT1_USE + OUT1_SLABS // 2
DOWN1_USE = UP1_USE + UP_STEPS
BASE_USE = DOWN1_USE + KD // 2
OUT1_AT = 2 + IN1_SLABS
UP1_AT = OUT1_AT + OUT1_SLABS
DOWN1_AT = UP1_AT + 2 * UP_STEPS
BASE_SLAB = DOWN1_AT + 2 * KD
NORMS1 = 4
CONV_AT = [9 * t_ for t_ in range(5)] + [36 + 12 * t_ for t_ in range(1, 5)]
CONV1 = CONV_AT[8]
LATC = (slice(CT, TA), slice(0, T))
CTXC = (slice(0, CT), slice(T, TA))
HG_ORDER = ((4, 5, 0, 1, 2), (5, 4, 3, 2, 1))

FFN_SLABS, FFN_USES = 2 * UP_STEPS + 2 * KD, UP_STEPS + KD // 2
MIX_SLABS, MIX_USES = 30, 24
SB_USE, FILL_USE, GATE_USE, RET_USE, BRANCH_USE = 2, 1, (6, 8), (7, 9), (8, 10)


def build(nc, io):
    with ExitStack() as ctx:
        base = [(nc.sbuf_base + 63) // 64 * 64]

        def place(name, shape, dt, at=None):
            size = int(np.prod(shape[1:])) * (1 if dt == U8 else 4)
            if at is None:
                at = base[0]
                base[0] = (at + size + 63) // 64 * 64
            return nc.alloc_sbuf_tensor_at(name, shape, dt, offset=at)

        def sem(name):
            return ctx.enter_context(nc.semaphore(name))

        x = place("x", [P, KD, T], F32)
        hh = place("hh", [P, KD, T], F32R)
        hl = place("hl", [P, KD, T], F32R)
        raw_at = base[0]
        raw = [place(f"raw{b}", [P, 8, SLAB], F32) for b in range(2)]
        whi = [place(f"whi{b}", [P, 8, SLAB], F32R) for b in range(2)]
        wlo = [place(f"wlo{b}", [P, 8, SLAB], F32R) for b in range(2)]
        arena = base[0]
        TILE = 4 * T
        uh = place("uh", [P, KF, T], F32R)
        ul = place("ul", [P, KF, T], F32R)
        scratch = base[0]
        sil = [place(f"sil{b}", [P, 2, T], F32) for b in range(2)]
        ut = place("ut", [P, 2, T], F32)
        sq = [place(f"sq{b}", [P, T], F32, scratch + b * TILE) for b in range(2)]
        std = place("std", [P, T], F32, scratch + 2 * TILE)
        rstd = place("rstd", [P, T], F32, scratch + 3 * TILE)
        hn = [place(f"hn{b}", [P, T], F32, scratch + (4 + b) * TILE) for b in range(2)]
        ident = place("ident", [P, P], F32)
        ones = place("ones", [P, P], F32)
        eps = place("eps", [P, 1], F32)
        col = place("col", [P, N_COL], F32)
        pad = [place(f"pad{b}", [P, GRID[0] + 2, GRID[1] + 2], F32) for b in range(2)]
        silc = place("silc", [P, KD, 2], F32)
        modc = place("modc", [P, MOD_TILES, 2], F32)
        wsc = place("wsc", [P, 3, KD], F32)
        lbm = place("lbm", [P, 2, 4], F32)
        lbe = place("lbe", [P, 2, 2, 4], F32)
        lb = place("lb", [P, 2, 4], F32)
        om = place("om", [P, 2, 4], F32)
        oms = place("oms", [P, 2, 4], F32)
        gcol = place("gcol", [P, 2, TAT, ML_HEADS], F32)
        pend = place("pend", [P, 2, HG_HEADS, TAT], F32)
        epend = place("epend", [P, 2, HG_HEADS, TAT], F32)

        def tile_at(name, shape, n, dt=F32):
            return place(name, shape, dt, int(arena + n * TILE))

        ch = tile_at("ch", [P, KD, CT], 0, F32R)
        cl = tile_at("cl", [P, KD, CT], 4, F32R)
        cx = tile_at("cx", [P, KD, CT], 8)
        mq = tile_at("mq", [P, ML_HEADS, T], 8)
        mk = tile_at("mk", [P, ML_HEADS, TA], 12)
        mv = tile_at("mv", [P, TAT, ML_W], 18)
        mo = tile_at("mo", [P, ML_HEADS, T], 24)
        GI = [tile_at(f"gi{d}", [4, TA], 28 + 1.5 * d) for d in range(2)]
        GF = [tile_at(f"gf{d}", [4, TA], 31 + 1.5 * d) for d in range(2)]
        GT = [tile_at(f"gt{d}", [4, TA], 34 + 1.5 * d) for d in range(2)]
        gall = tile_at("gall", [16, TA], 37)
        wt = [[tile_at(f"wt{d}{b}", [P, T], 38.5 + 2 * d + b) for b in range(2)] for d in range(2)]
        bsel = tile_at("bsel", [4, ML_HEADS, P], 42.5)
        mlmask = tile_at("mlmask", [P, 2, P], 43.5)
        aw = [[place(f"aw{d}{b}", [P, T], F32, scratch + (2 * d + b) * TILE) for b in range(2)] for d in range(2)]
        dnb = [place(f"dnb{d}", [P, T], F32, scratch + (4 + d) * TILE) for d in range(2)]
        nmb = [tile_at(f"nmb{d}", [P, T], 30 + 7 * d) for d in range(2)]
        dab = [tile_at(f"dab{d}", [P, T], 28 + d) for d in range(2)]
        cacc = [place(f"cacc{t}", [P, TA], F32, scratch + 2 * t * TILE) for t in range(2)]
        cpad = [place(f"cpad{t}", [P, CT + 2], F32, scratch + 4 * TILE + t * (TILE + 64) // 1) for t in range(2)]
        sq4 = place("sq4", [P, 4, T], F32, scratch)
        ym_h = tile_at("ym_h", [P, 4, T], 36, F32R)
        ym_l = tile_at("ym_l", [P, 4, T], 40, F32R)
        hq = tile_at("hq", [P, HG_HEADS, T], 8)
        hv = tile_at("hv", [P, TAT, ML_W], 12)
        hz = [tile_at(f"hz{d}", [P, HG_HEADS, TA], 18 + 6 * d) for d in range(2)]
        hg = tile_at("hg", [P, HG_HEADS, T], 30)
        h_at = raw_at - 16 * TILE
        hf = [place(f"hf{d}", [P, HG_HEADS, TA], F32, h_at + 6 * TILE * d) for d in range(2)]
        hgmask = place("hgmask", [P, 2 * LEVELS, P], F32, h_at + 12 * TILE)
        resetm = tile_at("resetm", [P, TA], 0)
        ptmp = tile_at("ptmp", [P, TA], 34)
        ea = tile_at("ea", [P, TA], 0)
        eb = tile_at("eb", [P, TA], 1.5)
        yl = [tile_at(f"yl{b}", [P, T], 3 + b) for b in range(2)]
        xl = [tile_at(f"xl{b}", [P, T], 5 + b) for b in range(2)]
        ah = tile_at("ah", [P, T], 7)
        kt = place("kt", [P, TA], F32, scratch)
        ktok = place("ktok", [P, 5, P], F32, scratch + 3 * TILE // 2)
        qt = [place(f"qt{d}", [P, T], F32, scratch + 11 * TILE // 4 + d * TILE) for d in range(2)]
        st = [place("st0", [P, 5, P], F32, scratch + 19 * TILE // 4), tile_at("st1", [P, 5, P], 34)]
        yh_h = tile_at("yh_h", [P, 4, T], 18, F32R)
        yh_l = tile_at("yh_l", [P, 4, T], 22, F32R)

        decay = tile_at("decay", [P, RET_HEADS, T], 0)
        rope = tile_at("rope", [P, 2, T], 4)
        perm = tile_at("perm", [P, P], 6)
        trineg = tile_at("trineg", [P, P], 6.25)
        onesneg = tile_at("onesneg", [P, P], 6.5)
        wpool = tile_at("wpool", [P, 2, P], 6.75)
        dmask = tile_at("dmask", [P, P], 7.25)
        invcnt = tile_at("invcnt", [P, 2, PAD], 43)
        zero = tile_at("zero", [P, P], 7.5)
        lowest = tile_at("lowest", [P, P], 7.75)
        q_sb = tile_at("q_sb", [P, 2, T], 8)
        k_sb = tile_at("k_sb", [P, 2, T], 10)
        v_sb = tile_at("v_sb", [P, TT, 256], 12)
        q_r = tile_at("q_r", [P, 2, T], 14)
        k_r = tile_at("k_r", [P, 2, T], 16)
        v_r = tile_at("v_r", [P, TT, 512], 18)
        u = tile_at("u", [P, 2, PAD + T], 22)
        rraw = [tile_at(f"rraw{i}", [P, 2, T], 36 + 2 * i) for i in range(2)]
        rt1 = place("rt1", [P, T], F32, scratch + 4 * TILE)
        rt2 = place("rt2", [P, T], F32, scratch + 5 * TILE)
        sc = tile_at("sc", [P, LIVE_ALL], 24.5)
        sp_ = tile_at("sp", [P, LIVE_ALL], 27)
        w_ = tile_at("w", [P, LIVE_ALL], 29.5)
        ysb_h = tile_at("ysb_h", [P, 2, T], 32, F32R)
        ysb_l = tile_at("ysb_l", [P, 2, T], 34, F32R)
        pw = [tile_at("pw0", [P, 2, PAD + T], 36), tile_at("pw1", [P, 2, PAD + T], 38.25)]
        pd = tile_at("pd", [P, 2, T], 40.5)
        pt = place("pt", [P, 2, T], F32, scratch + 4 * TILE)
        yp_h = tile_at("yp_h", [P, 2, T], 12, F32R)
        yp_l = tile_at("yp_l", [P, 2, T], 22, F32R)
        aret = [tile_at(f"aret{i}", [P, LIVE_ALL], 36 + 2.5 * i) for i in range(2)]
        ret_sqr = tile_at("ret_sqr", [P, T], 41)
        ret_root = tile_at("ret_root", [P, T], 42)
        ret_inv = tile_at("ret_inv", [P, T], 31)
        yraw = tile_at("yraw", [P, 4, T], 8)
        yr_h = tile_at("yr_h", [P, 4, T], 14, F32R)
        yr_l = tile_at("yr_l", [P, 4, T], 18, F32R)
        gates = tile_at("gates", [P, 3, 2, T], 24.5)
        mg = tile_at("mg", [P, 2, T], 8)
        mt = tile_at("mt", [P, 2, T], 10)
        mg_h = tile_at("mg_h", [P, KD, T], 0, F32R)
        mg_l = tile_at("mg_l", [P, KD, T], 36, F32R)

        uh_f = tile_at("yfin", [P, KD, T], 0)

        pm = [ctx.enter_context(nc.psum_tensor(f"pm{b}", [P, 2, T], F32)) for b in range(2)]
        pa = [ctx.enter_context(nc.psum_tensor(f"pa{b}", [P, T], F32)) for b in range(4)]

        raw_loaded = [sem("raw_loaded0"), sem("raw_loaded1")]
        hi_done, split_done, slab_used = sem("hi_done"), sem("split_done"), sem("slab_used")
        tick, vtick, stick, atick = sem("pool_tick"), sem("dve_tick"), sem("sync_tick"), sem("act_tick")
        pm_free = [sem("pm_free0"), sem("pm_free1")]
        sq_done, sq_summed, std_done, rstd_done = sem("sq_done"), sem("sq_summed"), sem("std_done"), sem("rstd_done")
        hn_done, hh_done, hl_done = sem("hn_done"), sem("hh_done"), sem("hl_done")
        hidden_done = sem("hidden_done")
        const_loaded, const_made = sem("const_loaded"), sem("const_made")
        x_loaded, ctx_loaded = sem("x_loaded"), sem("ctx_loaded")
        mod_loaded, mod_used, mod_in, mod_done, lb_step, lb_exp = (
            [sem("mod_loaded0"), sem("mod_loaded1")], sem("mod_used"), sem("mod_in"), sem("mod_done"), sem("lb_step"), sem("lb_exp"))
        ctx_free = [sem("ctx_free0"), sem("ctx_free1")]
        pad_zeroed, pad_filled, cpad_filled, conv_step, conv_silu = (
            sem("pad_zeroed"), sem("pad_filled"), sem("cpad_filled"), sem("conv_step"), sem("conv_silu"))
        gsel_ready, gsel_copied, gact, gstep, gdn, gtr, gcol_done = (
            sem("gsel_ready"), sem("gsel_copied"), sem("gact"), sem("gstep"), sem("gdn"), sem("gtr"), sem("gcol_done"))
        mb_ready, mb_copied, ms_ready, w_pre, w_exp, a_made, a_masked, nd_acc, den_abs, ml_h = (
            sem("mb_ready"), sem("mb_copied"), sem("ms_ready"), sem("w_pre"), sem("w_exp"), sem("a_made"), sem("a_masked"), sem("nd_acc"),
            sem("den_abs"), sem("ml_h"))
        t_sq, t_ss, t_std, t_step, t_done = sem("t_sq"), sem("t_ss"), sem("t_std"), sem("t_step"), sem("t_done")
        hgmask_loaded, hg_sig, hg_step, hg_ln, hep_done = (
            sem("hgmask_loaded"), sem("hg_sig"), sem("hg_step"), sem("hg_ln"), sem("hep_done"))
        hdb, heab, hkq, ht_ready, ht_copied, hkv_ready, hs_done = (
            sem("hdb"), sem("heab"), sem("hkq"), sem("ht_ready"), sem("ht_copied"), sem("hkv_ready"), sem("hs_done"))
        hd_ready, hd_copied, hy_done, hx_exp, hx_up, hx_lo, ha_ready, ha_copied, ho_ready = (
            sem("hd_ready"), sem("hd_copied"), sem("hy_done"), sem("hx_exp"), sem("hx_up"), sem("hx_lo"), sem("ha_ready"), sem("ha_copied"),
            sem("ho_ready"))
        x_mixed, usilu_done = sem("x_mixed"), sem("usilu_done")
        mixc_loaded, mixc_made = sem("mixc_loaded"), sem("mixc_made")
        qkv_done = sem("qkv_done")
        swapped, rot_made, rot_done = sem("swapped"), sem("rot_made"), sem("rot_done")
        z_ready, abs_done, exp_done, ln_done = sem("z_ready"), sem("abs_done"), sem("exp_done"), sem("ln_done")
        sp_done, sp_masked, logw_ready, w_done, w_masked, sb_out = (
            sem("sp_done"), sem("sp_masked"), sem("logw_ready"), sem("w_done"), sem("w_masked"), sem("sb_out"))
        sb_hi = sem("sb_hi")
        win_done, pd_done, pool_out, pool_scaled, pool_hi, pool_done = (
            sem("win_done"), sem("pd_done"), sem("pool_out"), sem("pool_scaled"), sem("pool_hi"), sem("pool_done"))
        s_ready, a_done, ret_out, ret_sq, ret_ss, ret_std, ret_rstd, ret_copied = (
            sem("s_ready"), sem("a_done"), sem("ret_out"), sem("ret_sq"), sem("ret_ss"), sem("ret_std"), sem("ret_rstd"),
            sem("ret_copied"))
        gr_silu, gr_prod, gr_hi, gr_done = sem("gr_silu"), sem("gr_prod"), sem("gr_hi"), sem("gr_done")
        branch_out, mix_sum, mg_hi, mg_done = sem("branch_out"), sem("mix_sum"), sem("mg_hi"), sem("mg_done")
        out_tr, out_copied, out_stored = sem("out_tr"), sem("out_copied"), sem("out_stored")

        GAINS = {"ffn1": COL_AT["g_ffn1"], "mix": COL_AT["g_mix"], "ffn2": COL_AT["g_ffn2"], "final": COL_AT["g_final"],
                 "pool": COL_AT["pool_scale"]}

        def cols(name, at, n=1):
            return col[:, COL_AT[name] + at:COL_AT[name] + at + n]

        def mod_col(part, k, ctx_=0):
            return modc[:, KD * part + k, ctx_:ctx_ + 1]

        def live(d, j):
            return slice(P * j, T) if d == 0 else slice(0, P * j + P)

        def gains(at):
            return lambda k: col[:, at + k:at + k + 1]

        def image(ap):
            return ap.rearrange("p (r c) -> p r c", c=GRID[1])

        def mod_out(a, b):
            return pm[1][:, 0, 2 * a:2 * b].rearrange("p (t j) -> p t j", j=2)

        def halves(ap, w):
            return ap.rearrange("p (n w) -> p n w", w=w)

        def ffn_slab(l, f):
            return BASE_SLAB + l * (2 * FFN_SLABS + MIX_SLABS) + f * (FFN_SLABS + MIX_SLABS)

        def ffn_use(l, f):
            return BASE_USE + l * (2 * FFN_USES + MIX_USES) + f * (FFN_USES + MIX_USES)

        def mix_slab(l):
            return ffn_slab(l, 0) + FFN_SLABS

        def mix_use(l):
            return ffn_use(l, 0) + FFN_USES


        def wait(eng, s, n):
            if not isinstance(n, int) or n > 0:
                eng.wait_ge(s, n)

        def slab_view(w, l, c0):
            return w[l].rearrange("(k p) n -> p k n", p=P)[:, :, c0:c0 + SLAB] if isinstance(c0, int) else \
                w[l].rearrange("(k p) n -> p k n", p=P)[:, :, bass.ds(c0, SLAB)]

        block = ctx.enter_context(nc.Block())

        @block.sync
        def _(sp):
            sp.dma_start(ident[:], io["c_ident"]).then_inc(const_loaded, 16)
            for dst, name in ((col, "cols"), (bsel, "c_bsel"), (mlmask, "c_mlmask")):
                sp.dma_start(dst[:], io[name]).then_inc(const_loaded, 16)
            sp.dma_start(cx[:], io["ctxT"].rearrange("(k p) t -> p k t", p=P)).then_inc(ctx_loaded, 16)
            wm = io["w_mod"][0].rearrange("(k p) n -> p k n", p=P)
            for b in range(2):
                sp.dma_start(raw[b][:], wm[:, :, SLAB * b:SLAB * b + SLAB]).then_inc(mod_loaded[b], 16)
            sp.dma_start(x[:], io["xT"].rearrange("(k p) t -> p k t", p=P)).then_inc(x_loaded, 16)
            with sp.Fori(1, MOD_FIRST // 2) as j:
                for b in range(2):
                    sp.wait_ge(mod_used, 2 * j + b - 1)
                    sp.sem_inc(stick, 1)
                    sp.dma_start(raw[b][:], wm[:, :, bass.ds(2 * SLAB * j + SLAB * b, SLAB)]).then_inc(mod_loaded[b], 16)
            for i, (name, c0) in enumerate(IN1):
                if i < 2:
                    sp.wait_ge(mod_used, MOD_FIRST - 1 + i)
                else:
                    sp.wait_ge(split_done, 2 + i - 1)
                if name == "gate":
                    src = io["w_in"][0].rearrange("(h k p) n -> h p k n", p=P, h=2)[i - 6][:, :, c0:c0 + P]
                    dst = raw[i % 2][:].rearrange("p k n -> p (k n)")[:, 0:KD // 2 * P].rearrange("p (k n) -> p k n", n=P)
                    sp.dma_start(dst, src).then_inc(raw_loaded[i % 2], 16)
                else:
                    sp.dma_start(raw[i % 2][:], slab_view(io["w_in"], 0, c0)).then_inc(raw_loaded[i % 2], 16)
            for b in range(2):
                sp.wait_ge(split_done, OUT1_AT + b - 1)
                sp.dma_start(raw[b][:], wm[:, :, SLAB * (MOD_FIRST + b):SLAB * (MOD_FIRST + b) + SLAB]).then_inc(mod_loaded[b], 16)
            with sp.Fori(MOD_FIRST // 2 + 1, MOD_SLABS // 2) as j:
                for b in range(2):
                    sp.wait_ge(mod_used, 2 * j + b - 1)
                    sp.sem_inc(stick, 1)
                    sp.dma_start(raw[b][:], wm[:, :, bass.ds(2 * SLAB * j + SLAB * b, SLAB)]).then_inc(mod_loaded[b], 16)
            for i in range(OUT1_SLABS):
                if i < 2:
                    sp.wait_ge(mod_used, MOD_SLABS - 1 + i)
                else:
                    sp.wait_ge(split_done, OUT1_AT + i - 1)
                sp.dma_start(raw[i % 2][:], slab_view(io["w_out"], 0, SLAB * i)).then_inc(raw_loaded[i % 2], 16)
            with sp.Fori(0, UP_STEPS) as j:
                for b in range(2):
                    sp.wait_ge(split_done, UP1_AT + b - 1 + 2 * j)
                    sp.sem_inc(stick, 1)
                    sp.dma_start(raw[b][:], slab_view(io["w_up"], 0, FF * b + SLAB * j)).then_inc(raw_loaded[b], 16)
            down1 = io["w_down"][0].rearrange("(h k p) n -> h p k n", p=P, h=2)
            with sp.Fori(0, KD) as n:
                for b in range(2):
                    sp.wait_ge(split_done, DOWN1_AT + b - 1 + 2 * n)
                    sp.sem_inc(stick, 1)
                    sp.dma_start(raw[b][:].rearrange("p k n -> p (k n)")[:, 0:DOWN_K * P].rearrange("p (k n) -> p k n", n=P),
                                 down1[b][:, :, bass.ds(P * n, P)]).then_inc(raw_loaded[b], 16)

            def ffn(l, f):
                w1, w3, w2 = (io[f"{n}_ffn{f + 1}_2"] for n in ("w1", "w3", "w2"))
                s0 = ffn_slab(l, f)
                with sp.Fori(0, UP_STEPS) as j:
                    for b, w in ((0, w1), (1, w3)):
                        sp.wait_ge(split_done, s0 + b - 1 + 2 * j)
                        sp.sem_inc(stick, 1)
                        sp.dma_start(raw[b][:], slab_view(w, l, SLAB * j)).then_inc(raw_loaded[b], 16)
                s1 = s0 + 2 * UP_STEPS
                w2v = w2[l].rearrange("(h k p) n -> h p k n", p=P, h=2)
                with sp.Fori(0, KD) as n:
                    for b in range(2):
                        sp.wait_ge(split_done, s1 + b - 1 + 2 * n)
                        sp.sem_inc(stick, 1)
                        sp.dma_start(raw[b][:].rearrange("p k n -> p (k n)")[:, 0:DOWN_K * P].rearrange("p (k n) -> p k n", n=P),
                                     w2v[b][:, :, bass.ds(P * n, P)]).then_inc(raw_loaded[b], 16)

            def mix(l):
                s0 = mix_slab(l)
                win = io["w_in_2"]
                order = [COL["q_sb"], COL["k_sb"], COL["v_sb"], COL["q_r"], COL["k_r"], COL["v_r"], COL["v_r"] + SLAB, COL["u"],
                         COL["g_r"], COL["g_r"] + SLAB]
                for i, c0 in enumerate(order):
                    sp.wait_ge(split_done, s0 + i - 1)
                    sp.dma_start(raw[i % 2][:], slab_view(win, l, c0)).then_inc(raw_loaded[i % 2], 16)
                with sp.Fori(0, 4) as j:
                    for g in range(3):
                        sp.wait_ge(split_done, s0 + 10 + g - 1 + 4 * j)
                        sp.sem_inc(stick, 1)
                        sp.dma_start(raw[g % 2][:], slab_view(win, l, COL["gate"] + g * D + SLAB * j)).then_inc(raw_loaded[g % 2], 16)
                    sp.wait_ge(split_done, s0 + 13 - 1 + 4 * j)
                    sp.sem_inc(stick, 1)
                    for k0, n, name in ((0, 2, "sb"), (2, 4, "ret"), (6, 2, "pool")):
                        sp.dma_start(raw[1][:, k0:k0 + n, :], slab_view(io[f"w_branch_{name}_2"], l, SLAB * j)).then_inc(raw_loaded[1], 16)
                with sp.Fori(0, 2) as j:
                    for b in range(2):
                        sp.wait_ge(split_done, s0 + 26 + b - 1 + 2 * j)
                        sp.sem_inc(stick, 1)
                        sp.dma_start(raw[b][:], slab_view(io["w_out_2"], l, SLAB * (2 * j + b))).then_inc(raw_loaded[b], 16)

            for l in range(LAYERS):
                ffn(l, 0)
                mix(l)
                ffn(l, 1)
            ov = io["out"].rearrange("b (t p) (k q) -> p (b t) k q", p=P, q=P)
            for k in range(KD):
                sp.wait_ge(out_copied, k + 1)
                sp.dma_start(ov[:, :, k, :], x[:, k, :].rearrange("p (t q) -> p t q", q=P)).then_inc(out_stored, 16)
            sp.wait_ge(out_stored, 16 * KD)

        EXTRA = 2 * 4

        def loads_before(l, stage, b):
            n = (BASE_SLAB - 2) // 2 + l * (2 * FFN_SLABS + MIX_SLABS) // 2 + (EXTRA * l if b == 1 else 0)
            if stage >= 1:
                n += FFN_SLABS // 2
            if stage >= 2:
                n += MIX_SLABS // 2 + (EXTRA if b == 1 else 0)
            return n

        @block.gpsimd
        def _(pool):
            nc.gpsimd.memset(ones[:], 1.0).then_inc(const_made, 1)
            nc.gpsimd.memset(eps[:], EPS).then_inc(const_made, 1)
            for b in range(2):
                nc.gpsimd.memset(pad[b][:], 0.0).then_inc(pad_zeroed, 1)
            pool.sem_inc(split_done, 2)
            pool.sem_inc(slab_used, 2)

            def split(idx, b, loaded, n=8 * SLAB):
                pool.wait_ge(raw_loaded[b], 16 * loaded)
                pool.wait_ge(slab_used, idx - 1)
                pool.sem_inc(tick, 1)
                r, h, o = (a[b][:].rearrange("p k n -> p (k n)")[:, 0:n] for a in (raw, whi, wlo))
                nc.gpsimd.tensor_scalar(h, r, 1.0, 1.0, ALU.mult, ALU.mult).then_inc(hi_done, 1)
                pool.wait_ge(hi_done, idx - 1)
                nc.gpsimd.tensor_tensor(o, r, h.bitcast(F32), ALU.subtract).then_inc(split_done, 1)

            def ffn(l, f):
                s0 = ffn_slab(l, f)
                with pool.Fori(0, UP_STEPS) as j:
                    for b in range(2):
                        split(s0 + b + 2 * j, b, loads_before(l, 2 * f, b) + 1 + j)
                with pool.Fori(0, KD) as n:
                    for b in range(2):
                        split(s0 + 2 * UP_STEPS + b + 2 * n, b, loads_before(l, 2 * f, b) + UP_STEPS + 1 + n, DOWN_K * P)

            def mix(l):
                s0 = mix_slab(l)
                for i in range(10):
                    split(s0 + i, i % 2, loads_before(l, 1, i % 2) + i // 2 + 1)
                n0, n1 = (loads_before(l, 1, b) + 5 for b in range(2))
                with pool.Fori(0, 4) as j:
                    split(s0 + 10 + 4 * j, 0, n0 + 1 + 2 * j)
                    split(s0 + 11 + 4 * j, 1, n1 + 1 + 4 * j)
                    split(s0 + 12 + 4 * j, 0, n0 + 2 + 2 * j)
                    split(s0 + 13 + 4 * j, 1, n1 + 4 + 4 * j)
                with pool.Fori(0, 2) as j:
                    split(s0 + 26 + 2 * j, 0, n0 + 9 + j)
                    split(s0 + 27 + 2 * j, 1, n1 + 17 + j)

            for i, (name, _) in enumerate(IN1):
                split(2 + i, i % 2, i // 2 + 1, KD // 2 * P if name == "gate" else 8 * SLAB)
            for n in range(HG_N):
                h, d = n // 2, n % 2
                for m in range(LEVELS):
                    lev = LEVELS * n + m
                    pool.wait_ge(hx_exp, 2 * lev + 2)
                    if lev >= 2:
                        pool.wait_ge(ha_ready, lev - 1)
                    half = 2 ** m
                    lo = slice(0, half)
                    src = hz[0][:, h, 0:T] if d == 0 else hq[:, h, :]
                    nc.gpsimd.tensor_tensor(halves(xl[lev % 2][:], 2 * half)[:, :, lo], halves(src, 2 * half)[:, :, lo],
                                            halves(yl[lev % 2][:], 2 * half)[:, :, lo], ALU.mult).then_inc(hx_lo, 1)
            for i in range(OUT1_SLABS):
                split(OUT1_AT + i, i % 2, (IN1_SLABS + i) // 2 + 1)
            up_loads = (IN1_SLABS + OUT1_SLABS) // 2
            with pool.Fori(0, UP_STEPS) as j:
                for b in range(2):
                    split(UP1_AT + b + 2 * j, b, up_loads + 1 + j)
            with pool.Fori(0, KD) as n:
                for b in range(2):
                    split(DOWN1_AT + b + 2 * n, b, up_loads + UP_STEPS + 1 + n, DOWN_K * P)

            for l in range(LAYERS):
                ffn(l, 0)
                mix(l)
                ffn(l, 1)

        def act_squares(act, n, src, W, made=None):
            for k in range(KD):
                if made is not None:
                    act.wait_ge(hn_done, 8 * made + k + 1)
                if 8 * n + k >= 2:
                    act.wait_ge(sq_summed, 8 * n + k - 1)
                nc.scalar.activation(sq[k % 2][:, 0:W], src[:, k, :], ACT.Square).then_inc(sq_done, 1)

        def act_squares_down(act, n, u1):
            with act.Fori(0, KD // 2) as j:
                for i in range(2):
                    act.wait_ge(pm_free[i], u1 + 1 + j)
                    act.wait_ge(sq_summed, 8 * n + i - 1 + 2 * j)
                    act.sem_inc(atick, 1)
                    nc.scalar.activation(sq[i][:].rearrange("p (o t) -> p o t", o=1), x[:, bass.ds(2 * j + i, 1), :], ACT.Square).then_inc(sq_done, 1)

        def act_root(act, n, W=T):
            act.wait_ge(sq_summed, 8 * n + KD)
            if n:
                act.wait_ge(rstd_done, n)
            nc.scalar.activation(std[:, 0:W], pa[0][:, 0:W], ACT.Sqrt, bias=eps[:], scale=1.0 / D).then_inc(std_done, 1)

        @block.scalar
        def _(act):
            act.wait_ge(const_loaded, 16 * 4)
            act.wait_ge(const_made, 2)
            nc.scalar.activation(silc[:], cols("c", 0, 16).rearrange("p (k j) -> p k j", j=2), ACT.Silu).then_inc(mod_in, 1)
            act.wait_ge(lb_step, 3)
            nc.scalar.activation(lbe[:], lbe[:], ACT.Exp).then_inc(lb_exp, 1)

            def norm_h(n, nh, src=x, W=T, hi=hh, shift=None, squares=True, made=None):
                if squares:
                    act_squares(act, n, src, W, made)
                act_root(act, n, W)
                for k in range(KD):
                    act.wait_ge(hn_done, 8 * n + k + 1)
                    if shift is None:
                        nc.scalar.activation(hi[:, k, :], hn[k % 2][:, 0:W], ACT.Copy).then_inc(hh_done, 1)
                    else:
                        nc.scalar.activation(hi[:, k, :], hn[k % 2][:, 0:W], ACT.Identity, bias=shift(k)).then_inc(hh_done, 1)

            def head_norm(e, y4):
                nc.scalar.activation(sq4[:], y4[:], ACT.Square).then_inc(t_sq, 1)
                for h in range(4):
                    act.wait_ge(t_ss, 4 * e + h + 1)
                    nc.scalar.activation(sq4[:, h, :], pa[h][:], ACT.Sqrt, bias=eps[:], scale=1.0 / HEAD_DIM).then_inc(t_std, 1)

            def first():
                act.wait_ge(ctx_loaded, 16)
                act.wait_ge(mod_done, 5)
                norm_h(0, 0, cx, CT, ch, lambda k: mod_col(0, k, 1))
                act.wait_ge(x_loaded, 16)
                norm_h(1, 1, shift=lambda k: mod_col(0, k))
                act.wait_ge(pad_zeroed, 2)
                act.wait_ge(hl_done, 16)
                for t in range(2):
                    nc.scalar.activation(cpad[t][:, 0:1], eps[:], ACT.Copy, scale=0.0).then_inc(cpad_filled, 1)
                    nc.scalar.activation(cpad[t][:, CT + 1:CT + 2], eps[:], ACT.Copy, scale=0.0).then_inc(cpad_filled, 1)
                for i in range(4):
                    p = IN1_P[i]
                    act.wait_ge(slab_used, 2 + i + 1)
                    for t in range(2):
                        if i:
                            act.wait_ge(conv_step, CONV_AT[2 * (i - 1) + t + 1])
                        if t == 1:
                            act.wait_ge(pad_filled, i + 1)
                        nc.scalar.activation(pad[t][:, 1:GRID[0] + 1, 1:GRID[1] + 1], image(pm[p][:, t, :]), ACT.Copy).then_inc(
                            pm_free[p] if t else pad_filled, 1)
                        if i >= 2:
                            if t == 1:
                                act.wait_ge(cpad_filled, 4 + i - 1)
                            nc.scalar.activation(cpad[t][:, 1:CT + 1], pa[p][:, CT * t:CT * t + CT], ACT.Copy).then_inc(
                                ctx_free[p] if t else cpad_filled, 1)
                    for t in range(2):
                        act.wait_ge(conv_step, CONV_AT[2 * i + t + 1])
                        dst, w = (mq[:, 2 * i + t, :], T) if i < 2 else (mk[:, 2 * i + t - 4, :], TA)
                        nc.scalar.activation(dst, cacc[t][:, 0:w], ACT.Silu).then_inc(conv_silu, 1)
                def tokens(i, dst, e):
                    p = IN1_P[i]
                    act.wait_ge(slab_used, 2 + i + 1)
                    c = slice(SLAB * e, SLAB * e + SLAB)
                    nc.scalar.activation(dst[:, 0:TT, c], pm[p][:].rearrange("p a (b c) -> p (a b) c", b=2), ACT.Copy).then_inc(pm_free[p], 1)
                    nc.scalar.activation(dst[:, TT:TAT, c], pa[p][:].rearrange("p (b c) -> p b c", b=2), ACT.Copy).then_inc(ctx_free[p], 1)

                for e in range(2):
                    tokens(4 + e, mv, e)
                act.wait_ge(slab_used, 2 + 8)
                nc.scalar.activation(gall[:, 0:T], pm[0][0:16, 0, :], ACT.Copy).then_inc(pm_free[0], 1)
                nc.scalar.activation(gall[:, T:TA], pa[0][0:16, 0:CT], ACT.Copy).then_inc(ctx_free[0], 1)
                for g in range(4):
                    d = g // 2
                    dst = (GI, GF)[g % 2][d]
                    gb = col[0:4, COL_AT["gate_b"] + g:COL_AT["gate_b"] + g + 1]
                    act.wait_ge(gsel_ready, 2 * g + 1)
                    nc.scalar.activation(dst[:, LATC[d]], pa[2][0:4, :], ACT.Identity, bias=gb).then_inc(gsel_copied, 1)
                    act.wait_ge(gsel_ready, 2 * g + 2)
                    nc.scalar.activation(dst[:, CTXC[d]], pa[3][0:4, 0:CT], ACT.Identity, bias=gb).then_inc(gsel_copied, 1)
                act.wait_ge(gsel_copied, 8)
                for d in range(2):
                    nc.scalar.activation(GT[d][:], GF[d][:], ACT.Abs).then_inc(gact, 1)
                    act.wait_ge(gact, 3 * d + 1)
                    nc.scalar.activation(GT[d][:], GT[d][:], ACT.Exp, scale=-1.0).then_inc(gact, 1)
                    act.wait_ge(gact, 3 * d + 2)
                    nc.scalar.activation(GT[d][:], GT[d][:], ACT.Ln, bias=1.0).then_inc(gact, 1)
                for d in range(2):
                    act.wait_ge(gstep, 6 * d + 6)
                    nc.scalar.activation(GT[d][:, LATC[d]], GT[d][:, LATC[d]], ACT.Exp, scale=-1.0).then_inc(gdn, 1)
                act.wait_ge(gtr, 1)
                nc.scalar.activation(gcol[:], pa[2][:, 0:2 * TAT * ML_HEADS].rearrange("p (d t h) -> p d t h", d=2, h=ML_HEADS),
                                     ACT.Copy).then_inc(gcol_done, 1)
                for e in range(2):
                    p = IN1_P[8 + e]
                    act.wait_ge(slab_used, 2 + 8 + e + 1)
                    nc.scalar.activation(mo[:, 2 * e:2 * e + 2, :], pm[p][:], ACT.Sigmoid).then_inc(pm_free[p], 1)
                act.wait_ge(gcol_done, 1)
                for h in range(ML_HEADS):
                    for d in range(2):
                        n = 2 * h + d
                        act.wait_ge(mb_ready, 2 * n + 1)
                        if h:
                            act.wait_ge(ml_h, 5 * (n - 2) + 1)
                        nc.scalar.activation(dnb[d][:], pa[2 + d][:], ACT.Copy).then_inc(mb_copied, 1)
                        act.wait_ge(mb_ready, 2 * n + 2)
                        if h:
                            act.wait_ge(w_exp, 12 * h - 1 + d)
                            act.wait_ge(w_pre, 8 * h - 1 + d)
                        nc.scalar.activation(nmb[d][:], pa[2 + d][:], ACT.Copy).then_inc(mb_copied, 1)
                    for i in range(TAT):
                        s = TAT * h + i
                        for d in range(2):
                            n, r = 2 * h + d, 2 * s + d
                            if i < 2:
                                act.wait_ge(mb_copied, 2 * n + 2)
                                if r >= 4:
                                    act.wait_ge(a_made, r - 3)
                                nc.scalar.activation(wt[d][s % 2][:], nmb[d][:], ACT.Exp, scale=-1.0,
                                                     bias=gcol[:, d, TT + i, h:h + 1]).then_inc(w_exp, 1)
                            else:
                                act.wait_ge(w_pre, 8 * h + 2 * (i - 2) + d + 1)
                                c = live(d, i - 2)
                                nc.scalar.activation(wt[d][s % 2][:, c], wt[d][s % 2][:, c], ACT.Exp, scale=-1.0).then_inc(w_exp, 1)
                    for d in range(2):
                        act.wait_ge(nd_acc, 12 * h + 10 + d + 1)
                        if h:
                            act.wait_ge(ml_h, 5 * (2 * h - 2 + d) + 5)
                        nc.scalar.activation(dab[d][:], pm[d][:, 1, :], ACT.Abs).then_inc(den_abs, 1)
                act.wait_ge(ml_h, 5 * 2 * ML_HEADS)
                head_norm(0, mq)
                act.wait_ge(t_done, 1)
                for i in range(10, IN1_SLABS):
                    name, e, p = IN1[i][0], i % 2, IN1_P[i]
                    act.wait_ge(slab_used, 2 + i + 1)
                    if name == "hv":
                        tokens(i, hv, e)
                    elif name in ("hq", "hg"):
                        dst = hq if name == "hq" else hg
                        nc.scalar.activation(dst[:, 2 * e:2 * e + 2, :], pm[p][:], ACT.Silu).then_inc(pm_free[p], 1)
                    else:
                        dst = hz[name == "zb"]
                        nc.scalar.activation(dst[:, 2 * e:2 * e + 2, 0:T], pm[p][:], ACT.Copy).then_inc(pm_free[p], 1)
                        nc.scalar.activation(dst[:, 2 * e:2 * e + 2, T:TA], pa[p][:].rearrange("p (b c) -> p b c", b=2),
                                             ACT.Copy).then_inc(ctx_free[p], 1)
                act.dma_start(hgmask[:], io["c_hgmask"]).then_inc(hgmask_loaded, 16)
                for p in range(2):
                    act.wait_ge(pm_free[p], HG_USE)
                    act.wait_ge(ctx_free[p], ctx_uses_[p])
                for d in range(2):
                    nc.scalar.activation(hf[d][:], hz[d][:], ACT.Sigmoid).then_inc(hg_sig, 1)
                    act.wait_ge(hg_sig, 2 * d + 1)
                    nc.scalar.activation(hz[d][:], hz[d][:], ACT.Sigmoid, scale=-1.0).then_inc(hg_sig, 1)
                for d in range(2):
                    act.wait_ge(hg_step, 2 + 8 * (d + 1))
                    nc.scalar.activation(hf[d][:], hf[d][:], ACT.Ln).then_inc(hg_ln, 1)
                act.wait_ge(hg_step, 2 + 16 + 8 + 12)
                nc.scalar.activation(epend[:], pend[:], ACT.Exp).then_inc(hep_done, 1)
                def decays(n):
                    h, d = n // 2, n % 2
                    act.wait_ge(hdb, n + 1)
                    nc.scalar.activation(ea[:], hf[d][:, h, :], ACT.Exp).then_inc(heab, 1)
                    nc.scalar.activation(eb[:], eb[:], ACT.Exp).then_inc(heab, 1)

                decays(0)
                for n in range(HG_N):
                    for m in range(LEVELS):
                        lev, half = LEVELS * n + m, 2 ** m
                        act.wait_ge(hy_done, lev + 1)
                        y = halves(yl[lev % 2][:], 2 * half)
                        for part, sign in ((slice(half, 2 * half), 1.0), (slice(0, half), -1.0)):
                            nc.scalar.activation(y[:, :, part], y[:, :, part], ACT.Exp, scale=sign).then_inc(hx_exp, 1)
                        if m == 0:
                            act.wait_ge(ht_ready, 2 * n + 1)
                            if n:
                                act.wait_ge(hkv_ready, n)
                            nc.scalar.activation(ktok[:, 0:4, :], pa[2][:].rearrange("p (c k) -> p c k", k=P), ACT.Copy).then_inc(ht_copied, 1)
                            act.wait_ge(ht_ready, 2 * n + 2)
                            nc.scalar.activation(ktok[:, 4, :], pa[3][:, 0:P], ACT.Copy).then_inc(ht_copied, 1)
                        if m == 3 and n + 1 < HG_N:
                            decays(n + 1)
                act.wait_ge(pm_free[0], OUT1_USE)
                head_norm(1, hq)
                act.wait_ge(x_mixed, OUT1_SLABS)
                for p in range(2):
                    act.wait_ge(pm_free[p], UP1_USE)
                norm_h(2, 2, shift=lambda k: mod_col(3, k))
                act.wait_ge(pad_filled, 4)
                with act.Fori(0, UP_STEPS) as j:
                    for b in range(2):
                        act.wait_ge(slab_used, UP1_AT + 1 + b + 2 * j)
                        for i in range(2):
                            act.wait_ge(conv_step, CONV1 + 18 * b - 9 + 9 * i + 36 * j)
                            if i == 1:
                                act.wait_ge(pad_filled, 4 + b + 1 + 2 * j)
                            nc.scalar.activation(pad[i][:, 1:GRID[0] + 1, 1:GRID[1] + 1], image(pm[b][:, i, :]), ACT.Copy).then_inc(
                                pm_free[b] if i else pad_filled, 1)
                    act.wait_ge(conv_step, CONV1 + 18 + 36 * j)
                    nc.scalar.activation(sil[0][:], sil[0][:], ACT.Silu).then_inc(usilu_done, 1)
                act_squares_down(act, 3, DOWN1_USE)
                act_root(act, 3)

            first()

            def ffn(l, f):
                s0, u0 = ffn_slab(l, f), ffn_use(l, f)
                n = NORMS1 + 3 * l + 2 * f
                if f:
                    for p in range(2):
                        act.wait_ge(pm_free[p], u0)
                norm_h(n, n - 1, squares=f == 1 or l == 0, made=None if f or l else NORMS1 - 1)
                with act.Fori(0, UP_STEPS) as j:
                    act.wait_ge(pm_free[1], u0 + j)
                    act.wait_ge(slab_used, s0 + 1 + 2 * j)
                    nc.scalar.activation(sil[0][:], pm[0][:], ACT.Silu).then_inc(pm_free[0], 1)
                act_squares_down(act, n + 1, u0 + UP_STEPS)

            def mix(l):
                s0, u0 = mix_slab(l), mix_use(l)
                n = NORMS1 + 3 * l + 1
                for p in range(2):
                    act.wait_ge(pm_free[p], u0)
                for dst, name in ((decay, "c_decay"), (rope, "c_rope"), (perm, "c_perm"), (trineg, "c_trineg"), (onesneg, "c_onesneg"),
                                  (dmask, "c_dmask"), (invcnt, "c_invcnt")):
                    act.dma_start(dst[:], io[name]).then_inc(mixc_loaded, 16)
                act.wait_ge(mixc_made, 4 * l + 1)
                for g in range(4):
                    o = 64 * (g % 2)
                    act.dma_start(wpool[o:o + 64, g // 2, o:o + 64], io["w_pool_2"][l, g]).then_inc(mixc_loaded, 16)
                norm_h(n, n - 1, squares=False)
                act.wait_ge(slab_used, s0 + 1)
                nc.scalar.activation(q_sb[:], pm[0][:], ACT.Copy, scale=SB_DIM ** -0.5).then_inc(pm_free[0], 1)
                act.wait_ge(slab_used, s0 + 2)
                nc.scalar.activation(k_sb[:], pm[1][:], ACT.Copy).then_inc(pm_free[1], 1)
                act.wait_ge(slab_used, s0 + 3)
                nc.scalar.activation(v_sb[:], pm[0][:].rearrange("p a (b c) -> p (a b) c", b=2), ACT.Copy).then_inc(pm_free[0], 1)
                nc.scalar.preload_act_table_set("natural_log_exp_and_others")

                def fill(i):
                    act.wait_ge(slab_used, s0 + i + 1)
                    if i == 3:
                        nc.scalar.activation(rraw[0][:], pm[1][:], ACT.Copy).then_inc(pm_free[1], 1)
                    elif i == 4:
                        nc.scalar.activation(rraw[1][:], pm[1][:], ACT.Copy, scale=RET_DIM ** -0.5).then_inc(pm_free[1], 1)
                    elif i in (5, 6):
                        nc.scalar.activation(v_r[:, :, SLAB * (i - 5):SLAB * (i - 4)], pm[1][:].rearrange("p a (b c) -> p (a b) c", b=2),
                                             ACT.Copy).then_inc(pm_free[1], 1)
                    elif i == 7:
                        act.wait_ge(mixc_made, 4 * l + 4)
                        nc.scalar.activation(u[:, :, PAD:], pm[1][:], ACT.Copy).then_inc(pm_free[1], 1)
                    else:
                        nc.scalar.activation(sil[i - 8][:], pm[1][:], ACT.Silu).then_inc(pm_free[1], 1)

                for h in range(SB_HEADS):
                    m = TT * (SB_HEADS * l + h)
                    for j in range(TT):
                        c = slice(LIVE_AT[j], LIVE_AT[j] + LIVE[j])
                        act.wait_ge(z_ready, m + j + 1)
                        if m + j >= TT:
                            act.wait_ge(sp_done, m + j + 1 - TT)
                        nc.scalar.activation(sc[:, c], pa[j][:, 0:LIVE[j]], ACT.Abs).then_inc(abs_done, 1)
                        act.wait_ge(abs_done, m + j + 1)
                        nc.scalar.activation(sc[:, c], sc[:, c], ACT.Exp, scale=-1.0).then_inc(exp_done, 1)
                        act.wait_ge(exp_done, m + j + 1)
                        nc.scalar.activation(sc[:, c], sc[:, c], ACT.Ln, bias=1.0).then_inc(ln_done, 1)
                    fill(3 + 2 * h)
                    for n_, j in enumerate(reversed(range(TT))):
                        c = slice(LIVE_AT[j], LIVE_AT[j] + LIVE[j])
                        act.wait_ge(w_masked, m + n_ + 1)
                        if m:
                            act.wait_ge(sb_out, SB_HEADS * l + h)
                        nc.scalar.activation(w_[:, c], pa[j][:, 0:LIVE[j]], ACT.Exp).then_inc(w_done, 1)
                    if h + 1 < SB_HEADS:
                        fill(4 + 2 * h)

                def gate(g, j):
                    act.wait_ge(slab_used, s0 + 10 + g + 1 + 4 * j)
                    nc.scalar.activation(gates[:, g], pm[g % 2][:], ACT.Sigmoid).then_inc(pm_free[g % 2], 1)

                gate(0, 0)
                gate(1, 0)
                for g in range(2):
                    act.wait_ge(pool_out, 2 * l + g + 1)
                    nc.scalar.activation(pt[:, g, :], pa[g][:], ACT.Copy, scale=col[:, GAINS["pool"] + 2 * l + g:GAINS["pool"] + 2 * l + g + 1]).then_inc(pool_scaled, 1)
                for h in range(RET_HEADS):
                    m = RET_HEADS * l + h
                    p = h % 2
                    act.wait_ge(ret_out, m + 1)
                    if m >= 1:
                        act.wait_ge(ret_ss, m)
                    nc.scalar.activation(ret_sqr[:], pm[p][:, 0, :], ACT.Square).then_inc(ret_sq, 1)
                    act.wait_ge(ret_ss, m + 1)
                    if m >= 1:
                        act.wait_ge(ret_rstd, m)
                    nc.scalar.activation(ret_root[:], pm[p][:, 1, :], ACT.Sqrt, bias=eps[:], scale=1.0 / P).then_inc(ret_std, 1)
                gate(2, 0)
                with act.Fori(1, 4) as j:
                    act.wait_ge(mix_sum, 1 + 3 * (4 * l) + 3 * j)
                    for g in range(3):
                        gate(g, j)

            for l in range(LAYERS):
                ffn(l, 0)
                mix(l)
                ffn(l, 1)
            act_root(act, NORMS1 + 3 * LAYERS)

        def dve_norm(v, n, nh, gain, out=None, src=x, W=T, hi=hh, lo=hl, shift=None):
            v.wait_ge(std_done, n + 1)
            if n:
                v.wait_ge(hn_done, 8 * n)
            nc.vector.reciprocal(rstd[:, 0:W], std[:, 0:W]).then_inc(rstd_done, 1)
            v.wait_ge(rstd_done, n + 1)
            def scaled(k):
                dst = hn[k % 2][:, 0:W] if out is None else out[:, k, :]
                if out is None and 8 * nh + k >= 2:
                    v.wait_ge(hl_done, 8 * nh + k - 1)
                nc.vector.scalar_tensor_tensor(dst, src[:, k, :], gain(k), rstd[:, 0:W], ALU.mult, ALU.mult).then_inc(hn_done, 1)

            def low(k):
                v.wait_ge(hh_done, 8 * nh + k + 1)
                v.wait_ge(hn_done, 8 * n + k + 1)
                if shift is None:
                    nc.vector.tensor_tensor(lo[:, k, :], hn[k % 2][:, 0:W], hi[:, k, :].bitcast(F32), ALU.subtract).then_inc(hl_done, 1)
                else:
                    nc.vector.scalar_tensor_tensor(lo[:, k, :], hn[k % 2][:, 0:W], shift(k), hi[:, k, :].bitcast(F32),
                                                   ALU.add, ALU.subtract).then_inc(hl_done, 1)

            for k in range(KD):
                scaled(k)
                if out is None and k:
                    low(k - 1)
            if out is None:
                low(KD - 1)

        @block.vector
        def _(v):
            for s in (hidden_done, mix_sum, mg_done):
                v.sem_inc(s, 1)
            v.wait_ge(const_loaded, 16 * 4)

            def lower_bounds():
                lg = cols("lb_logits", 0, 16).rearrange("p (j l h) -> p j l h", j=2, l=2)
                nc.vector.tensor_tensor(lbm[:], lg[:, :, 0, :], lg[:, :, 1, :], ALU.max).then_inc(lb_step, 1)
                v.wait_ge(lb_step, 1)
                for i in range(2):
                    nc.vector.tensor_tensor(lbe[:, :, i, :], lg[:, :, i, :], lbm[:], ALU.subtract).then_inc(lb_step, 1)
                v.wait_ge(lb_exp, 1)
                nc.vector.tensor_tensor(lbm[:], lbe[:, :, 0, :], lbe[:, :, 1, :], ALU.add).then_inc(lb_step, 1)
                v.wait_ge(lb_step, 4)
                nc.vector.reciprocal(oms[:], lbm[:]).then_inc(lb_step, 1)
                v.wait_ge(lb_step, 5)
                nc.vector.tensor_tensor(lb[:], lbe[:, :, 0, :], oms[:], ALU.mult).then_inc(lb_step, 1)
                nc.vector.tensor_tensor(om[:], lbe[:, :, 1, :], oms[:], ALU.mult).then_inc(lb_step, 1)
                v.wait_ge(lb_step, 7)
                nc.vector.tensor_scalar_max(lb[:], lb[:], 2.0 ** -60).then_inc(lb_step, 1)
                nc.vector.tensor_scalar(oms[:], om[:], HEAD_SCALE, 1.0, ALU.mult, ALU.mult).then_inc(lb_step, 1)

            def conv_tile(c0, dst, w, taps):
                for n, (tap, view) in enumerate(taps):
                    if n:
                        v.wait_ge(conv_step, c0 + n)
                    if n == 0:
                        nc.vector.tensor_scalar(dst, view, w(tap), 1.0, ALU.mult, ALU.mult).then_inc(conv_step, 1)
                    else:
                        nc.vector.scalar_tensor_tensor(dst, view, w(tap), dst, ALU.mult, ALU.add).then_inc(conv_step, 1)

            def windows(src):
                return [(3 * dy + dx, src[:, dy:dy + GRID[0], dx:dx + GRID[1]]) for dy in range(3) for dx in range(3)]

            def head_norm(e, y4, gate, norm, hi, lo):
                b = 8 * e
                v.wait_ge(t_std, 4 * e + 4)
                nc.vector.reciprocal(sq4[:], sq4[:]).then_inc(t_step, 1)
                v.wait_ge(t_step, b + 1)
                for h in range(4):
                    nc.vector.scalar_tensor_tensor(y4[:, h, :], y4[:, h, :], cols(norm, h), sq4[:, h, :], ALU.mult, ALU.mult).then_inc(t_step, 1)
                v.wait_ge(t_step, b + 5)
                nc.vector.tensor_tensor(y4[:], y4[:], gate[:], ALU.mult).then_inc(t_step, 1)
                v.wait_ge(t_step, b + 6)
                nc.vector.tensor_copy(hi[:], y4[:]).then_inc(t_step, 1)
                v.wait_ge(t_step, b + 7)
                nc.vector.tensor_tensor(lo[:], y4[:], hi[:].bitcast(F32), ALU.subtract).then_inc(t_done, 1)
                v.sem_inc(t_step, 1)

            def mlstm():
                for i in range(8):
                    t, c0 = i % 2, CONV_AT[i]
                    v.wait_ge(pad_filled, i // 2 + 1)
                    if t:
                        v.wait_ge(pm_free[IN1_P[i // 2]], IN1_USE[i // 2] + 1)
                    if i >= 2:
                        v.wait_ge(conv_silu, i - 1)
                    conv_tile(c0, image(cacc[t][:, 0:T]), lambda tap: cols("ml_conv", 8 * tap + i), windows(pad[t]))
                    if i >= 4:
                        s = i // 2
                        v.wait_ge(cpad_filled, 4 + s - 1)
                        if t:
                            v.wait_ge(ctx_free[IN1_P[s]], IN1_CTX[s] + 1)
                        conv_tile(c0 + 9, cacc[t][:, T:TA], lambda tap: cols("ml_conv", 8 * tap + i),
                                  [(3 + dx, cpad[t][:, dx:dx + CT]) for dx in range(3)])
                for d in range(2):
                    b = 6 * d
                    way = slice(None) if d == 0 else slice(None, None, -1)
                    v.wait_ge(gsel_copied, 8)
                    v.wait_ge(gact, 3 * d + 3)
                    nc.vector.scalar_tensor_tensor(GF[d][:], GF[d][:], 0.0, GT[d][:], ALU.min, ALU.subtract).then_inc(gstep, 1)
                    v.wait_ge(gstep, b + 1)
                    nc.vector.tensor_tensor_scan(GT[d][:, way], GF[d][:, way], GF[d][:, way], 0.0, ALU.add, ALU.min).then_inc(gstep, 1)
                    v.wait_ge(gstep, b + 2)
                    nc.vector.tensor_tensor(GI[d][:], GI[d][:], GT[d][:], ALU.subtract).then_inc(gstep, 1)
                    v.wait_ge(gstep, b + 3)
                    nc.vector.tensor_tensor_scan(GF[d][:, way], GI[d][:, way], GI[d][:, way], 0.0, ALU.max, ALU.max).then_inc(gstep, 1)
                    v.wait_ge(gstep, b + 4)
                    nc.vector.tensor_tensor(GT[d][:], GT[d][:], GF[d][:], ALU.add).then_inc(gstep, 1)
                    v.wait_ge(gstep, b + 5)
                    nc.vector.tensor_scalar_max(GT[d][:], GT[d][:], -80.0).then_inc(gstep, 1)
                v.wait_ge(gcol_done, 1)

                def pre(s):
                    h, i = s // TAT, s % TAT
                    if i < 2:
                        return
                    for d in range(2):
                        n, r = 2 * h + d, 2 * s + d
                        v.wait_ge(mb_copied, 2 * n + 2)
                        v.wait_ge(a_made, r - 3)
                        c = live(d, i - 2)
                        nc.vector.tensor_scalar(wt[d][s % 2][:, c], nmb[d][:, c], gcol[:, d, i - 2, h:h + 1], 0.0,
                                                ALU.subtract, ALU.max).then_inc(w_pre, 1)

                for s in range(TAT * ML_HEADS):
                    h, i = s // TAT, s % TAT
                    if s + 1 < TAT * ML_HEADS:
                        pre(s + 1)
                    for d in range(2):
                        r = 2 * s + d
                        v.wait_ge(ms_ready, s + 1)
                        v.wait_ge(w_exp, r + 1)
                        if r >= 4:
                            v.wait_ge(nd_acc, r - 3)
                        c = slice(0, T) if i < 2 else live(d, i - 2)
                        a = aw[d][s % 2]
                        nc.vector.scalar_tensor_tensor(a[:, c], pa[s % 2][:, c], HEAD_SCALE, wt[d][s % 2][:, c], ALU.mult, ALU.mult).then_inc(a_made, 1)
                        if i >= 2:
                            v.wait_ge(a_made, r + 1)
                            dg = slice(P * (i - 2), P * (i - 1))
                            nc.vector.tensor_tensor(a[:, dg], a[:, dg], mlmask[:, d, :], ALU.mult).then_inc(a_masked, 1)
                    if i == TAT - 1:
                        for d in range(2):
                            n = 2 * h + d
                            b = 5 * n
                            v.wait_ge(den_abs, n + 1)
                            v.wait_ge(mb_copied, 2 * n + 1)
                            nc.vector.tensor_tensor(dab[d][:], dab[d][:], dnb[d][:], ALU.max).then_inc(ml_h, 1)
                            v.wait_ge(ml_h, b + 1)
                            nc.vector.reciprocal(dab[d][:], dab[d][:]).then_inc(ml_h, 1)
                            v.wait_ge(ml_h, b + 2)
                            dst = dab[d][:] if d else mq[:, h, :]
                            nc.vector.tensor_tensor(dst, pm[d][:, 0, :], dab[d][:], ALU.mult).then_inc(pm_free[d], 1)
                            v.wait_ge(pm_free[d], ML_USE + h + 1)
                            v.sem_inc(ml_h, 2)
                            if d:
                                nc.vector.tensor_tensor(mq[:, h, :], mq[:, h, :], dab[d][:], ALU.add).then_inc(ml_h, 1)
                            else:
                                v.sem_inc(ml_h, 1)
                head_norm(0, mq, mo, "ml_norm", ym_h, ym_l)

            def hgrn():
                v.wait_ge(slab_used, 2 + IN1_SLABS)
                nc.vector.memset(resetm[:], 1.0).then_inc(hg_step, 1)
                v.wait_ge(hg_step, 1)
                nc.vector.memset(halves(resetm[:], P)[:, :, 0:1], 0.0).then_inc(hg_step, 1)
                v.wait_ge(lb_step, 9)
                for d in range(2):
                    v.wait_ge(hg_sig, 2 * d + 2)
                    for h in range(HG_HEADS):
                        nc.vector.tensor_scalar(hf[d][:, h, :], hf[d][:, h, :], om[:, d, h:h + 1], lb[:, d, h:h + 1], ALU.mult, ALU.add).then_inc(hg_step, 1)
                        nc.vector.tensor_scalar(hz[d][:, h, :], hz[d][:, h, :], oms[:, d, h:h + 1], 1.0, ALU.mult, ALU.mult).then_inc(hg_step, 1)
                b = 2 + 16
                ends = slice(P - 1, P)
                v.wait_ge(hg_step, b)
                for h in range(HG_HEADS):
                    v.wait_ge(hg_ln, 1)
                    nc.vector.tensor_tensor_scan(hf[0][:, h, :], resetm[:], hf[0][:, h, :], 0.0, ALU.mult, ALU.add).then_inc(hg_step, 1)
                    v.wait_ge(hg_step, b + 1)
                    nc.vector.tensor_copy(pend[:, 0, h, :], halves(hf[0][:, h, :], P)[:, :, P - 1]).then_inc(hg_step, 1)
                    b += 2
                for h in range(HG_HEADS):
                    v.wait_ge(hg_ln, 2)
                    v.wait_ge(hg_step, b)
                    nc.vector.tensor_tensor_scan(ptmp[:], resetm[:], hf[1][:, h, :], 0.0, ALU.mult, ALU.add).then_inc(hg_step, 1)
                    v.wait_ge(hg_step, b + 1)
                    nc.vector.tensor_copy(pend[:, 1, h, :], halves(ptmp[:], P)[:, :, P - 1]).then_inc(hg_step, 1)
                    nc.vector.tensor_tensor(hf[1][:, h, :], ptmp[:], hf[1][:, h, :], ALU.subtract).then_inc(hg_step, 1)
                    b += 3
                v.wait_ge(hg_step, b)
                v.wait_ge(hep_done, 1)
                v.wait_ge(hgmask_loaded, 16)
                def chunk_end(n):
                    h, d = n // 2, n % 2
                    if n:
                        v.wait_ge(hkq, 2 * n)
                    nc.vector.tensor_tensor(halves(eb[:], P), pend[:, d, h, :].rearrange("p (c o) -> p c o", o=1).to_broadcast([P, TAT, P]),
                                            halves(hf[d][:, h, :], P), ALU.subtract).then_inc(hdb, 1)

                def keys(n):
                    h, d = n // 2, n % 2
                    v.wait_ge(heab, 2 * n + 2)
                    if n:
                        v.wait_ge(ht_ready, 2 * n)
                    nc.vector.tensor_tensor(kt[:], hz[d][:, h, :], (ea if d else eb)[:], ALU.mult).then_inc(hkq, 1)

                def output(h):
                    v.wait_ge(ho_ready, h + 1)
                    nc.vector.tensor_copy(hq[:, h, :], pm[0][:, 0, :]).then_inc(pm_free[0], 1)

                chunk_end(0)
                keys(0)
                for n in range(HG_N):
                    h, d = n // 2, n % 2
                    bd = hf[d][:, h, :]

                    def level_y(m):
                        lev, half = LEVELS * n + m, 2 ** m
                        if lev >= 2:
                            v.wait_ge(hx_up, lev - 1)
                            v.wait_ge(hx_lo, lev - 1)
                        b3 = halves(bd[:, 0:T], 2 * half)
                        nc.vector.tensor_tensor(halves(yl[lev % 2][:], 2 * half), b3,
                                                b3[:, :, half - 1 + d:half + d].to_broadcast([P, T // (2 * half), 2 * half]), ALU.subtract).then_inc(hy_done, 1)

                    def level_a(m):
                        lev = LEVELS * n + m
                        v.wait_ge(ha_ready, lev + 1)
                        if m == 0:
                            v.wait_ge(hd_copied, h + 1)
                        if lev:
                            v.wait_ge(ha_copied, lev)
                        nc.vector.copy_predicated(halves(ah[:], P),
                                                  hgmask[:, LEVELS * d + m, :].rearrange("p (o t) -> p o t", o=1).to_broadcast([P, TT, P]).bitcast(mybir.dt.uint32),
                                                  halves(pa[lev % 2][:], P)).then_inc(ha_copied, 1)

                    level_y(0)
                    level_y(1)
                    if d == 0 and h:
                        output(h - 1)
                    v.wait_ge(heab, 2 * n + 2)
                    nc.vector.tensor_tensor(qt[d][:], hq[:, h, :], (eb if d else ea)[:, 0:T], ALU.mult).then_inc(hkq, 1)
                    if d == 0:
                        v.wait_ge(hd_ready, h + 1)
                        nc.vector.tensor_tensor(halves(ah[:], P), halves(pm[0][:, 0, :], P),
                                                ident[:].rearrange("p (o t) -> p o t", o=1).to_broadcast([P, TT, P]), ALU.mult).then_inc(hd_copied, 1)
                    for m in range(LEVELS):
                        lev, half = LEVELS * n + m, 2 ** m
                        up = slice(half, 2 * half)
                        v.wait_ge(hx_exp, 2 * lev + 2)
                        if lev >= 2:
                            v.wait_ge(ha_ready, lev - 1)
                        src = hq[:, h, :] if d == 0 else hz[1][:, h, 0:T]
                        nc.vector.tensor_tensor(halves(xl[lev % 2][:], 2 * half)[:, :, up], halves(src, 2 * half)[:, :, up],
                                                halves(yl[lev % 2][:], 2 * half)[:, :, up], ALU.mult).then_inc(hx_up, 1)
                        if m + 2 < LEVELS:
                            level_y(m + 2)
                        if m:
                            level_a(m - 1)
                        if m == 2 and n + 1 < HG_N:
                            chunk_end(n + 1)
                        if m == 3:
                            v.wait_ge(hkv_ready, n + 1)
                            for u in range(5):
                                kv = pm[0][:, 1, P * u:P * u + P] if u < 4 else pa[3][:, P:2 * P]
                                if u == 0:
                                    nc.vector.tensor_copy(st[d][:, 0, :], kv).then_inc(hs_done, 1)
                                else:
                                    v.wait_ge(hs_done, 5 * n + u)
                                    c = HG_ORDER[d][u]
                                    nc.vector.scalar_tensor_tensor(st[d][:, u, :], st[d][:, u - 1, :], epend[:, d, h, c:c + 1], kv, ALU.mult, ALU.add).then_inc(hs_done, 1)
                        if m == 5 and n + 1 < HG_N:
                            keys(n + 1)
                    level_a(LEVELS - 1)
                output(HG_HEADS - 1)
                head_norm(1, hq, hg, "hg_norm", yh_h, yh_l)
                v.wait_ge(mod_used, MOD_SLABS)
                for j in range(2):
                    nc.vector.tensor_tensor(modc[:, MOD_TILES1:, j], mod_out(MOD_TILES1, MOD_TILES)[:, :, j],
                                            cols("b_mod", MOD_TILES1, MOD_TILES - MOD_TILES1), ALU.add).then_inc(pm_free[1], 1)
                v.wait_ge(pm_free[1], HG_USE + 2)
                nc.vector.scalar_tensor_tensor(wsc[:, 2, :], modc[:, KD * 4:KD * 5, 0], 1.0, cols("norm2", 0, KD), ALU.add, ALU.mult).then_inc(pm_free[1], 1)
                v.wait_ge(pm_free[1], HG_USE + 3)
                v.sem_inc(pm_free[1], 1)

            def first():
                lower_bounds()
                v.wait_ge(mod_used, MOD_FIRST)
                for j in range(2):
                    if j:
                        v.wait_ge(mod_done, 1)
                    nc.vector.tensor_tensor(modc[:, 0:MOD_TILES1, j], mod_out(0, MOD_TILES1)[:, :, j],
                                            cols("b_mod", 0, MOD_TILES1), ALU.add).then_inc(pm_free[1] if j else mod_done, 1)
                v.wait_ge(pm_free[1], 1)
                v.wait_ge(mod_done, 1)
                for i, j in enumerate((1, 0)):
                    nc.vector.scalar_tensor_tensor(wsc[:, i, :], modc[:, KD:2 * KD, j], 1.0, cols("norm1", 0, KD), ALU.add, ALU.mult).then_inc(mod_done, 1)
                v.sem_inc(mod_done, 2)
                v.wait_ge(mod_done, 5)
                dve_norm(v, 0, 0, lambda k: wsc[:, 0, k:k + 1], None, cx, CT, ch, cl, lambda k: mod_col(0, k, 1))
                dve_norm(v, 1, 1, lambda k: wsc[:, 1, k:k + 1], shift=lambda k: mod_col(0, k))
                mlstm()
                hgrn()
                for i in range(OUT1_SLABS):
                    p = i % 2
                    v.wait_ge(slab_used, OUT1_AT + i + 1)
                    for t in range(2):
                        k = 2 * i + t
                        if t:
                            v.wait_ge(x_mixed, i + 1)
                        nc.vector.scalar_tensor_tensor(x[:, k, :], pm[p][:, t, :], mod_col(2, k), x[:, k, :], ALU.mult, ALU.add).then_inc(
                            pm_free[p] if t else x_mixed, 1)
                dve_norm(v, 2, 2, lambda k: wsc[:, 2, k:k + 1], shift=lambda k: mod_col(3, k))
                with v.Fori(0, UP_STEPS) as j:
                    v.wait_ge(hidden_done, 1 + 2 * j)
                    for b in range(2):
                        for i in range(2):
                            c0 = CONV1 + 18 * b + 9 * i + 36 * j
                            if i == 0:
                                v.wait_ge(pad_filled, 4 + b + 1 + 2 * j)
                            else:
                                v.wait_ge(pm_free[b], UP1_USE + 1 + j)
                            conv_tile(c0, image(sil[b][:, i, :]),
                                      lambda tap: col[:, bass.ds(COL_AT["ffn_conv"] + 2 * KF * tap + KF * b + i + 2 * j, 1)], windows(pad[i]))
                    v.wait_ge(usilu_done, 1 + j)
                    v.wait_ge(conv_step, CONV1 + 36 + 36 * j)
                    nc.vector.tensor_tensor(ut[:], sil[0][:], sil[1][:], ALU.mult).then_inc(x_mixed, 1)
                    v.wait_ge(x_mixed, OUT1_SLABS + 1 + j)
                    v.sem_inc(vtick, 1)
                    nc.vector.tensor_copy(uh[:, bass.ds(2 * j, 2), :], ut[:]).then_inc(hidden_done, 1)
                    v.wait_ge(hidden_done, 2 + 2 * j)
                    nc.vector.tensor_tensor(ul[:, bass.ds(2 * j, 2), :], ut[:], uh[:, bass.ds(2 * j, 2), :].bitcast(F32), ALU.subtract).then_inc(hidden_done, 1)
                with v.Fori(0, KD // 2) as n:
                    for b in range(2):
                        v.wait_ge(slab_used, DOWN1_AT + 2 * b + 2 + 4 * n)
                        xs = x[:, bass.ds(2 * n + b, 1), :]
                        g2 = modc[:, bass.ds(KD * 5 + b + 2 * n, 1), 0]
                        nc.vector.scalar_tensor_tensor(xs, pm[b][:, 0:1, :], g2, xs, ALU.mult, ALU.add).then_inc(pm_free[b], 1)
                dve_norm(v, 3, 3, gains(COL_AT["final_norm"]), out=x)

            first()

            def ffn(l, f):
                s0, u0 = ffn_slab(l, f), ffn_use(l, f)
                n = NORMS1 + 3 * l + 2 * f
                dve_norm(v, n, n - 1, gains(GAINS[f"ffn{f + 1}"] + 8 * l))
                d0 = 1 + 2 * UP_STEPS * (1 + 2 * l + f)
                with v.Fori(0, UP_STEPS) as j:
                    v.wait_ge(hidden_done, d0 + 2 * j)
                    v.wait_ge(pm_free[0], u0 + 1 + j)
                    v.wait_ge(slab_used, s0 + 2 + 2 * j)
                    nc.vector.tensor_tensor(ut[:], sil[0][:], pm[1][:], ALU.mult).then_inc(pm_free[1], 1)
                    v.wait_ge(pm_free[1], u0 + 1 + j)
                    v.sem_inc(vtick, 1)
                    nc.vector.tensor_copy(uh[:, bass.ds(2 * j, 2), :], ut[:]).then_inc(hidden_done, 1)
                    v.wait_ge(hidden_done, d0 + 1 + 2 * j)
                    nc.vector.tensor_tensor(ul[:, bass.ds(2 * j, 2), :], ut[:], uh[:, bass.ds(2 * j, 2), :].bitcast(F32), ALU.subtract).then_inc(hidden_done, 1)
                s1, u1 = s0 + 2 * UP_STEPS, u0 + UP_STEPS
                with v.Fori(0, KD // 2) as n:
                    for b in range(2):
                        v.wait_ge(slab_used, s1 + 2 * b + 2 + 4 * n)
                        xs = x[:, bass.ds(2 * n + b, 1), :]
                        nc.vector.scalar_tensor_tensor(xs, pm[b][:, 0:1, :], 0.5, xs, ALU.mult, ALU.add).then_inc(pm_free[b], 1)

            def mix(l):
                s0, u0 = mix_slab(l), mix_use(l)
                for p in range(2):
                    v.wait_ge(pm_free[p], u0)
                nc.vector.memset(wpool[:], 0.0).then_inc(mixc_made, 1)
                nc.vector.memset(zero[:], 0.0).then_inc(mixc_made, 1)
                nc.vector.memset(lowest[:], -1e30).then_inc(mixc_made, 1)
                nc.vector.memset(u[:, :, 0:PAD], 0.0).then_inc(mixc_made, 1)
                n = NORMS1 + 3 * l + 1
                dve_norm(v, n, n - 1, gains(GAINS["mix"] + 8 * l))
                v.wait_ge(mixc_loaded, 16 * 11 * (l + 1))
                v.wait_ge(mixc_made, 4 * l + 4)
                for h in range(SB_HEADS):
                    m = TT * (SB_HEADS * l + h)
                    hp = slice(64 * (h % 2), 64 * (h % 2) + 64)
                    for j in range(TT):
                        c = slice(LIVE_AT[j], LIVE_AT[j] + LIVE[j])
                        v.wait_ge(ln_done, m + j + 1)
                        if m + j >= TT:
                            v.wait_ge(logw_ready, m)
                        nc.vector.scalar_tensor_tensor(sp_[:, c], pa[j][:, 0:LIVE[j]], 0.0, sc[:, c], ALU.max, ALU.add).then_inc(sp_done, 1)
                        v.wait_ge(sp_done, m + j + 1)
                        nc.vector.copy_predicated(sp_[:, LIVE_AT[j]:LIVE_AT[j] + P], dmask[:].bitcast(mybir.dt.uint32), zero[:]).then_inc(sp_masked, 1)
                    for n_, j in enumerate(reversed(range(TT))):
                        v.wait_ge(logw_ready, m + n_ + 1)
                        nc.vector.copy_predicated(pa[j][:, 0:P], dmask[:].bitcast(mybir.dt.uint32), lowest[:]).then_inc(w_masked, 1)
                    v.wait_ge(sb_out, SB_HEADS * l + h + 1)
                    nc.vector.tensor_copy(ysb_h[hp, h // 2, :], pm[0][hp, 0, :]).then_inc(sb_hi, 1)
                    v.wait_ge(sb_hi, SB_HEADS * l + h + 1)
                    nc.vector.tensor_tensor(ysb_l[hp, h // 2, :], pm[0][hp, 0, :], ysb_h[hp, h // 2, :].bitcast(F32), ALU.subtract).then_inc(pm_free[0], 1)
                v.wait_ge(pm_free[1], u0 + 3)
                for i, dst in enumerate((q_r, k_r)):
                    for g in range(2):
                        m = 4 * l + 2 * i + g
                        if m:
                            v.wait_ge(rot_done, m)
                        nc.vector.tensor_tensor(rt1[:], rraw[i][:, g, :], rope[:, 0, :], ALU.mult).then_inc(rot_made, 1)
                        v.wait_ge(swapped, m + 1)
                        nc.vector.tensor_tensor(rt2[:], pa[2 * i + g][:], rope[:, 1, :], ALU.mult).then_inc(rot_made, 1)
                        v.wait_ge(rot_made, 2 * m + 2)
                        nc.vector.tensor_tensor(dst[:, g, :], rt1[:], rt2[:], ALU.add).then_inc(rot_done, 1)
                lo, hi = slice(0, 64), slice(64, 128)
                w0 = 5 * l
                v.wait_ge(pm_free[1], u0 + FILL_USE + 5)
                v.wait_ge(rot_done, 4 * l + 4)
                W = PAD + T
                nc.vector.tensor_copy(pw[0][:, :, 0:1], u[:, :, 0:1]).then_inc(win_done, 1)
                nc.vector.tensor_tensor(pw[0][:, :, 1:W], u[:, :, 1:W], u[:, :, 0:W - 1], ALU.add).then_inc(win_done, 1)
                v.wait_ge(win_done, w0 * 2 + 2)
                nc.vector.tensor_copy(pw[1][:, :, 0:2], pw[0][:, :, 0:2]).then_inc(win_done, 1)
                nc.vector.tensor_tensor(pw[1][:, :, 2:W], pw[0][:, :, 2:W], pw[0][:, :, 0:W - 2], ALU.add).then_inc(win_done, 1)
                v.wait_ge(win_done, w0 * 2 + 4)
                nc.vector.tensor_copy(pw[0][hi, 0, :], pw[1][hi, 0, :]).then_inc(win_done, 1)
                nc.vector.tensor_copy(pw[0][:, 1, 0:4], pw[1][:, 1, 0:4]).then_inc(win_done, 1)
                nc.vector.tensor_tensor(pw[0][:, 1, 4:W], pw[1][:, 1, 4:W], pw[1][:, 1, 0:W - 4], ALU.add).then_inc(win_done, 1)
                v.wait_ge(win_done, w0 * 2 + 7)
                nc.vector.tensor_copy(pw[1][hi, 1, 0:8], pw[0][hi, 1, 0:8]).then_inc(win_done, 1)
                nc.vector.tensor_tensor(pw[1][hi, 1, 8:W], pw[0][hi, 1, 8:W], pw[0][hi, 1, 0:W - 8], ALU.add).then_inc(win_done, 1)
                v.wait_ge(win_done, w0 * 2 + 9)
                nc.vector.tensor_copy(pw[0][hi, 1, :], pw[1][hi, 1, :]).then_inc(win_done, 1)
                v.wait_ge(win_done, w0 * 2 + 10)
                d0 = 6 * l
                for g in range(2):
                    for s, w in ((lo, POOL_WINDOWS[2 * g]), (hi, POOL_WINDOWS[2 * g + 1])):
                        nc.vector.scalar_tensor_tensor(pd[s, g, PAD:], pw[0][s, g, 2 * PAD:], 1.0 / w, u[s, g, 2 * PAD:], ALU.mult, ALU.subtract).then_inc(pd_done, 1)
                nc.vector.tensor_tensor(pd[:, :, 0:PAD], pw[0][:, :, PAD:2 * PAD], invcnt[:], ALU.mult).then_inc(pd_done, 1)
                v.wait_ge(pd_done, d0 + 5)
                nc.vector.tensor_tensor(pd[:, :, 0:PAD], pd[:, :, 0:PAD], u[:, :, PAD:2 * PAD], ALU.subtract).then_inc(pd_done, 1)
                v.wait_ge(pool_scaled, 2 * l + 2)
                nc.vector.tensor_copy(yp_h[:], pt[:]).then_inc(pool_hi, 1)
                v.wait_ge(pool_hi, l + 1)
                nc.vector.tensor_tensor(yp_l[:], pt[:], yp_h[:].bitcast(F32), ALU.subtract).then_inc(pool_done, 1)
                for h in range(RET_HEADS):
                    m = RET_HEADS * l + h
                    p = h % 2
                    for j in range(TT):
                        v.wait_ge(s_ready, TT * m + j + 1)
                        if m >= 2:
                            v.wait_ge(ret_out, m - 1)
                        nc.vector.tensor_tensor(aret[p][:, LIVE_AT[j]:LIVE_AT[j] + LIVE[j]], pa[j][:, 0:LIVE[j]], decay[:, h, 0:LIVE[j]], ALU.mult).then_inc(a_done, 1)
                    v.wait_ge(ret_std, m + 1)
                    nc.vector.reciprocal(ret_inv[:], ret_root[:]).then_inc(ret_rstd, 1)
                    v.wait_ge(ret_rstd, m + 1)
                    nc.vector.tensor_tensor(yraw[:, h, :], pm[p][:, 0, :], ret_inv[:], ALU.mult).then_inc(pm_free[p], 1)
                for i in range(2):
                    v.wait_ge(pm_free[0], u0 + RET_USE[0] + 2)
                    v.wait_ge(pm_free[1], u0 + RET_USE[1] + 2)
                    if i == 1 or l:
                        v.wait_ge(gr_done, 2 * l + i)
                    nc.vector.tensor_tensor(ut[:], sil[i][:], yraw[:, 2 * i:2 * i + 2, :], ALU.mult).then_inc(gr_prod, 1)
                    v.wait_ge(gr_prod, 2 * l + i + 1)
                    nc.vector.tensor_copy(yr_h[:, 2 * i:2 * i + 2, :], ut[:]).then_inc(gr_hi, 1)
                    v.wait_ge(gr_hi, 2 * l + i + 1)
                    nc.vector.tensor_tensor(yr_l[:, 2 * i:2 * i + 2, :], ut[:], yr_h[:, 2 * i:2 * i + 2, :].bitcast(F32), ALU.subtract).then_inc(gr_done, 1)
                r = [u0 + n for n in BRANCH_USE]
                b0, m0 = 2 * 4 * l, 1 + 3 * 4 * l
                with v.Fori(0, 4) as j:
                    v.wait_ge(mg_done, 1 + 4 * l + j)
                    v.wait_ge(pm_free[0], r[0] + 2 + 3 * j)
                    v.wait_ge(branch_out, b0 + 1 + 2 * j)
                    nc.vector.tensor_tensor(mg[:], gates[:, 0], pm[1][:], ALU.mult).then_inc(pm_free[1], 1)
                    v.wait_ge(branch_out, b0 + 2 + 2 * j)
                    nc.vector.tensor_tensor(mt[:], gates[:, 1], pm[0][:], ALU.mult).then_inc(pm_free[0], 1)
                    v.wait_ge(pm_free[1], r[1] + 2 + 3 * j)
                    v.wait_ge(pm_free[0], r[0] + 3 + 3 * j)
                    nc.vector.tensor_tensor(mg[:], mg[:], mt[:], ALU.add).then_inc(mix_sum, 1)
                    v.wait_ge(mix_sum, m0 + 1 + 3 * j)
                    v.wait_ge(slab_used, s0 + 14 + 4 * j)
                    nc.vector.tensor_tensor(mt[:], gates[:, 2], pm[1][:], ALU.mult).then_inc(pm_free[1], 1)
                    v.wait_ge(pm_free[1], r[1] + 3 + 3 * j)
                    nc.vector.tensor_tensor(mg[:], mg[:], mt[:], ALU.add).then_inc(mix_sum, 1)
                    v.wait_ge(mix_sum, m0 + 2 + 3 * j)
                    v.sem_inc(vtick, 1)
                    nc.vector.tensor_copy(mg_h[:, bass.ds(2 * j, 2), :], mg[:]).then_inc(mix_sum, 1)
                    v.wait_ge(mix_sum, m0 + 3 + 3 * j)
                    nc.vector.tensor_tensor(mg_l[:, bass.ds(2 * j, 2), :], mg[:], mg_h[:, bass.ds(2 * j, 2), :].bitcast(F32), ALU.subtract).then_inc(mg_done, 1)
                with v.Fori(0, 2) as j:
                    for b in range(2):
                        v.wait_ge(slab_used, s0 + 27 + b + 2 * j)
                        xs = x[:, bass.ds(4 * j + 2 * b, 2), :]
                        nc.vector.tensor_tensor(xs, xs, pm[b][:], ALU.add).then_inc(pm_free[b], 1)
                v.wait_ge(pm_free[0], u0 + MIX_USES - 2)
                v.sem_inc(pm_free[0], 2)

            for l in range(LAYERS):
                ffn(l, 0)
                mix(l)
                ffn(l, 1)
            n = NORMS1 + 3 * LAYERS
            dve_norm(v, n, n - 1, gains(GAINS["final"]), out=uh_f)
            for k in range(KD):
                v.wait_ge(out_tr, k + 1)
                nc.vector.tensor_copy(x[:, k, :], pa[k % 4][:]).then_inc(out_copied, 1)

        def mm3(out, wh, wl, ah, al, start, stop):
            nc.tensor.matmul(out, wh, ah, start=start, stop=False)
            nc.tensor.matmul(out, wh, al, start=False, stop=False)
            return nc.tensor.matmul(out, wl, ah, start=False, stop=stop)

        @block.tensor
        def _(pe):
            pe.wait_ge(const_loaded, 16 * 4)
            pe.wait_ge(const_made, 2)

            def norm(n, W=T):
                if n:
                    pe.wait_ge(std_done, n)
                for k in range(KD):
                    pe.wait_ge(sq_done, 8 * n + k + 1)
                    nc.tensor.matmul(pa[0][:, 0:W], ones[:], sq[k % 2][:, 0:W], start=k == 0, stop=k == KD - 1).then_inc(sq_summed, 1)

            def slab_first(b, use, nh):
                for k in range(KD):
                    pe.wait_ge(hl_done, 8 * nh + k + 1)
                    for i in range(2):
                        c = slice(P * i, P * i + P)
                        last = mm3(pm[use][:, i, :], whi[b][:, k, c], wlo[b][:, k, c], hh[:, k, :], hl[:, k, :], k == 0, k == KD - 1)
                return last

            def slab_t(b, ah, al, use, n):
                for i in range(2):
                    c = slice(P * i, P * i + P)
                    for k in range(KD):
                        last = mm3(pm[use][:, i, :], whi[b][:, k, c], wlo[b][:, k, c], ah[:, k, :], al[:, k, :], k == 0, k == KD - 1)
                return last

            def slab_tok(b, use):
                for t in range(TT):
                    c = slice(P * t, P * t + P)
                    o = pm[use][:, t // 2, SLAB * (t % 2):SLAB * (t % 2) + SLAB]
                    for k in range(KD):
                        nc.tensor.matmul(o, hh[:, k, c], whi[b][:, k, :], start=k == 0, stop=False)
                        nc.tensor.matmul(o, hl[:, k, c], whi[b][:, k, :], start=False, stop=False)
                        last = nc.tensor.matmul(o, hh[:, k, c], wlo[b][:, k, :], start=False, stop=k == KD - 1)
                return last

            def ffn_products(s0, u0, nh, hidden, after):
                pe.wait_ge(split_done, s0 + 1)
                pe.wait_ge(pm_free[0], u0)
                slab_first(0, 0, nh).then_inc(slab_used, 1)
                pe.wait_ge(split_done, s0 + 2)
                pe.wait_ge(pm_free[1], u0)
                slab_t(1, hh, hl, 1, KD).then_inc(slab_used, 1)
                with pe.Fori(1, UP_STEPS) as j:
                    for b in range(2):
                        pe.wait_ge(split_done, s0 + b + 1 + 2 * j)
                        pe.wait_ge(pm_free[b], u0 + j)
                        slab_t(b, hh, hl, b, KD).then_inc(slab_used, 1)
                pe.wait_ge(std_done, after)
                s1, u1 = s0 + 2 * UP_STEPS, u0 + UP_STEPS

                def down(j, first):
                    for i in range(2):
                        for b in range(2):
                            pe.wait_ge(split_done, s1 + 2 * i + b + 1 + 4 * j)
                            if b == 0:
                                pe.wait_ge(pm_free[i], u1 + j)
                            h, o = (a[b][:].rearrange("p k n -> p (k n)") for a in (whi, wlo))
                            for k in range(DOWN_K):
                                if first and i == 0 and (k == 0 or b == 1 and k == DOWN_K - 2):
                                    pe.wait_ge(hidden_done, 1 + hidden - 2 * UP_STEPS + (DOWN_K + 1 if b == 0 else 2 * UP_STEPS - 2 * (k == 0)))
                                c = slice(P * k, P * k + P)
                                last = mm3(pm[i][:, 0, :], h[:, c], o[:, c], uh[:, DOWN_K * b + k, :], ul[:, DOWN_K * b + k, :],
                                           b == 0 and k == 0, b == 1 and k == DOWN_K - 1)
                            last.then_inc(slab_used, 1)
                            if b == 0 and not (first and i == 0):
                                pe.wait_ge(sq_done, 8 * after + i + 2 * j)
                                nc.tensor.matmul(pa[0][:], ones[:], sq[1 - i][:], start=first, stop=False).then_inc(sq_summed, 1)

                down(0, True)
                with pe.Fori(1, KD // 2) as j:
                    down(j, False)
                pe.wait_ge(sq_done, 8 * after + KD)
                nc.tensor.matmul(pa[0][:], ones[:], sq[1][:], start=False, stop=True).then_inc(sq_summed, 1)

            def ffn(l, f):
                n = NORMS1 + 3 * l + 2 * f
                if f or not l:
                    norm(n)
                ffn_products(ffn_slab(l, f), ffn_use(l, f), n - 1, 2 * UP_STEPS * (2 + 2 * l + f), n + 1)

            def context_t(b, p):
                for i in range(2):
                    c = slice(P * i, P * i + P)
                    for k in range(KD):
                        last = mm3(pa[p][:, CT * i:CT * i + CT], whi[b][:, k, c], wlo[b][:, k, c], ch[:, k, :], cl[:, k, :], k == 0, k == KD - 1)
                return last

            def context_tok(b, p):
                for t in range(CTT):
                    c = slice(P * t, P * t + P)
                    o = pa[p][:, SLAB * t:SLAB * t + SLAB]
                    for k in range(KD):
                        nc.tensor.matmul(o, ch[:, k, c], whi[b][:, k, :], start=k == 0, stop=False)
                        nc.tensor.matmul(o, cl[:, k, c], whi[b][:, k, :], start=False, stop=False)
                        last = nc.tensor.matmul(o, ch[:, k, c], wlo[b][:, k, :], start=False, stop=k == KD - 1)
                return last

            def in1(i):
                name, b, p = IN1[i][0], i % 2, IN1_P[i]
                pe.wait_ge(split_done, 2 + i + 1)
                if IN1_USE[i]:
                    pe.wait_ge(pm_free[p], IN1_USE[i])
                if IN1_CTX[i]:
                    pe.wait_ge(ctx_free[p], IN1_CTX[i])
                if name == "gate":
                    h, o = (a[b][:].rearrange("p k n -> p (k n)") for a in (whi, wlo))
                    for out, yh, yl_ in ((pm[p][:, 0, :], hh, hl), (pa[p][:, 0:CT], ch, cl)):
                        for k in range(KD // 2):
                            kk, c = KD // 2 * (i - 6) + k, slice(P * k, P * k + P)
                            last = mm3(out, h[:, c], o[:, c], yh[:, kk, :], yl_[:, kk, :], kk == 0, kk == KD - 1)
                elif name in ("mv", "hv"):
                    slab_tok(b, p)
                    last = context_tok(b, p)
                else:
                    last = slab_first(b, p, 1) if i == 0 else slab_t(b, hh, hl, p, KD)
                    if name in ("mk", "zf", "zb"):
                        last = context_t(b, p)
                last.then_inc(slab_used, 1)

            def modulation(first_, end):
                for i in range(first_, end):
                    b = i % 2
                    pe.wait_ge(mod_loaded[b], 16 * (i // 2 + 1))
                    for t in range(2):
                        o = 2 * (2 * i + t)
                        for k in range(KD):
                            last = nc.tensor.matmul(pm[1][:, 0, o:o + 2], raw[b][:, k, P * t:P * t + P], silc[:, k, :], start=k == 0, stop=k == KD - 1)
                            if t == 1 and k == KD - 1:
                                last.then_inc(mod_used, 1)
                            yield

            def head_norm(e):
                pe.wait_ge(t_sq, e + 1)
                for h in range(4):
                    nc.tensor.matmul(pa[h][:], ones[:], sq4[:, h, :], start=True, stop=True).then_inc(t_ss, 1)

            def mlstm():
                pe.wait_ge(pm_free[0], IN1_USE[6] + 1)
                pe.wait_ge(ctx_free[0], IN1_CTX[6] + 1)
                for g in range(4):
                    if g:
                        pe.wait_ge(gsel_copied, 2 * g - 1)
                    nc.tensor.matmul(pa[2][0:4, :], ident[0:16, 4 * g:4 * g + 4], gall[:, 0:T], start=True, stop=True).then_inc(gsel_ready, 1)
                    if g:
                        pe.wait_ge(gsel_copied, 2 * g)
                    nc.tensor.matmul(pa[3][0:4, 0:CT], ident[0:16, 4 * g:4 * g + 4], gall[:, T:TA], start=True, stop=True).then_inc(gsel_ready, 1)
                in1(8)
                in1(9)
                pe.wait_ge(gsel_copied, 8)
                for d in range(2):
                    pe.wait_ge(gstep, 6 * d + 3)
                    for t in range(TAT):
                        at = LATC[d].start + P * t if t < TT else CTXC[d].start + P * (t - TT)
                        o = (d * TAT + t) * ML_HEADS
                        last = nc.tensor.transpose(pa[2][:, o:o + ML_HEADS], GI[d][:, at:at + P], ident[0:4, 0:4])
                last.then_inc(gtr, 1)
                pe.wait_ge(gcol_done, 1)
                pe.wait_ge(gdn, 2)
                pe.wait_ge(conv_silu, 8)
                pe.wait_ge(ctx_free[0], IN1_CTX[6] + 1)
                pe.wait_ge(ctx_free[1], IN1_CTX[5] + 1)
                pe.wait_ge(pm_free[1], IN1_USE[5] + 1)

                def scores(s):
                    h, i = s // TAT, s % TAT
                    if s >= 2:
                        pe.wait_ge(a_made, 2 * s - 2)
                    at = T + P * i if i < 2 else P * (i - 2)
                    nc.tensor.matmul(pa[s % 2][:], mk[:, h, at:at + P], mq[:, h, :], start=True, stop=True).then_inc(ms_ready, 1)

                scores(0)
                for h in range(ML_HEADS):
                    for d in range(2):
                        n = 2 * h + d
                        if h:
                            pe.wait_ge(mb_copied, 2 * n - 2)
                        nc.tensor.matmul(pa[2 + d][:], bsel[:, h, :], GT[d][:, LATC[d]], start=True, stop=True).then_inc(mb_ready, 1)
                        pe.wait_ge(mb_copied, 2 * n + 1)
                        nc.tensor.matmul(pa[2 + d][:], bsel[:, h, :], GF[d][:, LATC[d]], start=True, stop=True).then_inc(mb_ready, 1)
                    for i in range(TAT):
                        s = TAT * h + i
                        if s + 1 < TAT * ML_HEADS:
                            scores(s + 1)
                        for d in range(2):
                            r = 2 * s + d
                            if i == 0:
                                pe.wait_ge(pm_free[d], ML_USE + h)
                            if i < 2:
                                pe.wait_ge(a_made, r + 1)
                                c, st_ = slice(0, T), TT + i
                            else:
                                pe.wait_ge(a_masked, 8 * h + 2 * (i - 2) + d + 1)
                                c, st_ = live(d, i - 2), i - 2
                            a = aw[d][s % 2][:, c]
                            nc.tensor.matmul(pm[d][:, 0, c], mv[:, st_, P * h:P * h + P], a, start=i == 0, stop=i == TAT - 1)
                            nc.tensor.matmul(pm[d][:, 1, c], ones[:], a, start=i == 0, stop=i == TAT - 1).then_inc(nd_acc, 1)
                head_norm(0)

            def hgrn():
                for p in range(2):
                    pe.wait_ge(pm_free[p], HG_USE)
                    pe.wait_ge(ctx_free[p], ctx_uses_[p])
                rest = modulation(MOD_FIRST, MOD_SLABS)
                for _ in range(2 * KD * MOD_BEFORE):
                    next(rest)
                pe.wait_ge(hg_step, 2 + 16)
                for n in range(HG_N):
                    h, d = n // 2, n % 2
                    pe.wait_ge(hkq, 2 * n + 1)
                    if n:
                        pe.wait_ge(ht_copied, 2 * n)
                        pe.wait_ge(hs_done, 5 * n)
                    for u, c in enumerate(HG_ORDER[d]):
                        o = pa[2][:, P * u:P * u + P] if u < 4 else pa[3][:, 0:P]
                        last = nc.tensor.transpose(o, kt[:, P * c:P * c + P], ident[:])
                        if u >= 3:
                            last.then_inc(ht_ready, 1)
                    if d == 0:
                        if h:
                            pe.wait_ge(pm_free[0], HG_USE + h)
                        for c in range(TT):
                            cs = slice(P * c, P * c + P)
                            for e in range(2):
                                last = nc.tensor.matmul(pm[0][:, 0, cs], hz[e][:, h, cs], hq[:, h, cs], start=e == 0, stop=e == 1)
                        last.then_inc(hd_ready, 1)
                    for m in range(LEVELS):
                        lev = LEVELS * n + m
                        pe.wait_ge(hx_up, lev + 1)
                        pe.wait_ge(hx_lo, lev + 1)
                        if lev >= 2:
                            pe.wait_ge(ha_copied, lev - 1)
                        for c in range(TT):
                            cs = slice(P * c, P * c + P)
                            last = nc.tensor.matmul(pa[lev % 2][:, cs], xl[lev % 2][:, cs], xl[lev % 2][:, cs], start=True, stop=True)
                        last.then_inc(ha_ready, 1)
                        if m == 0:
                            pe.wait_ge(ht_copied, 2 * n + 2)
                            for u, c in enumerate(HG_ORDER[d]):
                                o = pm[0][:, 1, P * u:P * u + P] if u < 4 else pa[3][:, P:2 * P]
                                last = nc.tensor.matmul(o, ktok[:, u, :], hv[:, c, P * h:P * h + P], start=True, stop=True)
                            last.then_inc(hkv_ready, 1)
                        for _ in range(MOD_REST[m]):
                            next(rest)
                    if d:
                        pe.wait_ge(hs_done, 5 * n + 5)
                        pe.wait_ge(ha_copied, LEVELS * (n + 1))
                        pe.wait_ge(hkq, 2 * n + 2)
                        for c in range(TT):
                            cs = slice(P * c, P * c + P)
                            o = pm[0][:, 0, cs]
                            nc.tensor.matmul(o, hv[:, c, P * h:P * h + P], ah[:, cs], start=True, stop=False)
                            nc.tensor.matmul(o, st[0][:, 1 + c, :], qt[0][:, cs], start=False, stop=False)
                            last = nc.tensor.matmul(o, st[1][:, 1 + TT - 1 - c, :], qt[1][:, cs], start=False, stop=True)
                        last.then_inc(ho_ready, 1)
                for _ in range(KD):
                    next(rest)
                head_norm(1)
                for _ in rest:
                    pass

            def first():
                pe.wait_ge(mod_in, 1)
                for _ in modulation(0, MOD_FIRST):
                    pass
                norm(0, CT)
                norm(1)
                for i in range(8):
                    in1(i)
                mlstm()
                pe.wait_ge(t_std, 4)
                for i in range(10, IN1_SLABS):
                    in1(i)
                hgrn()
                pe.wait_ge(t_done, 2)
                for i in range(OUT1_SLABS):
                    b = i % 2
                    pe.wait_ge(split_done, OUT1_AT + i + 1)
                    pe.wait_ge(pm_free[b], OUT1_USE + i // 2)
                    for t in range(2):
                        c = slice(P * t, P * t + P)
                        for k in range(KD):
                            yh, yl_ = (ym_h, ym_l) if k < 4 else (yh_h, yh_l)
                            last = mm3(pm[b][:, t, :], whi[b][:, k, c], wlo[b][:, k, c], yh[:, k % 4, :], yl_[:, k % 4, :], k == 0, k == KD - 1)
                    last.then_inc(slab_used, 1)
                norm(2)
                ffn_products(UP1_AT, UP1_USE, 2, 2 * UP_STEPS, 3)

            def mix(l):
                s0, u0 = mix_slab(l), mix_use(l)
                n = NORMS1 + 3 * l + 1
                def slab(i, p, use):
                    b = i % 2
                    pe.wait_ge(split_done, s0 + i + 1)
                    pe.wait_ge(pm_free[p], u0 + use)
                    last = slab_first(b, p, n - 1) if i == 0 else slab_tok(b, p) if i in (2, 5, 6) else slab_t(b, hh, hl, p, KD)
                    last.then_inc(slab_used, 1)

                slab(0, 0, 0)
                slab(1, 1, 0)
                slab(2, 0, 1)
                pe.wait_ge(mixc_loaded, 16 * 11 * (l + 1))
                pe.wait_ge(pm_free[0], u0 + 1)
                pe.wait_ge(pm_free[1], u0 + 1)
                for h in range(SB_HEADS):
                    hp = slice(64 * (h % 2), 64 * (h % 2) + 64)
                    m = TT * (SB_HEADS * l + h)

                    def scores(j, start):
                        return nc.tensor.matmul(pa[j][:, 0:LIVE[j]], k_sb[hp, h // 2, P * j:P * j + P], q_sb[hp, h // 2, P * j:],
                                                start=start, stop=True)

                    for j in range(TT):
                        if h:
                            pe.wait_ge(w_done, m - j)
                        scores(j, True).then_inc(z_ready, 1)
                    slab(3 + 2 * h, 1, FILL_USE + 2 * h)
                    for n_, j in enumerate(reversed(range(TT))):
                        if n_ == 0:
                            pe.wait_ge(sp_masked, m + TT)
                        for i in range(j, TT):
                            o = P * (i - j)
                            nc.tensor.matmul(pa[j][:, o:LIVE[j]], trineg[:] if i == j else onesneg[:],
                                             sp_[:, LIVE_AT[i]:LIVE_AT[i] + LIVE[i]], start=i == j, stop=False)
                        scores(j, False).then_inc(logw_ready, 1)
                    if h + 1 < SB_HEADS:
                        slab(4 + 2 * h, 1, FILL_USE + 2 * h + 1)
                    pe.wait_ge(pm_free[0], u0 + SB_USE + h)
                    pe.wait_ge(w_done, m + TT)
                    for j in range(TT):
                        last = nc.tensor.matmul(pm[0][hp, 0, P * j:], v_sb[:, j, 64 * h:64 * h + 64], w_[:, LIVE_AT[j]:LIVE_AT[j] + LIVE[j]],
                                                start=j == 0, stop=j == TT - 1)
                    last.then_inc(sb_out, 1)
                pe.wait_ge(pm_free[1], u0 + FILL_USE + 2)
                for i in range(2):
                    for g in range(2):
                        nc.tensor.matmul(pa[2 * i + g][:], perm[:], rraw[i][:, g, :], start=True, stop=True).then_inc(swapped, 1)
                slab(10, 0, GATE_USE[0])
                slab(11, 1, GATE_USE[1])
                pe.wait_ge(pd_done, 6 * l + 6)
                for g in range(2):
                    nc.tensor.matmul(pa[g][:], wpool[:, g, :], pd[:, g, :], start=True, stop=True).then_inc(pool_out, 1)
                for h in range(RET_HEADS):
                    hp = slice(64 * (h % 2), 64 * (h % 2) + 64)
                    m = RET_HEADS * l + h
                    p = h % 2
                    if h == 0:
                        pe.wait_ge(rot_done, 4 * l + 4)
                        pe.wait_ge(pool_scaled, 2 * l + 2)
                    for j in range(TT):
                        if h:
                            pe.wait_ge(a_done, TT * (m - 1) + j + 1)
                        nc.tensor.matmul(pa[j][:, 0:LIVE[j]], k_r[hp, h // 2, P * j:P * j + P], q_r[hp, h // 2, P * j:],
                                         start=True, stop=True).then_inc(s_ready, 1)
                    pe.wait_ge(pm_free[p], u0 + RET_USE[p] + h // 2)
                    for j in range(TT):
                        pe.wait_ge(a_done, TT * m + j + 1)
                        last = nc.tensor.matmul(pm[p][:, 0, P * j:], v_r[:, j, P * h:P * h + P], aret[p][:, LIVE_AT[j]:LIVE_AT[j] + LIVE[j]],
                                                start=j == 0, stop=j == TT - 1)
                    last.then_inc(ret_out, 1)
                    pe.wait_ge(ret_sq, m + 1)
                    nc.tensor.matmul(pm[p][:, 1, :], ones[:], ret_sqr[:], start=True, stop=True).then_inc(ret_ss, 1)
                slab(12, 0, BRANCH_USE[0] + 1)
                r = [u0 + n for n in BRANCH_USE]
                pe.wait_ge(gr_done, 2 * l + 2)

                def branches(j):
                    pe.wait_ge(split_done, s0 + 14 + 4 * j)
                    for p, n, k0, nk, yh, yl in ((1, 1, 0, 2, ysb_h, ysb_l), (0, 2, 2, 4, yr_h, yr_l), (1, 2, 6, 2, yp_h, yp_l)):
                        pe.wait_ge(pm_free[p], r[p] + n + 3 * j)
                        for i in range(2):
                            c = slice(P * i, P * i + P)
                            for k in range(nk):
                                last = mm3(pm[p][:, i, :], whi[1][:, k0 + k, c], wlo[1][:, k0 + k, c], yh[:, k, :], yl[:, k, :], k == 0, k == nk - 1)
                        last.then_inc(slab_used if k0 == 6 else branch_out, 1)

                branches(0)
                with pe.Fori(1, 4) as j:
                    for g in range(3):
                        pe.wait_ge(split_done, s0 + 11 + g + 4 * j)
                        pe.wait_ge(pm_free[g % 2], r[g % 2] + g // 2 + 3 * j)
                        slab_t(g % 2, hh, hl, g % 2, KD).then_inc(slab_used, 1)
                    branches(j)
                pe.wait_ge(mg_done, 1 + 4 * (l + 1))
                with pe.Fori(0, 2) as j:
                    for b in range(2):
                        pe.wait_ge(split_done, s0 + 27 + b + 2 * j)
                        pe.wait_ge(pm_free[b], r[b] + 12 + j)
                        slab_t(b, mg_h, mg_l, b, KD).then_inc(slab_used, 1)

            first()
            for l in range(LAYERS):
                ffn(l, 0)
                mix(l)
                ffn(l, 1)
            n = NORMS1 + 3 * LAYERS
            for k in range(KD):
                pe.wait_ge(hn_done, 8 * n + k + 1)
                if k >= 4:
                    pe.wait_ge(out_copied, k - 3)
                for t in range(TT):
                    last = nc.tensor.transpose(pa[k % 4][:, P * t:P * t + P], uh_f[:, k, P * t:P * t + P], ident[:])
                last.then_inc(out_tr, 1)


def constants():
    c = {}
    c["c_ident"] = np.eye(P, dtype=np.float32)
    j, i = np.meshgrid(np.arange(P), np.arange(P), indexing="xy")
    c["c_trineg"] = -(i >= j).astype(np.float32)
    c["c_onesneg"] = -np.ones((P, P), np.float32)
    c["c_dmask"] = (i >= j).astype(np.float32)
    f = np.float32
    half = RET_DIM // 2
    inv = f(10000.0) ** (-np.arange(half, dtype=f) / f(half))
    ang = np.arange(T, dtype=f)[:, None] * inv[None, :]
    cos, sin = np.cos(ang).T, np.sin(ang).T
    c["c_rope"] = np.ascontiguousarray(np.stack([np.tile(cos, (4, 1)), np.tile(sin, (4, 1))], 1).astype(f))
    perm = np.zeros((P, P), f)
    for h in range(2):
        for a in range(half):
            perm[64 * h + half + a, 64 * h + a] = -1.0
            perm[64 * h + a, 64 * h + half + a] = 1.0
    c["c_perm"] = perm
    lg = np.log(1.0 - 2.0 ** (-5.0 - np.arange(RET_HEADS, dtype=np.float64)))
    diff = (np.arange(T)[None, :] - np.arange(P)[:, None]).astype(np.float64)
    dec = np.where(diff[:, None, :] >= 0, np.exp(np.maximum(diff, 0)[:, None, :] * lg[None, :, None]), 0.0)
    c["c_decay"] = np.ascontiguousarray(dec.astype(f))
    c["c_bsel"] = np.ascontiguousarray(np.repeat(np.eye(ML_HEADS, dtype=f)[:, :, None], P, 2))
    c["c_mlmask"] = np.ascontiguousarray(np.stack([(i <= j), (i >= j)], 1).astype(f))
    levels = []
    for d in range(2):
        s, t = (i, j) if d == 0 else (j, i)
        for m in range(LEVELS):
            levels.append((s >> (m + 1) == t >> (m + 1)) & (s >> m & 1 == 0) & (t >> m & 1 == 1))
    c["c_hgmask"] = np.ascontiguousarray(np.stack(levels, 1).astype(f))
    win = np.repeat(np.array(POOL_WINDOWS), 64).reshape(2, P)
    cnt = np.minimum(np.arange(PAD)[None, None, :] + 1, win.T[:, :, None])
    c["c_invcnt"] = np.ascontiguousarray((1.0 / cnt).astype(f))
    return c


def packed(g):
    gate = np.zeros((4, P), np.float32)
    gate[:, 0:ML_HEADS] = g["mlstm_gate_b"][0].reshape(4, ML_HEADS)
    rows = [g["g_ffn1_2"], g["g_mix_2"], g["g_ffn2_2"], g["g_final_2"], g["pool_scale_2"], g["norm1_w"], g["norm2_w"], g["final_norm_w"],
            np.stack([g["c"][0].reshape(KD, P), g["c_ctx"].reshape(KD, P)], 1), g["mlstm_norm_w"], g["hgrn_norm_w"], g["hgrn_lb_logits"],
            g["b_mod"], g["mlstm_conv_w"], g["ffn_conv_w"], gate]
    return np.ascontiguousarray(np.concatenate([r.reshape(-1, P) for r in rows]).T)


def kernel(**inputs):
    import concourse.bacc as bacc
    from concourse.bass_utils import run_bass_kernel_spmd as run

    nc = bacc.Bacc("TRN2", target_bir_lowering=False, num_devices=1)
    arrays, io = {}, {}
    given = {k: np.ascontiguousarray(v) for k, v in inputs.items()}
    given["cols"] = packed(given)
    given["xT"] = np.ascontiguousarray(given.pop("x")[0].T)
    given["ctxT"] = np.ascontiguousarray(given.pop("ctx")[0].T)
    given.update(constants())
    for name, a in given.items():
        arrays["in_" + name] = a
        io[name] = nc.dram_tensor("in_" + name, a.shape, mybir.dt.from_np(a.dtype), kind="ExternalInput").ap()
    io["out"] = nc.dram_tensor("out_0", (1, T, D), F32, kind="ExternalOutput").ap()
    build(nc, io)
    r = run(nc, [arrays], core_ids=[0])
    return r.results[0]["out_0"]
```

```python
from contextlib import ExitStack

import concourse.bass as bass
import numpy as np
from concourse import mybir

F32 = mybir.dt.float32
F32R = mybir.dt.float32r
U8 = mybir.dt.uint8
ALU = mybir.AluOpType
ACT = mybir.ActivationFunctionType

P = 128
D = 1024
KD = D // P
T = 512
FF = 2816
KF = FF // P
EPS = 1e-6
LAYERS = 2
SLAB = 256
SB_HEADS, SB_DIM = 4, 64
RET_HEADS, RET_DIM = 4, 64
TT = T // P
UP_STEPS = FF // SLAB
DOWN_K = KF // 2
COL = {"q_sb": 0, "k_sb": 256, "v_sb": 512, "q_r": 768, "k_r": 1024, "v_r": 1280, "g_r": 1792, "u": 2304, "gate": 2560}
POOL_WINDOWS = (2, 4, 8, 16)
PAD = 16
LIVE = [T - P * j for j in range(TT)]
LIVE_AT = [sum(LIVE[:j]) for j in range(TT)]
LIVE_ALL = sum(LIVE)

CT = 256
CTT = CT // P
TA = T + CT
TAT = TA // P
GRID = (T // 64, 64)
ML_HEADS, HG_HEADS = 4, 4
HEAD_DIM = 128
HEAD_SCALE = HEAD_DIM ** -0.5
ML_W = ML_HEADS * HEAD_DIM
HG_AT = 4 * ML_W + 4 * ML_HEADS
N_MOD = 6
MOD_TILES = N_MOD * KD
MOD_SLABS = N_MOD * D // SLAB
MOD_FIRST = 2 * D // SLAB
MOD_TILES1 = 2 * KD
LEVELS = 7
IN1 = ([("mq", 0), ("mq", SLAB), ("mk", ML_W), ("mk", ML_W + SLAB), ("mv", 2 * ML_W), ("mv", 2 * ML_W + SLAB), ("gate", 4 * ML_W),
        ("gate", 4 * ML_W), ("mo", 3 * ML_W), ("mo", 3 * ML_W + SLAB)]
       + [(n, HG_AT + o + e) for n, o in (("hq", 0), ("zf", ML_W), ("zb", 2 * ML_W), ("hv", 3 * ML_W), ("hg", 4 * ML_W)) for e in (0, SLAB)])
IN1_SLABS = len(IN1)
OUT1_SLABS = D // SLAB

COL_AT, n_col = {}, 0
for name_, width_ in (("g_ffn1", 16), ("g_mix", 16), ("g_ffn2", 16), ("g_final", 8), ("pool_scale", 4), ("norm1", 8), ("norm2", 8),
                      ("final_norm", 8), ("c", 16), ("ml_norm", 4), ("hg_norm", 4), ("lb_logits", 16), ("b_mod", MOD_TILES),
                      ("ml_conv", 72), ("ffn_conv", 9 * 2 * KF), ("gate_b", 4)):
    COL_AT[name_] = n_col
    n_col += width_
N_COL = n_col
HG_N = 2 * HG_HEADS
MOD_REST = (0, 0, 4, 3, 3, 3, 3)

IN1_P, IN1_USE, IN1_CTX = [], [], []
uses_, ctx_uses_ = [0, 1], [0, 0]
for i_, (name_, _) in enumerate(IN1):
    p_ = i_ % 2 if i_ < 6 else 0 if i_ < 8 else (i_ + 1) % 2
    IN1_P.append(p_)
    if i_ == 7:
        IN1_USE.append(IN1_USE[-1])
        IN1_CTX.append(IN1_CTX[-1])
        continue
    IN1_USE.append(uses_[p_])
    IN1_CTX.append(ctx_uses_[p_])
    uses_[p_] += 1
    ctx_uses_[p_] += name_ in ("mk", "mv", "gate", "hv", "zf", "zb")
    if i_ == 9:
        ML_USE = uses_[0]
        uses_ = [u_ + ML_HEADS for u_ in uses_]
HG_USE = uses_[0]
OUT1_USE = HG_USE + HG_HEADS
UP1_USE = OUT1_USE + OUT1_SLABS // 2
DOWN1_USE = UP1_USE + UP_STEPS
BASE_USE = DOWN1_USE + KD // 2
OUT1_AT = 2 + IN1_SLABS
UP1_AT = OUT1_AT + OUT1_SLABS
DOWN1_AT = UP1_AT + 2 * UP_STEPS
BASE_SLAB = DOWN1_AT + 2 * KD
NORMS1 = 4
CONV_AT = [9 * t_ for t_ in range(5)] + [36 + 12 * t_ for t_ in range(1, 5)]
CONV1 = CONV_AT[8]
LATC = (slice(CT, TA), slice(0, T))
CTXC = (slice(0, CT), slice(T, TA))
HG_ORDER = ((4, 5, 0, 1, 2), (5, 4, 3, 2, 1))

FFN_SLABS, FFN_USES = 2 * UP_STEPS + 2 * KD, UP_STEPS + KD // 2
MIX_SLABS, MIX_USES = 30, 24
SB_USE, FILL_USE, GATE_USE, RET_USE, BRANCH_USE = 2, 1, (6, 8), (7, 9), (8, 10)


def build(nc, io):
    with ExitStack() as ctx:
        base = [(nc.sbuf_base + 63) // 64 * 64]

        def place(name, shape, dt, at=None):
            size = int(np.prod(shape[1:])) * (1 if dt == U8 else 4)
            if at is None:
                at = base[0]
                base[0] = (at + size + 63) // 64 * 64
            return nc.alloc_sbuf_tensor_at(name, shape, dt, offset=at)

        def sem(name):
            return ctx.enter_context(nc.semaphore(name))

        x = place("x", [P, KD, T], F32)
        hh = place("hh", [P, KD, T], F32R)
        hl = place("hl", [P, KD, T], F32R)
        raw_at = base[0]
        raw = [place(f"raw{b}", [P, 8, SLAB], F32) for b in range(2)]
        whi = [place(f"whi{b}", [P, 8, SLAB], F32R) for b in range(2)]
        wlo = [place(f"wlo{b}", [P, 8, SLAB], F32R) for b in range(2)]
        modraw = raw + [place(f"modraw{b}", [P, 8, SLAB], F32, raw_at + 4 * 8 * SLAB * b) for b in range(2, 6)]
        arena = base[0]
        TILE = 4 * T
        uh = place("uh", [P, KF, T], F32R)
        ul = place("ul", [P, KF, T], F32R)
        scratch = base[0]
        sil = [place(f"sil{b}", [P, 2, T], F32) for b in range(2)]
        ut = place("ut", [P, 2, T], F32)
        sq = [place(f"sq{b}", [P, T], F32, scratch + b * TILE) for b in range(2)]
        std = place("std", [P, T], F32, scratch + 2 * TILE)
        rstd = place("rstd", [P, T], F32, scratch + 3 * TILE)
        hn = [place(f"hn{b}", [P, T], F32, scratch + (4 + b) * TILE) for b in range(2)]
        ident = place("ident", [P, P], F32)
        ones = place("ones", [P, P], F32)
        eps = place("eps", [P, 1], F32)
        col = place("col", [P, N_COL], F32)
        pad_at = (base[0] + 63) // 64 * 64
        pad = [place(f"pad{b}", [P, GRID[0] + 2, GRID[1] + 2], F32) for b in range(2)]
        img = [place("img0", [P, 2, T], F32, scratch + 4 * TILE), place("img1", [P, 2, T], F32, pad_at)]
        silc = place("silc", [P, KD, 2], F32)
        modc = place("modc", [P, MOD_TILES, 2], F32)
        wsc = place("wsc", [P, 3, KD], F32)
        lbm = place("lbm", [P, 2, 4], F32)
        lbe = place("lbe", [P, 2, 2, 4], F32)
        lb = place("lb", [P, 2, 4], F32)
        om = place("om", [P, 2, 4], F32)
        oms = place("oms", [P, 2, 4], F32)
        gcol = place("gcol", [P, 2, TAT, ML_HEADS], F32)

        def tile_at(name, shape, n, dt=F32):
            return place(name, shape, dt, int(arena + n * TILE))

        ch = tile_at("ch", [P, KD, CT], 0, F32R)
        cl = tile_at("cl", [P, KD, CT], 4, F32R)
        cx = tile_at("cx", [P, KD, CT], 8)
        modrow = [tile_at("modrow0", [2, 2 * D], 14), place("modrow1", [2, (N_MOD - 2) * D], F32, raw_at + 4 * 4 * 8 * SLAB)]
        cstd = tile_at("cstd", [P, CT], 12)
        crstd = tile_at("crstd", [P, CT], 12.5)
        mq = tile_at("mq", [P, ML_HEADS, T], 8)
        mk = tile_at("mk", [P, ML_HEADS, TA], 12)
        mv = tile_at("mv", [P, TAT, ML_W], 18)
        mo = tile_at("mo", [P, ML_HEADS, T], 24)
        GI = [tile_at(f"gi{d}", [4, TA], 28 + 1.5 * d) for d in range(2)]
        GF = [tile_at(f"gf{d}", [4, TA], 31 + 1.5 * d) for d in range(2)]
        GT = [tile_at(f"gt{d}", [4, TA], 34 + 1.5 * d) for d in range(2)]
        gall = tile_at("gall", [16, TA], 37)
        wt = [[tile_at(f"wt{d}{b}", [P, T], 38.5 + 2 * d + b) for b in range(2)] for d in range(2)]
        bsel = tile_at("bsel", [4, ML_HEADS, P], 42.5)
        mlmask = tile_at("mlmask", [P, 2, P], 43.5)
        aw = [[place(f"aw{d}{b}", [P, T], F32, scratch + (2 * d + b) * TILE) for b in range(2)] for d in range(2)]
        dnb = [place(f"dnb{d}", [P, T], F32, scratch + (4 + d) * TILE) for d in range(2)]
        asum = [place(f"asum{d}", [P, T], F32, pad_at + d * TILE) for d in range(2)]
        nmb = [tile_at(f"nmb{d}", [P, T], 30 + 7 * d) for d in range(2)]
        dab = [tile_at(f"dab{d}", [P, T], 28 + d) for d in range(2)]
        cacc = [place(f"cacc{t}", [P, TA], F32, scratch + 2 * t * TILE) for t in range(2)]
        cpad = [place(f"cpad{t}", [P, CT + 2], F32, scratch + 4 * TILE + t * (TILE + 64) // 1) for t in range(2)]
        ym_h = tile_at("ym_h", [P, 4, T], 36, F32R)
        ym_l = tile_at("ym_l", [P, 4, T], 40, F32R)
        hq = tile_at("hq", [P, HG_HEADS, T], 8)
        hv = tile_at("hv", [P, TAT, ML_W], 12)
        hz = [tile_at(f"hz{d}", [P, HG_HEADS, TA], 18 + 6 * d) for d in range(2)]
        hg = tile_at("hg", [P, HG_HEADS, T], 0)
        hf = [place("hf0", [P, HG_HEADS, TA], F32, scratch), tile_at("hf1", [P, HG_HEADS, TA], 30)]
        resetm = place("resetm", [P, TA], F32, pad_at)
        ptmp = tile_at("ptmp", [P, TA], 5.5)
        pend = place("pend", [P, 2, HG_HEADS, TAT], F32, pad_at + 2 * TILE)
        epend = place("epend", [P, 2, HG_HEADS, TAT], F32, pad_at + 2 * TILE + 256)
        qt = [tile_at(f"qt{d}", [P, T], 4 + d) for d in range(2)]

        def over_h(name, shape, n):
            return place(name, shape, F32, int(raw_at + (n - 16) * TILE))

        ea = over_h("ea", [P, TA], 0)
        eb = over_h("eb", [P, TA], 1.5)
        yl = [over_h("yl0", [P, T], 3), over_h("yl1", [P, T], 4), place("yl2", [P, T], F32, pad_at)]
        xl = [over_h(f"xl{b}", [P, T], 5 + b) for b in range(2)]
        ah = [over_h("ah0", [P, T], 7), place("ah1", [P, T], F32, pad_at + TILE)]
        kt = over_h("kt", [P, TA], 8)
        ktok = over_h("ktok", [P, 5, P], 9.5)
        st = [over_h("st0", [P, 5, P], 10.75), tile_at("st1", [P, 5, P], 6)]
        hgmask = over_h("hgmask", [P, 2 * LEVELS, P // 2], 12)
        yh_h = place("yh_h", [P, HG_HEADS, TA], F32R, scratch)
        yh_l = tile_at("yh_l", [P, HG_HEADS, TA], 30, F32R)

        decay = tile_at("decay", [P, RET_HEADS, T], 0)
        rope = tile_at("rope", [P, 2, T], 4)
        perm = tile_at("perm", [P, P], 6)
        trineg = tile_at("trineg", [P, P], 6.25)
        onesneg = tile_at("onesneg", [P, P], 6.5)
        wpool = tile_at("wpool", [P, 2, P], 6.75)
        dmask = tile_at("dmask", [P, P], 7.25)
        invcnt = tile_at("invcnt", [P, 2, PAD], 43)
        zero = tile_at("zero", [P, P], 7.5)
        lowest = tile_at("lowest", [P, P], 7.75)
        q_sb = tile_at("q_sb", [P, 2, T], 8)
        k_sb = tile_at("k_sb", [P, 2, T], 10)
        v_sb = tile_at("v_sb", [P, TT, 256], 12)
        q_r = tile_at("q_r", [P, 2, T], 14)
        k_r = tile_at("k_r", [P, 2, T], 16)
        v_r = tile_at("v_r", [P, TT, 512], 18)
        u = tile_at("u", [P, 2, PAD + T], 22)
        rraw = [tile_at(f"rraw{i}", [P, 2, T], 36 + 2 * i) for i in range(2)]
        rt1 = place("rt1", [P, T], F32, scratch + 4 * TILE)
        rt2 = place("rt2", [P, T], F32, scratch + 5 * TILE)
        sc = tile_at("sc", [P, LIVE_ALL], 24.5)
        sp_ = tile_at("sp", [P, LIVE_ALL], 27)
        w_ = tile_at("w", [P, LIVE_ALL], 29.5)
        ysb_h = tile_at("ysb_h", [P, 2, T], 32, F32R)
        ysb_l = tile_at("ysb_l", [P, 2, T], 34, F32R)
        pw = [tile_at("pw0", [P, 2, PAD + T], 36), tile_at("pw1", [P, 2, PAD + T], 38.25)]
        pd = tile_at("pd", [P, 2, T], 40.5)
        pt = place("pt", [P, 2, T], F32, scratch + 4 * TILE)
        yp_h = tile_at("yp_h", [P, 2, T], 12, F32R)
        yp_l = tile_at("yp_l", [P, 2, T], 22, F32R)
        aret = [tile_at(f"aret{i}", [P, LIVE_ALL], 36 + 2.5 * i) for i in range(2)]
        ret_sqr = tile_at("ret_sqr", [P, T], 41)
        ret_root = tile_at("ret_root", [P, T], 42)
        ret_inv = tile_at("ret_inv", [P, T], 31)
        yraw = tile_at("yraw", [P, 4, T], 8)
        yr_h = tile_at("yr_h", [P, 4, T], 14, F32R)
        yr_l = tile_at("yr_l", [P, 4, T], 18, F32R)
        gates = tile_at("gates", [P, 3, 2, T], 24.5)
        mg = tile_at("mg", [P, 2, T], 8)
        mt = tile_at("mt", [P, 2, T], 10)
        mg_h = tile_at("mg_h", [P, KD, T], 0, F32R)
        mg_l = tile_at("mg_l", [P, KD, T], 36, F32R)

        uh_f = tile_at("yfin", [P, KD, T], 0)

        pm = [ctx.enter_context(nc.psum_tensor(f"pm{b}", [P, 2, T], F32)) for b in range(2)]
        pa = [ctx.enter_context(nc.psum_tensor(f"pa{b}", [P, T], F32)) for b in range(4)]

        raw_loaded = [sem("raw_loaded0"), sem("raw_loaded1")]
        hi_done, split_done, slab_used = sem("hi_done"), sem("split_done"), sem("slab_used")
        tick, vtick, stick, atick = sem("pool_tick"), sem("dve_tick"), sem("sync_tick"), sem("act_tick")
        pm_free = [sem("pm_free0"), sem("pm_free1")]
        sq_done, sq_added, sq_summed, std_done, rstd_done = sem("sq_done"), sem("sq_added"), sem("sq_summed"), sem("std_done"), sem("rstd_done")
        hn_done, hh_done, hl_done = sem("hn_done"), sem("hh_done"), sem("hl_done")
        hidden_done = sem("hidden_done")
        const_loaded, const_made = sem("const_loaded"), sem("const_made")
        x_loaded, ctx_loaded = sem("x_loaded"), sem("ctx_loaded")
        mod_row, mod_turned = sem("mod_row"), sem("mod_turned")
        mod_loaded, mod_used, mod_in, mod_done, lb_step, lb_exp = (
            [sem(f"mod_loaded{b}") for b in range(6)], sem("mod_used"), sem("mod_in"), sem("mod_done"), sem("lb_step"), sem("lb_exp"))
        ctx_free = [sem("ctx_free0"), sem("ctx_free1")]
        pad_zeroed, pad_filled, cpad_filled, conv_step, conv_silu = (
            sem("pad_zeroed"), sem("pad_filled"), sem("cpad_filled"), sem("conv_step"), sem("conv_silu"))
        gsel_ready, gsel_copied, gact, gstep, gdn, gtr, gcol_done = (
            sem("gsel_ready"), sem("gsel_copied"), sem("gact"), sem("gstep"), sem("gdn"), sem("gtr"), sem("gcol_done"))
        mb_ready, mb_copied, ms_ready, w_pre, w_exp, a_made, a_masked, a_added, nd_acc, den_ready, den_abs, ml_h = (
            sem("mb_ready"), sem("mb_copied"), sem("ms_ready"), sem("w_pre"), sem("w_exp"), sem("a_made"), sem("a_masked"), sem("a_added"), sem("nd_acc"), sem("den_ready"),
            sem("den_abs"), sem("ml_h"))
        t_sq, t_ss, t_std, t_step, t_hi, t_done = sem("t_sq"), sem("t_ss"), sem("t_std"), sem("t_step"), sem("t_hi"), sem("t_done")
        hgmask_loaded, hg_sig, hg_step, hg_ln, hep_done = (
            sem("hgmask_loaded"), sem("hg_sig"), sem("hg_step"), sem("hg_ln"), sem("hep_done"))
        hdb, heab, hkq, ht_ready, ht_copied, hkv_ready, hs_done = (
            sem("hdb"), sem("heab"), sem("hkq"), sem("ht_ready"), sem("ht_copied"), sem("hkv_ready"), sem("hs_done"))
        hd_ready, hd_copied, hy_done, hx_exp, hx_up, hx_lo, ha_ready, ha_copied, ho_ready = (
            sem("hd_ready"), sem("hd_copied"), sem("hy_done"), sem("hx_exp"), sem("hx_up"), sem("hx_lo"), sem("ha_ready"), sem("ha_copied"),
            sem("ho_ready"))
        x_mixed, usilu_done, img_filled, up_product = sem("x_mixed"), sem("usilu_done"), sem("img_filled"), sem("up_product")
        mixc_loaded, mixc_made = sem("mixc_loaded"), sem("mixc_made")
        qkv_done = sem("qkv_done")
        swapped, rot_made, rot_done = sem("swapped"), sem("rot_made"), sem("rot_done")
        z_ready, abs_done, exp_done, ln_done = sem("z_ready"), sem("abs_done"), sem("exp_done"), sem("ln_done")
        sp_done, sp_masked, logw_ready, w_done, w_masked, sb_out = (
            sem("sp_done"), sem("sp_masked"), sem("logw_ready"), sem("w_done"), sem("w_masked"), sem("sb_out"))
        sb_hi = sem("sb_hi")
        win_done, pd_done, pool_out, pool_scaled, pool_hi, pool_done = (
            sem("win_done"), sem("pd_done"), sem("pool_out"), sem("pool_scaled"), sem("pool_hi"), sem("pool_done"))
        s_ready, a_done, ret_out, ret_sq, ret_ss, ret_std, ret_rstd, ret_copied = (
            sem("s_ready"), sem("a_done"), sem("ret_out"), sem("ret_sq"), sem("ret_ss"), sem("ret_std"), sem("ret_rstd"),
            sem("ret_copied"))
        gr_silu, gr_prod, gr_hi, gr_done = sem("gr_silu"), sem("gr_prod"), sem("gr_hi"), sem("gr_done")
        branch_out, mix_sum, mg_hi, mg_done = sem("branch_out"), sem("mix_sum"), sem("mg_hi"), sem("mg_done")
        out_tr, out_copied, out_stored = sem("out_tr"), sem("out_copied"), sem("out_stored")

        GAINS = {"ffn1": COL_AT["g_ffn1"], "mix": COL_AT["g_mix"], "ffn2": COL_AT["g_ffn2"], "final": COL_AT["g_final"],
                 "pool": COL_AT["pool_scale"]}

        def cols(name, at, n=1):
            return col[:, COL_AT[name] + at:COL_AT[name] + at + n]

        def mod_col(part, k, ctx_=0):
            return modc[:, KD * part + k, ctx_:ctx_ + 1]

        def live(d, j):
            return slice(P * j, T) if d == 0 else slice(0, P * j + P)

        def ffn_gain(l, f):
            return GAINS[f"ffn{f + 1}"] + KD * l

        def gains(at):
            return lambda k: col[:, at + k:at + k + 1]

        def tap_views(ap, tap):
            (r0, r1), (c0, c1) = (((max(0, e - 1), n + min(0, e - 1)) for e, n in zip((tap // 3, tap % 3), GRID)))
            dr, dc = tap // 3 - 1, tap % 3 - 1
            return ap[:, r0:r1, c0:c1], (slice(r0 - dr, r1 - dr), slice(c0 - dc, c1 - dc))

        def image(ap):
            return ap.rearrange("p (r c) -> p r c", c=GRID[1])

        def mod_columns(bank, n):
            return bank[:, 0:2 * n].rearrange("p (t j) -> p t j", j=2)

        def chunk_blocks(ap, half):
            return ap.rearrange("p (c b w) -> p c b w", c=TT, w=2 * half)

        def query_part(d, half):
            return slice(0, half) if d else slice(half, 2 * half)

        def head_sq(e, h):
            return (hz[0] if e else mk)[:, h, 0:T]

        def halves(ap, w):
            return ap.rearrange("p (n w) -> p n w", w=w)

        def ffn_slab(l, f):
            return BASE_SLAB + l * (2 * FFN_SLABS + MIX_SLABS) + f * (FFN_SLABS + MIX_SLABS)

        def ffn_use(l, f):
            return BASE_USE + l * (2 * FFN_USES + MIX_USES) + f * (FFN_USES + MIX_USES)

        def mix_slab(l):
            return ffn_slab(l, 0) + FFN_SLABS

        def mix_use(l):
            return ffn_use(l, 0) + FFN_USES


        def wait(eng, s, n):
            if not isinstance(n, int) or n > 0:
                eng.wait_ge(s, n)

        def slab_view(w, l, c0):
            return w[l].rearrange("(k p) n -> p k n", p=P)[:, :, c0:c0 + SLAB] if isinstance(c0, int) else \
                w[l].rearrange("(k p) n -> p k n", p=P)[:, :, bass.ds(c0, SLAB)]

        block = ctx.enter_context(nc.Block())

        @block.sync
        def _(sp):
            def down_loads(s1, w):
                with sp.Fori(0, KD // 2) as j:
                    for b in range(2):
                        for i in range(2):
                            sp.wait_ge(split_done, s1 + 2 * b + i - 1 + 4 * j)
                            sp.sem_inc(stick, 1)
                            sp.dma_start(raw[i][:].rearrange("p k n -> p (k n)")[:, 0:DOWN_K * P].rearrange("p (k n) -> p k n", n=P),
                                         w[b][:, :, bass.ds(2 * P * j + P * i, P)]).then_inc(raw_loaded[i], 16)

            sp.dma_start(ident[:], io["c_ident"]).then_inc(const_loaded, 16)
            for dst, name in ((col, "cols"), (bsel, "c_bsel"), (mlmask, "c_mlmask")):
                sp.dma_start(dst[:], io[name]).then_inc(const_loaded, 16)
            sp.dma_start(cx[:], io["ctxT"].rearrange("(k p) t -> p k t", p=P)).then_inc(ctx_loaded, 16)
            sp.dma_start(x[:], io["xT"].rearrange("(k p) t -> p k t", p=P)).then_inc(x_loaded, 16)
            wm = io["w_mod"][0].rearrange("(k p) n -> p k n", p=P)
            for i in range(MOD_FIRST):
                b = i % len(modraw)
                if i >= len(modraw):
                    sp.wait_ge(mod_used, i - len(modraw) + 1)
                sp.dma_start(modraw[b][:], wm[:, :, SLAB * i:SLAB * i + SLAB]).then_inc(mod_loaded[b], 16)
            for i, (name, c0) in enumerate(IN1):
                if i < 2:
                    sp.wait_ge(mod_used, MOD_FIRST - 1 + i)
                else:
                    sp.wait_ge(split_done, 2 + i - 1)
                if name == "gate":
                    src = io["w_in"][0].rearrange("(h k p) n -> h p k n", p=P, h=2)[i - 6][:, :, c0:c0 + P]
                    dst = raw[i % 2][:].rearrange("p k n -> p (k n)")[:, 0:KD // 2 * P].rearrange("p (k n) -> p k n", n=P)
                    sp.dma_start(dst, src).then_inc(raw_loaded[i % 2], 16)
                else:
                    sp.dma_start(raw[i % 2][:], slab_view(io["w_in"], 0, c0)).then_inc(raw_loaded[i % 2], 16)
            for b in range(2):
                sp.wait_ge(split_done, OUT1_AT + b - 1)
                sp.dma_start(raw[b][:], wm[:, :, SLAB * (MOD_FIRST + b):SLAB * (MOD_FIRST + b) + SLAB]).then_inc(mod_loaded[b], 16)
            with sp.Fori(MOD_FIRST // 2 + 1, MOD_SLABS // 2) as j:
                for b in range(2):
                    sp.wait_ge(mod_used, 2 * j + b - 1)
                    sp.sem_inc(stick, 1)
                    sp.dma_start(raw[b][:], wm[:, :, bass.ds(2 * SLAB * j + SLAB * b, SLAB)]).then_inc(mod_loaded[b], 16)
            for i in range(OUT1_SLABS):
                if i < 2:
                    sp.wait_ge(mod_used, MOD_SLABS - 1 + i)
                else:
                    sp.wait_ge(split_done, OUT1_AT + i - 1)
                sp.dma_start(raw[i % 2][:], slab_view(io["w_out"], 0, SLAB * i)).then_inc(raw_loaded[i % 2], 16)
            with sp.Fori(0, UP_STEPS) as j:
                for b in range(2):
                    sp.wait_ge(split_done, UP1_AT + b - 1 + 2 * j)
                    sp.sem_inc(stick, 1)
                    sp.dma_start(raw[b][:], slab_view(io["w_up"], 0, FF * b + SLAB * j)).then_inc(raw_loaded[b], 16)
            down1 = io["w_down"][0].rearrange("(h k p) n -> h p k n", p=P, h=2)
            down_loads(DOWN1_AT, down1)

            def ffn(l, f):
                w1, w3, w2 = (io[f"{n}_ffn{f + 1}_2"] for n in ("w1", "w3", "w2"))
                s0 = ffn_slab(l, f)
                with sp.Fori(0, UP_STEPS) as j:
                    for b, w in ((0, w1), (1, w3)):
                        sp.wait_ge(split_done, s0 + b - 1 + 2 * j)
                        sp.sem_inc(stick, 1)
                        sp.dma_start(raw[b][:], slab_view(w, l, SLAB * j)).then_inc(raw_loaded[b], 16)
                s1 = s0 + 2 * UP_STEPS
                w2v = w2[l].rearrange("(h k p) n -> h p k n", p=P, h=2)
                down_loads(s1, w2v)

            def mix(l):
                s0 = mix_slab(l)
                win = io["w_in_2"]
                order = [COL["q_sb"], COL["k_sb"], COL["v_sb"], COL["q_r"], COL["k_r"], COL["v_r"], COL["v_r"] + SLAB, COL["u"],
                         COL["g_r"], COL["g_r"] + SLAB]
                for i, c0 in enumerate(order):
                    sp.wait_ge(split_done, s0 + i - 1)
                    sp.dma_start(raw[i % 2][:], slab_view(win, l, c0)).then_inc(raw_loaded[i % 2], 16)
                with sp.Fori(0, 4) as j:
                    for g in range(3):
                        sp.wait_ge(split_done, s0 + 10 + g - 1 + 4 * j)
                        sp.sem_inc(stick, 1)
                        sp.dma_start(raw[g % 2][:], slab_view(win, l, COL["gate"] + g * D + SLAB * j)).then_inc(raw_loaded[g % 2], 16)
                    sp.wait_ge(split_done, s0 + 13 - 1 + 4 * j)
                    sp.sem_inc(stick, 1)
                    for k0, n, name in ((0, 2, "sb"), (2, 4, "ret"), (6, 2, "pool")):
                        sp.dma_start(raw[1][:, k0:k0 + n, :], slab_view(io[f"w_branch_{name}_2"], l, SLAB * j)).then_inc(raw_loaded[1], 16)
                with sp.Fori(0, 2) as j:
                    for b in range(2):
                        sp.wait_ge(split_done, s0 + 26 + b - 1 + 2 * j)
                        sp.sem_inc(stick, 1)
                        sp.dma_start(raw[b][:], slab_view(io["w_out_2"], l, SLAB * (2 * j + b))).then_inc(raw_loaded[b], 16)

            for l in range(LAYERS):
                ffn(l, 0)
                mix(l)
                ffn(l, 1)
            ov = io["out"].rearrange("b (t p) (k q) -> p (b t) k q", p=P, q=P)
            for k in range(KD):
                sp.wait_ge(out_copied, k + 1)
                sp.dma_start(ov[:, :, k, :], x[:, k, :].rearrange("p (t q) -> p t q", q=P)).then_inc(out_stored, 16)
            sp.wait_ge(out_stored, 16 * KD)

        EXTRA = 2 * 4

        def loads_before(l, stage, b):
            n = (BASE_SLAB - 2) // 2 + l * (2 * FFN_SLABS + MIX_SLABS) // 2 + (EXTRA * l if b == 1 else 0)
            if stage >= 1:
                n += FFN_SLABS // 2
            if stage >= 2:
                n += MIX_SLABS // 2 + (EXTRA if b == 1 else 0)
            return n

        @block.gpsimd
        def _(pool):
            nc.gpsimd.memset(ones[:], 1.0).then_inc(const_made, 1)
            nc.gpsimd.memset(eps[:], EPS).then_inc(const_made, 1)
            for b in range(2):
                nc.gpsimd.memset(pad[b][:], 0.0).then_inc(pad_zeroed, 1)
            pool.sem_inc(split_done, 2)
            pool.sem_inc(slab_used, 2)

            def split(idx, b, loaded, n=8 * SLAB):
                pool.wait_ge(raw_loaded[b], 16 * loaded)
                pool.wait_ge(slab_used, idx - 1)
                pool.sem_inc(tick, 1)
                r, h, o = (a[b][:].rearrange("p k n -> p (k n)")[:, 0:n] for a in (raw, whi, wlo))
                nc.gpsimd.tensor_scalar(h, r, 1.0, 1.0, ALU.mult, ALU.mult).then_inc(hi_done, 1)
                pool.wait_ge(hi_done, idx - 1)
                nc.gpsimd.tensor_tensor(o, r, h.bitcast(F32), ALU.subtract).then_inc(split_done, 1)

            def ffn(l, f):
                s0 = ffn_slab(l, f)
                with pool.Fori(0, UP_STEPS) as j:
                    for b in range(2):
                        split(s0 + b + 2 * j, b, loads_before(l, 2 * f, b) + 1 + j)
                with pool.Fori(0, KD) as n:
                    for b in range(2):
                        split(s0 + 2 * UP_STEPS + b + 2 * n, b, loads_before(l, 2 * f, b) + UP_STEPS + 1 + n, DOWN_K * P)

            def mix(l):
                s0 = mix_slab(l)
                for i in range(10):
                    split(s0 + i, i % 2, loads_before(l, 1, i % 2) + i // 2 + 1)
                n0, n1 = (loads_before(l, 1, b) + 5 for b in range(2))
                with pool.Fori(0, 4) as j:
                    split(s0 + 10 + 4 * j, 0, n0 + 1 + 2 * j)
                    split(s0 + 11 + 4 * j, 1, n1 + 1 + 4 * j)
                    split(s0 + 12 + 4 * j, 0, n0 + 2 + 2 * j)
                    split(s0 + 13 + 4 * j, 1, n1 + 4 + 4 * j)
                with pool.Fori(0, 2) as j:
                    split(s0 + 26 + 2 * j, 0, n0 + 9 + j)
                    split(s0 + 27 + 2 * j, 1, n1 + 17 + j)

            def denominators():
                for h in range(ML_HEADS):
                    for i in range(1, TAT):
                        for d in range(2):
                            s, n = TAT * h + i, 10 * h + 2 * (i - 1) + d
                            if i == 1:
                                pool.wait_ge(a_made, 2 * s + d + 1)
                                if h:
                                    pool.wait_ge(den_ready, 2 * h - 1 + d)
                                nc.gpsimd.tensor_tensor(asum[d][:], aw[d][(s - 1) % 2][:], aw[d][s % 2][:], ALU.add).then_inc(a_added, 1)
                            else:
                                pool.wait_ge(a_masked, 8 * h + 2 * (i - 2) + d + 1)
                                pool.wait_ge(a_added, n - 1)
                                c = live(d, i - 2)
                                nc.gpsimd.tensor_tensor(asum[d][:, c], asum[d][:, c], aw[d][s % 2][:, c], ALU.add).then_inc(a_added, 1)

            pool.wait_ge(mod_used, MOD_FIRST)
            for i, (name, _) in enumerate(IN1):
                if i == 12:
                    denominators()
                split(2 + i, i % 2, i // 2 + 1, KD // 2 * P if name == "gate" else 8 * SLAB)
            def chunk_end(n):
                h, d = n // 2, n % 2
                if n:
                    pool.wait_ge(hkq, 2 * n)
                else:
                    pool.wait_ge(hgmask_loaded, 16)
                nc.gpsimd.tensor_tensor(halves(eb[:], P), pend[:, d, h, :].rearrange("p (c o) -> p c o", o=1).to_broadcast([P, TAT, P]),
                                        halves(hf[d][:, h, :], P), ALU.subtract).then_inc(hdb, 1)

            def keys(n):
                h, d = n // 2, n % 2
                pool.wait_ge(heab, 2 * n + 2)
                if n:
                    pool.wait_ge(ht_ready, 2 * n)
                nc.gpsimd.tensor_tensor(kt[:], hz[d][:, h, :], (ea if d else eb)[:], ALU.mult).then_inc(hkq, 1)

            def queries(n):
                h, d = n // 2, n % 2
                if h:
                    pool.wait_ge(ho_ready, h)
                nc.gpsimd.tensor_tensor(qt[d][:], hq[:, h, :], (eb if d else ea)[:, 0:T], ALU.mult).then_inc(hkq, 1)

            pool.wait_ge(hep_done, 1)
            pool.wait_ge(slab_used, 2 + IN1_SLABS)
            pool.wait_ge(hg_step, 2 + 19 + 20)
            chunk_end(0)
            for lev in range(LEVELS * HG_N):
                n, m = lev // LEVELS, lev % LEVELS
                h, d, half = n // 2, n % 2, 2 ** m
                if lev >= 3:
                    pool.wait_ge(hx_up, lev - 2)
                    pool.wait_ge(hx_lo, lev - 2)
                b3 = halves(hf[d][:, h, 0:T], 2 * half)
                nc.gpsimd.tensor_tensor(halves(yl[lev % 3][:], 2 * half), b3,
                                        b3[:, :, half - 1 + d:half + d].to_broadcast([P, T // (2 * half), 2 * half]), ALU.subtract).then_inc(hy_done, 1)
                if m == 1:
                    keys(n)
                if m == 4:
                    queries(n)
                if m == 5 and n + 1 < HG_N:
                    chunk_end(n + 1)
            pool.wait_ge(mod_turned, 2)
            for i in range(OUT1_SLABS):
                split(OUT1_AT + i, i % 2, (IN1_SLABS + i) // 2 + 1)
            up_loads = (IN1_SLABS + OUT1_SLABS) // 2

            def hidden_low(j):
                pool.wait_ge(hidden_done, 2 + 2 * j)
                pool.sem_inc(tick, 1)
                at = slice(2 * j, 2 * j + 2) if isinstance(j, int) else bass.ds(2 * j, 2)
                nc.gpsimd.tensor_tensor(ul[:, at, :], sil[1][:], uh[:, at, :].bitcast(F32), ALU.subtract).then_inc(hidden_done, 1)

            for b in range(2):
                split(UP1_AT + b, b, up_loads + 1)
            with pool.Fori(1, UP_STEPS) as j:
                for b in range(2):
                    split(UP1_AT + b + 2 * j, b, up_loads + 1 + j)
                hidden_low(j - 1)
            for b in range(2):
                split(DOWN1_AT + b, b, up_loads + UP_STEPS + 1, DOWN_K * P)
            hidden_low(UP_STEPS - 1)
            with pool.Fori(1, KD) as n:
                for b in range(2):
                    split(DOWN1_AT + b + 2 * n, b, up_loads + UP_STEPS + 1 + n, DOWN_K * P)

            for l in range(LAYERS):
                ffn(l, 0)
                mix(l)
                ffn(l, 1)

        def act_squares(act, n, src, W):
            for k in range(KD):
                if 8 * n + k >= 2:
                    act.wait_ge(sq_added, 8 * n + k - 1)
                nc.scalar.activation(sq[k % 2][:, 0:W], src[:, k, :], ACT.Square).then_inc(sq_done, 1)

        def act_high(k, gain):
            at = bass.ds(k, 1)
            nc.scalar.activation(hh[:, at, :], x[:, at, :], ACT.Copy, scale=col[:, bass.ds(gain + k, 1)]).then_inc(hh_done, 1)

        def act_squares_down(act, n, u1, high=None):
            with act.Fori(0, KD // 2) as j:
                for i in range(2):
                    act.wait_ge(pm_free[i], u1 + 1 + j)
                    if high is not None:
                        act.sem_inc(atick, 1)
                        act_high(2 * j + i, high)
                    act.wait_ge(sq_added, 8 * n + i - 1 + 2 * j)
                    act.sem_inc(atick, 1)
                    nc.scalar.activation(sq[i][:].rearrange("p (o t) -> p o t", o=1), x[:, bass.ds(2 * j + i, 1), :], ACT.Square).then_inc(sq_done, 1)

        def act_root(act, n, W=T, std=std):
            act.wait_ge(sq_summed, n + 1)
            if n:
                act.wait_ge(rstd_done, n)
            nc.scalar.activation(std[:, 0:W], pa[0][:, 0:W], ACT.Sqrt, bias=eps[:], scale=1.0 / D).then_inc(std_done, 1)

        @block.scalar
        def _(act):
            act.wait_ge(const_loaded, 16 * 4)
            act.wait_ge(const_made, 2)
            nc.scalar.activation(silc[:], cols("c", 0, 16).rearrange("p (k j) -> p k j", j=2), ACT.Silu).then_inc(mod_in, 1)
            act.wait_ge(lb_step, 3)
            nc.scalar.activation(lbe[:], lbe[:], ACT.Exp).then_inc(lb_exp, 1)

            def norm_h(n, nh, src=x, W=T, hi=hh, shift=None, squares=True):
                if n >= 2:
                    if squares:
                        act_squares(act, n, src, W)
                    act_root(act, n, W)
                for k in range(KD):
                    act.wait_ge(hn_done, 8 * n + k + 1)
                    if shift is None:
                        nc.scalar.activation(hi[:, k, :], hn[k % 2][:, 0:W], ACT.Copy).then_inc(hh_done, 1)
                    else:
                        nc.scalar.activation(hi[:, k, :], hn[k % 2][:, 0:W], ACT.Identity, bias=shift(k)).then_inc(hh_done, 1)

            def head_square(e, h, y4):
                nc.scalar.activation(head_sq(e, h), y4[:, h, :], ACT.Square).then_inc(t_sq, 1)

            def head_root(e, h, bank):
                act.wait_ge(t_ss, 4 * e + h + 1)
                nc.scalar.activation(head_sq(e, h), bank, ACT.Sqrt, bias=eps[:], scale=1.0 / HEAD_DIM).then_inc(t_std, 1)

            def first():
                act.wait_ge(ctx_loaded, 16)
                act_squares(act, 0, cx, CT)
                act_root(act, 0, CT, cstd)
                act.wait_ge(x_loaded, 16)
                act_squares(act, 1, x, T)
                act_root(act, 1)
                for g in range(2):
                    act.wait_ge(mod_used, MOD_FIRST // 2 * (g + 1))
                    nc.scalar.activation(modrow[0][:, D * g:D * g + D].rearrange("p (b n) -> p b n", b=2), pm[g][0:2, :, :], ACT.Copy).then_inc(mod_row, 1)
                act.wait_ge(mod_done, 5)
                norm_h(0, 0, cx, CT, ch, lambda k: mod_col(0, k, 1))
                norm_h(1, 1, shift=lambda k: mod_col(0, k))
                act.wait_ge(pad_zeroed, 2)
                act.wait_ge(hl_done, 16)
                for t in range(2):
                    nc.scalar.activation(cpad[t][:, 0:1], eps[:], ACT.Copy, scale=0.0).then_inc(cpad_filled, 1)
                    nc.scalar.activation(cpad[t][:, CT + 1:CT + 2], eps[:], ACT.Copy, scale=0.0).then_inc(cpad_filled, 1)
                for i in range(4):
                    p = IN1_P[i]
                    act.wait_ge(slab_used, 2 + i + 1)
                    for t in range(2):
                        if i:
                            act.wait_ge(conv_step, CONV_AT[2 * (i - 1) + t + 1])
                        if t == 1:
                            act.wait_ge(pad_filled, i + 1)
                        nc.scalar.activation(pad[t][:, 1:GRID[0] + 1, 1:GRID[1] + 1], image(pm[p][:, t, :]), ACT.Copy).then_inc(
                            pm_free[p] if t else pad_filled, 1)
                        if i >= 2:
                            if t == 1:
                                act.wait_ge(cpad_filled, 4 + i - 1)
                            nc.scalar.activation(cpad[t][:, 1:CT + 1], pa[p][:, CT * t:CT * t + CT], ACT.Copy).then_inc(
                                ctx_free[p] if t else cpad_filled, 1)
                    for t in range(2):
                        act.wait_ge(conv_step, CONV_AT[2 * i + t + 1])
                        dst, w = (mq[:, 2 * i + t, :], T) if i < 2 else (mk[:, 2 * i + t - 4, :], TA)
                        nc.scalar.activation(dst, cacc[t][:, 0:w], ACT.Silu).then_inc(conv_silu, 1)
                def tokens(i, dst, e):
                    p = IN1_P[i]
                    act.wait_ge(slab_used, 2 + i + 1)
                    c = slice(SLAB * e, SLAB * e + SLAB)
                    nc.scalar.activation(dst[:, 0:TT, c], pm[p][:].rearrange("p a (b c) -> p (a b) c", b=2), ACT.Copy).then_inc(pm_free[p], 1)
                    nc.scalar.activation(dst[:, TT:TAT, c], pa[p][:].rearrange("p (b c) -> p b c", b=2), ACT.Copy).then_inc(ctx_free[p], 1)

                for e in range(2):
                    tokens(4 + e, mv, e)
                act.wait_ge(slab_used, 2 + 8)
                nc.scalar.activation(gall[:, 0:T], pm[0][0:16, 0, :], ACT.Copy).then_inc(pm_free[0], 1)
                nc.scalar.activation(gall[:, T:TA], pa[0][0:16, 0:CT], ACT.Copy).then_inc(ctx_free[0], 1)
                for g in range(4):
                    d = g // 2
                    dst = (GI, GF)[g % 2][d]
                    gb = col[0:4, COL_AT["gate_b"] + g:COL_AT["gate_b"] + g + 1]
                    act.wait_ge(gsel_ready, 2 * g + 1)
                    nc.scalar.activation(dst[:, LATC[d]], pa[2][0:4, :], ACT.Identity, bias=gb).then_inc(gsel_copied, 1)
                    act.wait_ge(gsel_ready, 2 * g + 2)
                    nc.scalar.activation(dst[:, CTXC[d]], pa[3][0:4, 0:CT], ACT.Identity, bias=gb).then_inc(gsel_copied, 1)
                act.wait_ge(gsel_copied, 8)
                for d in range(2):
                    nc.scalar.activation(GT[d][:], GF[d][:], ACT.Abs).then_inc(gact, 1)
                    act.wait_ge(gact, 3 * d + 1)
                    nc.scalar.activation(GT[d][:], GT[d][:], ACT.Exp, scale=-1.0).then_inc(gact, 1)
                    act.wait_ge(gact, 3 * d + 2)
                    nc.scalar.activation(GT[d][:], GT[d][:], ACT.Ln, bias=1.0).then_inc(gact, 1)
                for d in range(2):
                    act.wait_ge(gstep, 6 * d + 6)
                    nc.scalar.activation(GT[d][:, LATC[d]], GT[d][:, LATC[d]], ACT.Exp, scale=-1.0).then_inc(gdn, 1)
                act.wait_ge(gtr, 1)
                nc.scalar.activation(gcol[:], pa[2][:, 0:2 * TAT * ML_HEADS].rearrange("p (d t h) -> p d t h", d=2, h=ML_HEADS),
                                     ACT.Copy).then_inc(gcol_done, 1)
                for e in range(2):
                    p = IN1_P[8 + e]
                    act.wait_ge(slab_used, 2 + 8 + e + 1)
                    nc.scalar.activation(mo[:, 2 * e:2 * e + 2, :], pm[p][:], ACT.Sigmoid).then_inc(pm_free[p], 1)
                act.wait_ge(gcol_done, 1)
                for h in range(ML_HEADS):
                    for d in range(2):
                        n = 2 * h + d
                        act.wait_ge(mb_ready, 2 * n + 1)
                        if h:
                            act.wait_ge(ml_h, 5 * (n - 2) + 1)
                        nc.scalar.activation(dnb[d][:], pa[2 + d][:], ACT.Copy).then_inc(mb_copied, 1)
                        act.wait_ge(mb_ready, 2 * n + 2)
                        if h:
                            act.wait_ge(w_exp, 12 * h - 1 + d)
                            act.wait_ge(w_pre, 8 * h - 1 + d)
                        nc.scalar.activation(nmb[d][:], pa[2 + d][:], ACT.Copy).then_inc(mb_copied, 1)
                    for i in range(TAT):
                        s = TAT * h + i
                        for d in range(2):
                            n, r = 2 * h + d, 2 * s + d
                            if i < 2:
                                act.wait_ge(mb_copied, 2 * n + 2)
                                if r >= 4:
                                    act.wait_ge(a_made, r - 3)
                                nc.scalar.activation(wt[d][s % 2][:], nmb[d][:], ACT.Exp, scale=-1.0,
                                                     bias=gcol[:, d, TT + i, h:h + 1]).then_inc(w_exp, 1)
                            else:
                                act.wait_ge(w_pre, 8 * h + 2 * (i - 2) + d + 1)
                                c = live(d, i - 2)
                                nc.scalar.activation(wt[d][s % 2][:, c], wt[d][s % 2][:, c], ACT.Exp, scale=-1.0).then_inc(w_exp, 1)
                        if h and i == 1:
                            act.wait_ge(ml_h, 10 * h)
                            head_square(0, h - 1, mq)
                        if h and i == 4:
                            head_root(0, h - 1, pa[2][:])
                    for d in range(2):
                        act.wait_ge(den_ready, 2 * h + d + 1)
                        if h:
                            act.wait_ge(ml_h, 5 * (2 * h - 2 + d) + 5)
                        nc.scalar.activation(dab[d][:], pm[d][:, 1, :], ACT.Abs).then_inc(den_abs, 1)
                act.wait_ge(ml_h, 5 * 2 * ML_HEADS)
                head_square(0, ML_HEADS - 1, mq)
                head_root(0, ML_HEADS - 1, pa[2][:])
                act.wait_ge(t_done, 1)
                def log_forget(d):
                    act.wait_ge(hg_step, 2 + 19 * d + 8)
                    nc.scalar.activation(hf[d][:], hf[d][:], ACT.Ln).then_inc(hg_ln, 1)

                for i in range(10, IN1_SLABS):
                    name, e, p = IN1[i][0], i % 2, IN1_P[i]
                    if i == IN1_SLABS - 4:
                        log_forget(0)
                    act.wait_ge(slab_used, 2 + i + 1)
                    if name == "hv":
                        tokens(i, hv, e)
                    elif name in ("hq", "hg"):
                        dst = hq if name == "hq" else hg
                        if i == IN1_SLABS - 2:
                            log_forget(1)
                        nc.scalar.activation(dst[:, 2 * e:2 * e + 2, :], pm[p][:], ACT.Silu).then_inc(pm_free[p], 1)
                    else:
                        d = int(name == "zb")
                        n = 4 * d + 2 * e
                        two = slice(2 * e, 2 * e + 2)
                        z, zc = pm[p][:], pa[p][:].rearrange("p (b c) -> p b c", b=2)
                        nc.scalar.activation(hf[d][:, two, 0:T], z, ACT.Sigmoid).then_inc(hg_sig, 1)
                        act.wait_ge(hg_sig, n + 1)
                        nc.scalar.activation(hz[d][:, two, 0:T], z, ACT.Sigmoid, scale=-1.0).then_inc(pm_free[p], 1)
                        nc.scalar.activation(hf[d][:, two, T:TA], zc, ACT.Sigmoid).then_inc(hg_sig, 1)
                        act.wait_ge(hg_sig, n + 2)
                        nc.scalar.activation(hz[d][:, two, T:TA], zc, ACT.Sigmoid, scale=-1.0).then_inc(ctx_free[p], 1)
                act.dma_start(hgmask[:], io["c_hgmask"]).then_inc(hgmask_loaded, 16)
                for p in range(2):
                    act.wait_ge(pm_free[p], HG_USE)
                    act.wait_ge(ctx_free[p], ctx_uses_[p])
                act.wait_ge(hg_step, 2 + 19 + 20)
                nc.scalar.activation(epend[:], pend[:], ACT.Exp).then_inc(hep_done, 1)
                def decays(n):
                    h, d = n // 2, n % 2
                    act.wait_ge(hdb, n + 1)
                    nc.scalar.activation(ea[:], hf[d][:, h, :], ACT.Exp).then_inc(heab, 1)
                    nc.scalar.activation(eb[:], eb[:], ACT.Exp).then_inc(heab, 1)

                def mod_rest(n):
                    act.wait_ge(mod_used, MOD_FIRST + 2 * n + 2)
                    nc.scalar.activation(modrow[1][:, 2 * SLAB * n:2 * SLAB * n + 2 * SLAB], pm[1][0:2, 0, :], ACT.Copy).then_inc(mod_row, 1)

                decays(0)
                for lev in range(LEVELS * HG_N):
                    n, m = lev // LEVELS, lev % LEVELS
                    half = 2 ** m
                    act.wait_ge(hy_done, lev + 1)
                    y = halves(yl[lev % 3][:], 2 * half)
                    for part, sign in ((slice(half, 2 * half), 1.0), (slice(0, half), -1.0)):
                        nc.scalar.activation(y[:, :, part], y[:, :, part], ACT.Exp, scale=sign).then_inc(hx_exp, 1)
                    if m == 4:
                        act.wait_ge(ht_ready, 2 * n + 1)
                        if n:
                            act.wait_ge(hkv_ready, n)
                        nc.scalar.activation(ktok[:, 0:4, :], pa[2][:].rearrange("p (c k) -> p c k", k=P), ACT.Copy).then_inc(ht_copied, 1)
                        act.wait_ge(ht_ready, 2 * n + 2)
                        nc.scalar.activation(ktok[:, 4, :], pa[3][:, 0:P], ACT.Copy).then_inc(ht_copied, 1)
                    if m == LEVELS - 1 and n + 1 < HG_N:
                        decays(n + 1)
                    if m == 1 and n:
                        mod_rest(n - 1)
                    h = n // 2
                    if h and n % 2 == 0 and m == 4:
                        act.wait_ge(pm_free[0], HG_USE + h)
                        head_square(1, h - 1, hq)
                    if h and n % 2 == 1 and m == 0:
                        head_root(1, h - 1, pm[0][:, 0, :])
                mod_rest(HG_N - 1)
                act.wait_ge(pm_free[0], OUT1_USE)
                head_square(1, HG_HEADS - 1, hq)
                head_root(1, HG_HEADS - 1, pm[0][:, 0, :])
                act.wait_ge(x_mixed, OUT1_SLABS)
                for p in range(2):
                    act.wait_ge(pm_free[p], UP1_USE)
                norm_h(2, 2, shift=lambda k: mod_col(3, k))
                def take_image(b, j):
                    act.wait_ge(slab_used, UP1_AT + 1 + b + 2 * j)
                    act.wait_ge(conv_step, CONV1 - 16 + 16 * b + 32 * j)
                    nc.scalar.activation(img[b][:], pm[b][:], ACT.Copy).then_inc(img_filled, 1)

                def take_centre(b, j):
                    for i in range(2):
                        w = col[:, bass.ds(COL_AT["ffn_conv"] + 2 * KF * 4 + KF * b + i + 2 * j, 1)]
                        if i == 1:
                            act.wait_ge(img_filled, 2 + 3 * b + 6 * j)
                        act.sem_inc(atick, 1)
                        nc.scalar.activation(sil[b][:, i, :], pm[b][:, i, :], ACT.Copy, scale=w).then_inc(pm_free[b] if i else img_filled, 1)
                    act.sem_inc(img_filled, 1)

                def up_step(j, last):
                    act.wait_ge(hidden_done, 1 + 2 * j)
                    take_image(1, j)
                    take_centre(1, j)
                    act.wait_ge(conv_step, CONV1 + 16 + 32 * j)
                    nc.scalar.activation(sil[0][:], sil[0][:], ACT.Silu).then_inc(usilu_done, 1)
                    if not last:
                        take_image(0, j + 1)
                    act.wait_ge(up_product, 1 + j)
                    if not last:
                        take_centre(0, j + 1)
                    act.sem_inc(atick, 1)
                    nc.scalar.activation(uh[:, bass.ds(2 * j, 2), :], sil[1][:], ACT.Copy).then_inc(hidden_done, 1)

                take_image(0, 0)
                take_centre(0, 0)
                with act.Fori(0, UP_STEPS - 1) as j:
                    up_step(j, False)
                up_step(UP_STEPS - 1, True)
                act_squares_down(act, 3, DOWN1_USE)
                act_root(act, 3)
                n = NORMS1
                for k in range(KD):
                    act.wait_ge(hn_done, 8 * (n - 1) + k + 1)
                    act_high(k, ffn_gain(0, 0))
                    act.wait_ge(sq_added, 8 * n + k - 1)
                    nc.scalar.activation(sq[k % 2][:], x[:, k, :], ACT.Square).then_inc(sq_done, 1)

            first()

            def ffn(l, f):
                s0, u0 = ffn_slab(l, f), ffn_use(l, f)
                n = NORMS1 + 3 * l + 2 * f
                act_root(act, n)
                with act.Fori(0, UP_STEPS) as j:
                    act.wait_ge(pm_free[0], u0 + 1 + j)
                    nc.scalar.activation(sil[0][:], sil[0][:], ACT.Silu).then_inc(usilu_done, 1)
                act_squares_down(act, n + 1, u0 + UP_STEPS, ffn_gain(1, 0) if f and not l else None)

            def mix(l):
                s0, u0 = mix_slab(l), mix_use(l)
                n = NORMS1 + 3 * l + 1
                for p in range(2):
                    act.wait_ge(pm_free[p], u0)
                norm_h(n, n - 1, squares=False)
                for dst, name in ((decay, "c_decay"), (rope, "c_rope"), (perm, "c_perm"), (trineg, "c_trineg"), (onesneg, "c_onesneg"),
                                  (dmask, "c_dmask"), (invcnt, "c_invcnt")):
                    act.dma_start(dst[:], io[name]).then_inc(mixc_loaded, 16)
                act.wait_ge(mixc_made, 4 * l + 1)
                for g in range(4):
                    o = 64 * (g % 2)
                    act.dma_start(wpool[o:o + 64, g // 2, o:o + 64], io["w_pool_2"][l, g]).then_inc(mixc_loaded, 16)
                act.wait_ge(slab_used, s0 + 1)
                nc.scalar.activation(q_sb[:], pm[0][:], ACT.Copy, scale=SB_DIM ** -0.5).then_inc(pm_free[0], 1)
                act.wait_ge(slab_used, s0 + 2)
                nc.scalar.activation(k_sb[:], pm[1][:], ACT.Copy).then_inc(pm_free[1], 1)
                act.wait_ge(slab_used, s0 + 3)
                nc.scalar.activation(v_sb[:], pm[0][:].rearrange("p a (b c) -> p (a b) c", b=2), ACT.Copy).then_inc(pm_free[0], 1)
                nc.scalar.preload_act_table_set("natural_log_exp_and_others")

                def fill(i):
                    act.wait_ge(slab_used, s0 + i + 1)
                    if i == 3:
                        nc.scalar.activation(rraw[0][:], pm[1][:], ACT.Copy).then_inc(pm_free[1], 1)
                    elif i == 4:
                        nc.scalar.activation(rraw[1][:], pm[1][:], ACT.Copy, scale=RET_DIM ** -0.5).then_inc(pm_free[1], 1)
                    elif i in (5, 6):
                        nc.scalar.activation(v_r[:, :, SLAB * (i - 5):SLAB * (i - 4)], pm[1][:].rearrange("p a (b c) -> p (a b) c", b=2),
                                             ACT.Copy).then_inc(pm_free[1], 1)
                    elif i == 7:
                        act.wait_ge(mixc_made, 4 * l + 4)
                        nc.scalar.activation(u[:, :, PAD:], pm[1][:], ACT.Copy).then_inc(pm_free[1], 1)
                    else:
                        nc.scalar.activation(sil[i - 8][:], pm[1][:], ACT.Silu).then_inc(pm_free[1], 1)

                for h in range(SB_HEADS):
                    m = TT * (SB_HEADS * l + h)
                    for j in range(TT):
                        c = slice(LIVE_AT[j], LIVE_AT[j] + LIVE[j])
                        act.wait_ge(z_ready, m + j + 1)
                        if m + j >= TT:
                            act.wait_ge(sp_done, m + j + 1 - TT)
                        nc.scalar.activation(sc[:, c], pa[j][:, 0:LIVE[j]], ACT.Abs).then_inc(abs_done, 1)
                        act.wait_ge(abs_done, m + j + 1)
                        nc.scalar.activation(sc[:, c], sc[:, c], ACT.Exp, scale=-1.0).then_inc(exp_done, 1)
                        act.wait_ge(exp_done, m + j + 1)
                        nc.scalar.activation(sc[:, c], sc[:, c], ACT.Ln, bias=1.0).then_inc(ln_done, 1)
                    fill(3 + 2 * h)
                    for n_, j in enumerate(reversed(range(TT))):
                        c = slice(LIVE_AT[j], LIVE_AT[j] + LIVE[j])
                        act.wait_ge(w_masked, m + n_ + 1)
                        if m:
                            act.wait_ge(sb_out, SB_HEADS * l + h)
                        nc.scalar.activation(w_[:, c], pa[j][:, 0:LIVE[j]], ACT.Exp).then_inc(w_done, 1)
                    if h + 1 < SB_HEADS:
                        fill(4 + 2 * h)

                def gate(g, j):
                    act.wait_ge(slab_used, s0 + 10 + g + 1 + 4 * j)
                    nc.scalar.activation(gates[:, g], pm[g % 2][:], ACT.Sigmoid).then_inc(pm_free[g % 2], 1)

                gate(0, 0)
                gate(1, 0)
                for g in range(2):
                    act.wait_ge(pool_out, 2 * l + g + 1)
                    nc.scalar.activation(pt[:, g, :], pa[g][:], ACT.Copy, scale=col[:, GAINS["pool"] + 2 * l + g:GAINS["pool"] + 2 * l + g + 1]).then_inc(pool_scaled, 1)
                for h in range(RET_HEADS):
                    m = RET_HEADS * l + h
                    p = h % 2
                    act.wait_ge(ret_out, m + 1)
                    if m >= 1:
                        act.wait_ge(ret_ss, m)
                    nc.scalar.activation(ret_sqr[:], pm[p][:, 0, :], ACT.Square).then_inc(ret_sq, 1)
                    act.wait_ge(ret_ss, m + 1)
                    if m >= 1:
                        act.wait_ge(ret_rstd, m)
                    nc.scalar.activation(ret_root[:], pm[p][:, 1, :], ACT.Sqrt, bias=eps[:], scale=1.0 / P).then_inc(ret_std, 1)
                gate(2, 0)
                with act.Fori(1, 4) as j:
                    act.wait_ge(mix_sum, 1 + 3 * (4 * l) + 3 * j)
                    for g in range(3):
                        gate(g, j)
                for m in range(KD // 2):
                    act.wait_ge(pm_free[m % 2], u0 + BRANCH_USE[m % 2] + 13 + m // 2)
                    for k in (2 * m, 2 * m + 1):
                        act_high(k, ffn_gain(l, 1))
                    for k in (2 * m, 2 * m + 1):
                        act.wait_ge(sq_added, 8 * (n + 1) + k - 1)
                        nc.scalar.activation(sq[k % 2][:], x[:, k, :], ACT.Square).then_inc(sq_done, 1)

            for l in range(LAYERS):
                ffn(l, 0)
                mix(l)
                ffn(l, 1)
            act_root(act, NORMS1 + 3 * LAYERS)

        def dve_square(v, n, i, done, start=False, W=T):
            acc = (std if n else cstd)[:, 0:W]
            v.wait_ge(sq_done, done)
            if start:
                nc.vector.tensor_copy(acc, sq[0][:, 0:W]).then_inc(sq_added, 1)
            else:
                v.wait_ge(sq_added, done - 1)
                nc.vector.tensor_tensor(acc, acc, sq[i][:, 0:W], ALU.add).then_inc(sq_added, 1)

        def dve_squares(v, n, W=T):
            for k in range(KD):
                dve_square(v, n, k % 2, 8 * n + k + 1, k == 0, W)

        def dve_low(v, n, k, gain):
            v.wait_ge(hh_done, 8 * (n - 1) + 1 + k)
            at = bass.ds(k, 1)
            nc.vector.scalar_tensor_tensor(hl[:, at, :], x[:, at, :], col[:, bass.ds(gain + k, 1)], hh[:, at, :].bitcast(F32),
                                           ALU.mult, ALU.subtract).then_inc(hl_done, 1)

        def dve_down(v, n, s1, add, low=None):
            def pair(j, first):
                for i in range(2):
                    v.wait_ge(slab_used, s1 + 3 + i + 4 * j)
                    add(i, 2 * j + i)
                    if not (first and i == 0):
                        if low is not None:
                            dve_low(v, n, 2 * j + i - 1, low)
                        dve_square(v, n, 1 - i, 8 * n + i + 2 * j, first)

            pair(0, True)
            with v.Fori(1, KD // 2) as j:
                pair(j, False)
            if low is not None:
                dve_low(v, n, KD - 1, low)
                v.sem_inc(hn_done, KD)
            dve_square(v, n, 1, 8 * n + KD)

        def dve_rstd(v, n, W=T, std=std, rstd=rstd):
            v.wait_ge(std_done, n + 1)
            if n >= 2:
                v.wait_ge(hn_done, 8 * n)
            nc.vector.reciprocal(rstd[:, 0:W], std[:, 0:W]).then_inc(rstd_done, 1)
            v.wait_ge(rstd_done, n + 1)

        def dve_norm(v, n, nh, gain, out=None, src=x, W=T, hi=hh, lo=hl, shift=None):
            if n >= 2:
                dve_rstd(v, n)
            else:
                v.wait_ge(rstd_done, n + 1)
            def scaled(k):
                dst = hn[k % 2][:, 0:W] if out is None else out[:, k, :]
                if out is None and 8 * nh + k >= 2:
                    v.wait_ge(hl_done, 8 * nh + k - 1)
                nc.vector.scalar_tensor_tensor(dst, src[:, k, :], gain(k), (rstd if n else crstd)[:, 0:W], ALU.mult, ALU.mult).then_inc(hn_done, 1)

            def low(k):
                v.wait_ge(hh_done, 8 * nh + k + 1)
                v.wait_ge(hn_done, 8 * n + k + 1)
                if shift is None:
                    nc.vector.tensor_tensor(lo[:, k, :], hn[k % 2][:, 0:W], hi[:, k, :].bitcast(F32), ALU.subtract).then_inc(hl_done, 1)
                else:
                    nc.vector.scalar_tensor_tensor(lo[:, k, :], hn[k % 2][:, 0:W], shift(k), hi[:, k, :].bitcast(F32),
                                                   ALU.add, ALU.subtract).then_inc(hl_done, 1)

            for k in range(KD):
                scaled(k)
                if out is None and k:
                    low(k - 1)
            if out is None:
                low(KD - 1)

        @block.vector
        def _(v):
            for s in (hidden_done, mix_sum, mg_done):
                v.sem_inc(s, 1)
            v.wait_ge(const_loaded, 16 * 4)

            def lower_bounds():
                lg = cols("lb_logits", 0, 16).rearrange("p (j l h) -> p j l h", j=2, l=2)
                nc.vector.tensor_tensor(lbm[:], lg[:, :, 0, :], lg[:, :, 1, :], ALU.max).then_inc(lb_step, 1)
                v.wait_ge(lb_step, 1)
                for i in range(2):
                    nc.vector.tensor_tensor(lbe[:, :, i, :], lg[:, :, i, :], lbm[:], ALU.subtract).then_inc(lb_step, 1)
                v.wait_ge(lb_exp, 1)
                nc.vector.tensor_tensor(lbm[:], lbe[:, :, 0, :], lbe[:, :, 1, :], ALU.add).then_inc(lb_step, 1)
                v.wait_ge(lb_step, 4)
                nc.vector.reciprocal(oms[:], lbm[:]).then_inc(lb_step, 1)
                v.wait_ge(lb_step, 5)
                nc.vector.tensor_tensor(lb[:], lbe[:, :, 0, :], oms[:], ALU.mult).then_inc(lb_step, 1)
                nc.vector.tensor_tensor(om[:], lbe[:, :, 1, :], oms[:], ALU.mult).then_inc(lb_step, 1)
                v.wait_ge(lb_step, 7)
                nc.vector.tensor_scalar_max(lb[:], lb[:], 2.0 ** -60).then_inc(lb_step, 1)
                nc.vector.tensor_scalar(oms[:], om[:], HEAD_SCALE, 1.0, ALU.mult, ALU.mult).then_inc(lb_step, 1)

            def conv_tile(c0, dst, w, taps):
                for n, (tap, view) in enumerate(taps):
                    if n:
                        v.wait_ge(conv_step, c0 + n)
                    if n == 0:
                        nc.vector.tensor_scalar(dst, view, w(tap), 1.0, ALU.mult, ALU.mult).then_inc(conv_step, 1)
                    else:
                        nc.vector.scalar_tensor_tensor(dst, view, w(tap), dst, ALU.mult, ALU.add).then_inc(conv_step, 1)

            def windows(src):
                return [(3 * dy + dx, src[:, dy:dy + GRID[0], dx:dx + GRID[1]]) for dy in range(3) for dx in range(3)]

            def head_norm(e, h, y4, gate, norm):
                g = 4 * e + h
                v.wait_ge(t_std, g + 1)
                nc.vector.reciprocal(head_sq(e, h), head_sq(e, h)).then_inc(t_step, 1)
                v.wait_ge(t_step, 3 * g + 1)
                nc.vector.scalar_tensor_tensor(y4[:, h, :], y4[:, h, :], cols(norm, h), head_sq(e, h), ALU.mult, ALU.mult).then_inc(t_step, 1)
                v.wait_ge(t_step, 3 * g + 2)
                nc.vector.tensor_tensor(y4[:, h, :], y4[:, h, :], gate[:, h, :], ALU.mult).then_inc(t_step, 1)
                v.wait_ge(t_step, 3 * g + 3)

            def mlstm():
                for i in range(8):
                    t, c0 = i % 2, CONV_AT[i]
                    v.wait_ge(pad_filled, i // 2 + 1)
                    if t:
                        v.wait_ge(pm_free[IN1_P[i // 2]], IN1_USE[i // 2] + 1)
                    if i >= 2:
                        v.wait_ge(conv_silu, i - 1)
                    conv_tile(c0, image(cacc[t][:, 0:T]), lambda tap: cols("ml_conv", 8 * tap + i), windows(pad[t]))
                    if i >= 4:
                        s = i // 2
                        v.wait_ge(cpad_filled, 4 + s - 1)
                        if t:
                            v.wait_ge(ctx_free[IN1_P[s]], IN1_CTX[s] + 1)
                        conv_tile(c0 + 9, cacc[t][:, T:TA], lambda tap: cols("ml_conv", 8 * tap + i),
                                  [(3 + dx, cpad[t][:, dx:dx + CT]) for dx in range(3)])
                for d in range(2):
                    b = 6 * d
                    way = slice(None) if d == 0 else slice(None, None, -1)
                    v.wait_ge(gsel_copied, 8)
                    v.wait_ge(gact, 3 * d + 3)
                    nc.vector.scalar_tensor_tensor(GF[d][:], GF[d][:], 0.0, GT[d][:], ALU.min, ALU.subtract).then_inc(gstep, 1)
                    v.wait_ge(gstep, b + 1)
                    nc.vector.tensor_tensor_scan(GT[d][:, way], GF[d][:, way], GF[d][:, way], 0.0, ALU.add, ALU.min).then_inc(gstep, 1)
                    v.wait_ge(gstep, b + 2)
                    nc.vector.tensor_tensor(GI[d][:], GI[d][:], GT[d][:], ALU.subtract).then_inc(gstep, 1)
                    v.wait_ge(gstep, b + 3)
                    nc.vector.tensor_tensor_scan(GF[d][:, way], GI[d][:, way], GI[d][:, way], 0.0, ALU.max, ALU.max).then_inc(gstep, 1)
                    v.wait_ge(gstep, b + 4)
                    nc.vector.tensor_tensor(GT[d][:], GT[d][:], GF[d][:], ALU.add).then_inc(gstep, 1)
                    v.wait_ge(gstep, b + 5)
                    nc.vector.tensor_scalar_max(GT[d][:], GT[d][:], -80.0).then_inc(gstep, 1)
                v.wait_ge(gcol_done, 1)

                def pre(s):
                    h, i = s // TAT, s % TAT
                    if i < 2:
                        return
                    for d in range(2):
                        n, r = 2 * h + d, 2 * s + d
                        v.wait_ge(mb_copied, 2 * n + 2)
                        v.wait_ge(a_made, r - 3)
                        c = live(d, i - 2)
                        nc.vector.tensor_scalar(wt[d][s % 2][:, c], nmb[d][:, c], gcol[:, d, i - 2, h:h + 1], 0.0,
                                                ALU.subtract, ALU.max).then_inc(w_pre, 1)

                for s in range(TAT * ML_HEADS):
                    h, i = s // TAT, s % TAT
                    if s + 1 < TAT * ML_HEADS:
                        pre(s + 1)
                    for d in range(2):
                        r = 2 * s + d
                        v.wait_ge(ms_ready, s + 1)
                        v.wait_ge(w_exp, r + 1)
                        if s >= 2:
                            v.wait_ge(nd_acc, r - 3)
                            h2, i2 = (s - 2) // TAT, (s - 2) % TAT
                            v.wait_ge(a_added, 10 * h2 + 2 * max(i2 - 1, 0) + d + 1)
                        c = slice(0, T) if i < 2 else live(d, i - 2)
                        a = aw[d][s % 2]
                        nc.vector.scalar_tensor_tensor(a[:, c], pa[s % 2][:, c], HEAD_SCALE, wt[d][s % 2][:, c], ALU.mult, ALU.mult).then_inc(a_made, 1)
                        if i >= 2:
                            v.wait_ge(a_made, r + 1)
                            dg = slice(P * (i - 2), P * (i - 1))
                            nc.vector.tensor_tensor(a[:, dg], a[:, dg], mlmask[:, d, :], ALU.mult).then_inc(a_masked, 1)
                    if h and i == 4:
                        head_norm(0, h - 1, mq, mo, "ml_norm")
                    if i == TAT - 1:
                        for d in range(2):
                            n = 2 * h + d
                            b = 5 * n
                            v.wait_ge(den_abs, n + 1)
                            v.wait_ge(nd_acc, 12 * h + 10 + d + 1)
                            v.wait_ge(mb_copied, 2 * n + 1)
                            nc.vector.tensor_tensor(dab[d][:], dab[d][:], dnb[d][:], ALU.max).then_inc(ml_h, 1)
                            v.wait_ge(ml_h, b + 1)
                            nc.vector.reciprocal(dab[d][:], dab[d][:]).then_inc(ml_h, 1)
                            v.wait_ge(ml_h, b + 2)
                            dst = dab[d][:] if d else mq[:, h, :]
                            nc.vector.tensor_tensor(dst, pm[d][:, 0, :], dab[d][:], ALU.mult).then_inc(pm_free[d], 1)
                            v.wait_ge(pm_free[d], ML_USE + h + 1)
                            v.sem_inc(ml_h, 2)
                            if d:
                                nc.vector.tensor_tensor(mq[:, h, :], mq[:, h, :], dab[d][:], ALU.add).then_inc(ml_h, 1)
                            else:
                                v.sem_inc(ml_h, 1)
                head_norm(0, ML_HEADS - 1, mq, mo, "ml_norm")
                nc.vector.tensor_copy(ym_h[:], mq[:]).then_inc(t_hi, 1)
                v.wait_ge(t_hi, 1)
                nc.vector.tensor_tensor(ym_l[:], mq[:], ym_h[:].bitcast(F32), ALU.subtract).then_inc(t_done, 1)

            def hgrn():
                last_ctx = max(i for i, c in enumerate(IN1) if c[0] == "hv")
                nc.vector.memset(resetm[:], 1.0).then_inc(hg_step, 1)
                v.wait_ge(hg_step, 1)
                nc.vector.memset(halves(resetm[:], P)[:, :, 0:1], 0.0).then_inc(hg_step, 1)
                v.wait_ge(lb_step, 9)
                b = 2
                for d in range(2):
                    for i, c in enumerate(IN1):
                        if c[0] == ("zf", "zb")[d]:
                            v.wait_ge(pm_free[IN1_P[i]], IN1_USE[i] + 1)
                            v.wait_ge(ctx_free[IN1_P[i]], IN1_CTX[i] + 1)
                    v.wait_ge(hg_sig, 4 * d + 4)
                    for h in range(HG_HEADS):
                        nc.vector.tensor_scalar(hf[d][:, h, :], hf[d][:, h, :], om[:, d, h:h + 1], lb[:, d, h:h + 1], ALU.mult, ALU.add).then_inc(hg_step, 1)
                        nc.vector.tensor_scalar(hz[d][:, h, :], hz[d][:, h, :], oms[:, d, h:h + 1], 1.0, ALU.mult, ALU.mult).then_inc(hg_step, 1)
                    b += 8
                    v.wait_ge(hg_step, b)
                    v.wait_ge(hg_ln, d + 1)
                    for h in range(HG_HEADS):
                        if d == 0:
                            nc.vector.tensor_tensor_scan(hf[0][:, h, :], resetm[:], hf[0][:, h, :], 0.0, ALU.mult, ALU.add).then_inc(hg_step, 1)
                            v.wait_ge(hg_step, b + 1)
                            nc.vector.tensor_copy(pend[:, 0, h, :], halves(hf[0][:, h, :], P)[:, :, P - 1]).then_inc(hg_step, 1)
                            b += 2
                        else:
                            v.wait_ge(slab_used, 2 + last_ctx + 1)
                            v.wait_ge(hg_step, b)
                            nc.vector.tensor_tensor_scan(ptmp[:], resetm[:], hf[1][:, h, :], 0.0, ALU.mult, ALU.add).then_inc(hg_step, 1)
                            v.wait_ge(hg_step, b + 1)
                            nc.vector.tensor_copy(pend[:, 1, h, :], halves(ptmp[:], P)[:, :, P - 1]).then_inc(hg_step, 1)
                            nc.vector.tensor_tensor(hf[1][:, h, :], ptmp[:], hf[1][:, h, :], ALU.subtract).then_inc(hg_step, 1)
                            b += 3
                    if d == 0:
                        v.sem_inc(hg_step, 3)
                        b += 3
                v.wait_ge(hg_step, b)
                v.wait_ge(slab_used, 2 + IN1_SLABS)
                v.wait_ge(hep_done, 1)
                v.wait_ge(hgmask_loaded, 16)
                def output(h):
                    v.wait_ge(ho_ready, h + 1)
                    nc.vector.tensor_copy(hq[:, h, :], pm[0][:, 0, :]).then_inc(pm_free[0], 1)

                def hgrn_norm(h):
                    head_norm(1, h, hq, hg, "hg_norm")
                    nc.vector.tensor_copy(yh_h[:, h, 0:T], hq[:, h, :]).then_inc(t_hi, 1)
                    v.wait_ge(t_hi, h + 2)
                    nc.vector.tensor_tensor(yh_l[:, h, 0:T], hq[:, h, :], yh_h[:, h, 0:T].bitcast(F32), ALU.subtract).then_inc(t_done, 1)

                def level_a(lev):
                    n, m = lev // LEVELS, lev % LEVELS
                    h, d = n // 2, n % 2
                    v.wait_ge(ha_ready, lev + 1)
                    if lev:
                        v.wait_ge(ha_copied, lev)
                    half = 2 ** m
                    nc.vector.copy_predicated(chunk_blocks(ah[h % 2][:], half)[:, :, :, query_part(d, half)],
                                              hgmask[:, LEVELS * d + m, :].rearrange("p (o b w) -> p o b w", o=1, w=half).to_broadcast(
                                                  [P, TT, P // (2 * half), half]).bitcast(mybir.dt.uint32),
                                              pa[lev % 2][:, 0:T // 2].rearrange("p (c b w) -> p c b w", c=TT, w=half)).then_inc(ha_copied, 1)

                def level_x(lev):
                    n, half = lev // LEVELS, 2 ** (lev % LEVELS)
                    h, d = n // 2, n % 2
                    v.wait_ge(hx_exp, 2 * lev + 2)
                    if lev >= 2:
                        v.wait_ge(ha_ready, lev - 1)
                    q, k = hq[:, h, :], hz[d][:, h, 0:T]
                    for part, src, done in ((slice(half, 2 * half), k if d else q, hx_up), (slice(0, half), q if d else k, hx_lo)):
                        nc.vector.tensor_tensor(halves(xl[lev % 2][:], 2 * half)[:, :, part], halves(src, 2 * half)[:, :, part],
                                                halves(yl[lev % 3][:], 2 * half)[:, :, part], ALU.mult).then_inc(done, 1)

                def states(n):
                    h, d = n // 2, n % 2
                    v.wait_ge(hkv_ready, n + 1)
                    if h:
                        v.wait_ge(ho_ready, h)
                    for u in range(5):
                        kv = pm[0][:, 1, P * u:P * u + P] if u < 4 else pa[3][:, P:2 * P]
                        if u == 0:
                            nc.vector.tensor_copy(st[d][:, 0, :], kv).then_inc(hs_done, 1)
                        else:
                            v.wait_ge(hs_done, 5 * n + u)
                            c = HG_ORDER[d][u]
                            nc.vector.scalar_tensor_tensor(st[d][:, u, :], st[d][:, u - 1, :], epend[:, d, h, c:c + 1], kv, ALU.mult, ALU.add).then_inc(hs_done, 1)

                for lev in range(LEVELS * HG_N):
                    h, m = lev // (2 * LEVELS), lev % (2 * LEVELS)
                    if m == 0:
                        v.wait_ge(hd_ready, h + 1)
                        if h >= 2:
                            v.wait_ge(ho_ready, h - 1)
                        nc.vector.tensor_tensor(halves(ah[h % 2][:], P), halves(pm[1][:, 1, :], P),
                                                ident[:].rearrange("p (o t) -> p o t", o=1).to_broadcast([P, TT, P]), ALU.mult).then_inc(hd_copied, 1)
                    if m == 1:
                        v.wait_ge(hd_copied, h + 1)
                    level_x(lev)
                    if lev >= 2:
                        level_a(lev - 2)
                    if h and m == 3:
                        output(h - 1)
                    if m % LEVELS == 6:
                        states(lev // LEVELS)
                    if h and m == 9:
                        hgrn_norm(h - 1)
                level_a(LEVELS * HG_N - 2)
                level_a(LEVELS * HG_N - 1)
                output(HG_HEADS - 1)
                hgrn_norm(HG_HEADS - 1)
                v.wait_ge(mod_turned, 2)
                for j in range(2):
                    nc.vector.tensor_tensor(modc[:, MOD_TILES1:, j], mod_columns(pm[1][:, 0, :], MOD_TILES - MOD_TILES1)[:, :, j],
                                            cols("b_mod", MOD_TILES1, MOD_TILES - MOD_TILES1), ALU.add).then_inc(pm_free[1], 1)
                v.wait_ge(pm_free[1], HG_USE + 2)
                nc.vector.scalar_tensor_tensor(wsc[:, 2, :], modc[:, KD * 4:KD * 5, 0], 1.0, cols("norm2", 0, KD), ALU.add, ALU.mult).then_inc(pm_free[1], 1)
                v.wait_ge(pm_free[1], HG_USE + 3)
                v.sem_inc(pm_free[1], 1)

            def first():
                lower_bounds()
                dve_squares(v, 0, CT)
                dve_rstd(v, 0, CT, cstd, crstd)
                dve_squares(v, 1)
                dve_rstd(v, 1)
                v.wait_ge(mod_turned, 1)
                for j in range(2):
                    if j:
                        v.wait_ge(mod_done, 1)
                    nc.vector.tensor_tensor(modc[:, 0:MOD_TILES1, j], mod_columns(pa[1], MOD_TILES1)[:, :, j],
                                            cols("b_mod", 0, MOD_TILES1), ALU.add).then_inc(pm_free[1] if j else mod_done, 1)
                v.wait_ge(pm_free[1], 1)
                v.wait_ge(mod_done, 1)
                for i, j in enumerate((1, 0)):
                    nc.vector.scalar_tensor_tensor(wsc[:, i, :], modc[:, KD:2 * KD, j], 1.0, cols("norm1", 0, KD), ALU.add, ALU.mult).then_inc(mod_done, 1)
                v.sem_inc(mod_done, 2)
                v.wait_ge(mod_done, 5)
                dve_norm(v, 0, 0, lambda k: wsc[:, 0, k:k + 1], None, cx, CT, ch, cl, lambda k: mod_col(0, k, 1))
                dve_norm(v, 1, 1, lambda k: wsc[:, 1, k:k + 1], shift=lambda k: mod_col(0, k))
                mlstm()
                hgrn()
                for i in range(OUT1_SLABS):
                    p = i % 2
                    v.wait_ge(slab_used, OUT1_AT + i + 1)
                    for t in range(2):
                        k = 2 * i + t
                        if t:
                            v.wait_ge(x_mixed, i + 1)
                        nc.vector.scalar_tensor_tensor(x[:, k, :], pm[p][:, t, :], mod_col(2, k), x[:, k, :], ALU.mult, ALU.add).then_inc(
                            pm_free[p] if t else x_mixed, 1)
                dve_squares(v, 2)
                dve_norm(v, 2, 2, lambda k: wsc[:, 2, k:k + 1], shift=lambda k: mod_col(3, k))
                with v.Fori(0, UP_STEPS) as j:
                    for b in range(2):
                        for q, tap in enumerate(t_ for t_ in range(9) if t_ != 4):
                            for i in range(2):
                                c0 = CONV1 + 16 * b + 32 * j
                                src, at = tap_views(image(img[b][:, i, :]), tap)
                                dst = image(sil[b][:, i, :])[:, at[0], at[1]]
                                if q:
                                    v.wait_ge(conv_step, c0 + 2 * q + i - 1)
                                elif i == 0:
                                    v.wait_ge(img_filled, 2 + 3 * b + 6 * j)
                                else:
                                    v.wait_ge(pm_free[b], UP1_USE + 1 + j)
                                w = col[:, bass.ds(COL_AT["ffn_conv"] + 2 * KF * tap + KF * b + i + 2 * j, 1)]
                                nc.vector.scalar_tensor_tensor(dst, src, w, dst, ALU.mult, ALU.add).then_inc(conv_step, 1)
                    v.wait_ge(usilu_done, 1 + j)
                    v.wait_ge(conv_step, CONV1 + 32 + 32 * j)
                    nc.vector.tensor_tensor(sil[1][:], sil[0][:], sil[1][:], ALU.mult).then_inc(up_product, 1)

                def add_gated(i, k):
                    xs, g2 = x[:, bass.ds(k, 1), :], modc[:, bass.ds(KD * 5 + k, 1), 0]
                    nc.vector.scalar_tensor_tensor(xs, pm[i][:, 0:1, :], g2, xs, ALU.mult, ALU.add).then_inc(pm_free[i], 1)

                dve_down(v, 3, DOWN1_AT, add_gated)
                n = NORMS1
                dve_rstd(v, n - 1)
                for k in range(KD + 1):
                    if k < KD:
                        nc.vector.scalar_tensor_tensor(x[:, k, :], x[:, k, :], cols("final_norm", k), rstd[:], ALU.mult, ALU.mult).then_inc(hn_done, 1)
                    if k:
                        dve_low(v, n, k - 1, ffn_gain(0, 0))
                        dve_square(v, n, (k - 1) % 2, 8 * n + k, k == 1)
                v.sem_inc(hn_done, KD)

            first()

            def ffn(l, f):
                s0, u0 = ffn_slab(l, f), ffn_use(l, f)
                n = NORMS1 + 3 * l + 2 * f
                dve_rstd(v, n)
                root = rstd[:].rearrange("p (o t) -> p o t", o=1).to_broadcast([P, 2, T])
                q = UP_STEPS * (1 + 2 * l + f)
                d0 = 1 + 2 * q
                with v.Fori(0, UP_STEPS) as j:
                    v.wait_ge(hidden_done, d0 + 2 * j)
                    v.wait_ge(slab_used, s0 + 1 + 2 * j)
                    nc.vector.tensor_tensor(sil[0][:], pm[0][:], root, ALU.mult).then_inc(pm_free[0], 1)
                    v.wait_ge(slab_used, s0 + 2 + 2 * j)
                    nc.vector.tensor_tensor(ut[:], pm[1][:], root, ALU.mult).then_inc(pm_free[1], 1)
                    v.wait_ge(pm_free[1], u0 + 1 + j)
                    v.wait_ge(usilu_done, q + 1 + j)
                    nc.vector.tensor_tensor(ut[:], sil[0][:], ut[:], ALU.mult).then_inc(up_product, 1)
                    v.wait_ge(up_product, q + 1 + j)
                    v.sem_inc(vtick, 1)
                    nc.vector.tensor_copy(uh[:, bass.ds(2 * j, 2), :], ut[:]).then_inc(hidden_done, 1)
                    v.wait_ge(hidden_done, d0 + 1 + 2 * j)
                    nc.vector.tensor_tensor(ul[:, bass.ds(2 * j, 2), :], ut[:], uh[:, bass.ds(2 * j, 2), :].bitcast(F32), ALU.subtract).then_inc(hidden_done, 1)
                s1, u1 = s0 + 2 * UP_STEPS, u0 + UP_STEPS

                def add_half(i, k):
                    xs = x[:, bass.ds(k, 1), :]
                    nc.vector.scalar_tensor_tensor(xs, pm[i][:, 0:1, :], 0.5, xs, ALU.mult, ALU.add).then_inc(pm_free[i], 1)

                dve_down(v, n + 1, s1, add_half, ffn_gain(1, 0) if f and not l else None)

            def mix(l):
                s0, u0 = mix_slab(l), mix_use(l)
                for p in range(2):
                    v.wait_ge(pm_free[p], u0)
                nc.vector.memset(wpool[:], 0.0).then_inc(mixc_made, 1)
                nc.vector.memset(zero[:], 0.0).then_inc(mixc_made, 1)
                nc.vector.memset(lowest[:], -1e30).then_inc(mixc_made, 1)
                nc.vector.memset(u[:, :, 0:PAD], 0.0).then_inc(mixc_made, 1)
                n = NORMS1 + 3 * l + 1
                dve_norm(v, n, n - 1, gains(GAINS["mix"] + 8 * l))
                v.wait_ge(mixc_loaded, 16 * 11 * (l + 1))
                v.wait_ge(mixc_made, 4 * l + 4)
                for h in range(SB_HEADS):
                    m = TT * (SB_HEADS * l + h)
                    hp = slice(64 * (h % 2), 64 * (h % 2) + 64)
                    for j in range(TT):
                        c = slice(LIVE_AT[j], LIVE_AT[j] + LIVE[j])
                        v.wait_ge(ln_done, m + j + 1)
                        if m + j >= TT:
                            v.wait_ge(logw_ready, m)
                        nc.vector.scalar_tensor_tensor(sp_[:, c], pa[j][:, 0:LIVE[j]], 0.0, sc[:, c], ALU.max, ALU.add).then_inc(sp_done, 1)
                        v.wait_ge(sp_done, m + j + 1)
                        nc.vector.copy_predicated(sp_[:, LIVE_AT[j]:LIVE_AT[j] + P], dmask[:].bitcast(mybir.dt.uint32), zero[:]).then_inc(sp_masked, 1)
                    for n_, j in enumerate(reversed(range(TT))):
                        v.wait_ge(logw_ready, m + n_ + 1)
                        nc.vector.copy_predicated(pa[j][:, 0:P], dmask[:].bitcast(mybir.dt.uint32), lowest[:]).then_inc(w_masked, 1)
                    v.wait_ge(sb_out, SB_HEADS * l + h + 1)
                    nc.vector.tensor_copy(ysb_h[hp, h // 2, :], pm[0][hp, 0, :]).then_inc(sb_hi, 1)
                    v.wait_ge(sb_hi, SB_HEADS * l + h + 1)
                    nc.vector.tensor_tensor(ysb_l[hp, h // 2, :], pm[0][hp, 0, :], ysb_h[hp, h // 2, :].bitcast(F32), ALU.subtract).then_inc(pm_free[0], 1)
                v.wait_ge(pm_free[1], u0 + 3)
                for i, dst in enumerate((q_r, k_r)):
                    for g in range(2):
                        m = 4 * l + 2 * i + g
                        if m:
                            v.wait_ge(rot_done, m)
                        nc.vector.tensor_tensor(rt1[:], rraw[i][:, g, :], rope[:, 0, :], ALU.mult).then_inc(rot_made, 1)
                        v.wait_ge(swapped, m + 1)
                        nc.vector.tensor_tensor(rt2[:], pa[2 * i + g][:], rope[:, 1, :], ALU.mult).then_inc(rot_made, 1)
                        v.wait_ge(rot_made, 2 * m + 2)
                        nc.vector.tensor_tensor(dst[:, g, :], rt1[:], rt2[:], ALU.add).then_inc(rot_done, 1)
                lo, hi = slice(0, 64), slice(64, 128)
                w0 = 5 * l
                v.wait_ge(pm_free[1], u0 + FILL_USE + 5)
                v.wait_ge(rot_done, 4 * l + 4)
                W = PAD + T
                nc.vector.tensor_copy(pw[0][:, :, 0:1], u[:, :, 0:1]).then_inc(win_done, 1)
                nc.vector.tensor_tensor(pw[0][:, :, 1:W], u[:, :, 1:W], u[:, :, 0:W - 1], ALU.add).then_inc(win_done, 1)
                v.wait_ge(win_done, w0 * 2 + 2)
                nc.vector.tensor_copy(pw[1][:, :, 0:2], pw[0][:, :, 0:2]).then_inc(win_done, 1)
                nc.vector.tensor_tensor(pw[1][:, :, 2:W], pw[0][:, :, 2:W], pw[0][:, :, 0:W - 2], ALU.add).then_inc(win_done, 1)
                v.wait_ge(win_done, w0 * 2 + 4)
                nc.vector.tensor_copy(pw[0][hi, 0, :], pw[1][hi, 0, :]).then_inc(win_done, 1)
                nc.vector.tensor_copy(pw[0][:, 1, 0:4], pw[1][:, 1, 0:4]).then_inc(win_done, 1)
                nc.vector.tensor_tensor(pw[0][:, 1, 4:W], pw[1][:, 1, 4:W], pw[1][:, 1, 0:W - 4], ALU.add).then_inc(win_done, 1)
                v.wait_ge(win_done, w0 * 2 + 7)
                nc.vector.tensor_copy(pw[1][hi, 1, 0:8], pw[0][hi, 1, 0:8]).then_inc(win_done, 1)
                nc.vector.tensor_tensor(pw[1][hi, 1, 8:W], pw[0][hi, 1, 8:W], pw[0][hi, 1, 0:W - 8], ALU.add).then_inc(win_done, 1)
                v.wait_ge(win_done, w0 * 2 + 9)
                nc.vector.tensor_copy(pw[0][hi, 1, :], pw[1][hi, 1, :]).then_inc(win_done, 1)
                v.wait_ge(win_done, w0 * 2 + 10)
                d0 = 6 * l
                for g in range(2):
                    for s, w in ((lo, POOL_WINDOWS[2 * g]), (hi, POOL_WINDOWS[2 * g + 1])):
                        nc.vector.scalar_tensor_tensor(pd[s, g, PAD:], pw[0][s, g, 2 * PAD:], 1.0 / w, u[s, g, 2 * PAD:], ALU.mult, ALU.subtract).then_inc(pd_done, 1)
                nc.vector.tensor_tensor(pd[:, :, 0:PAD], pw[0][:, :, PAD:2 * PAD], invcnt[:], ALU.mult).then_inc(pd_done, 1)
                v.wait_ge(pd_done, d0 + 5)
                nc.vector.tensor_tensor(pd[:, :, 0:PAD], pd[:, :, 0:PAD], u[:, :, PAD:2 * PAD], ALU.subtract).then_inc(pd_done, 1)
                v.wait_ge(pool_scaled, 2 * l + 2)
                nc.vector.tensor_copy(yp_h[:], pt[:]).then_inc(pool_hi, 1)
                v.wait_ge(pool_hi, l + 1)
                nc.vector.tensor_tensor(yp_l[:], pt[:], yp_h[:].bitcast(F32), ALU.subtract).then_inc(pool_done, 1)
                for h in range(RET_HEADS):
                    m = RET_HEADS * l + h
                    p = h % 2
                    for j in range(TT):
                        v.wait_ge(s_ready, TT * m + j + 1)
                        if m >= 2:
                            v.wait_ge(ret_out, m - 1)
                        nc.vector.tensor_tensor(aret[p][:, LIVE_AT[j]:LIVE_AT[j] + LIVE[j]], pa[j][:, 0:LIVE[j]], decay[:, h, 0:LIVE[j]], ALU.mult).then_inc(a_done, 1)
                    v.wait_ge(ret_std, m + 1)
                    nc.vector.reciprocal(ret_inv[:], ret_root[:]).then_inc(ret_rstd, 1)
                    v.wait_ge(ret_rstd, m + 1)
                    nc.vector.tensor_tensor(yraw[:, h, :], pm[p][:, 0, :], ret_inv[:], ALU.mult).then_inc(pm_free[p], 1)
                for i in range(2):
                    v.wait_ge(pm_free[0], u0 + RET_USE[0] + 2)
                    v.wait_ge(pm_free[1], u0 + RET_USE[1] + 2)
                    if i == 1 or l:
                        v.wait_ge(gr_done, 2 * l + i)
                    nc.vector.tensor_tensor(ut[:], sil[i][:], yraw[:, 2 * i:2 * i + 2, :], ALU.mult).then_inc(gr_prod, 1)
                    v.wait_ge(gr_prod, 2 * l + i + 1)
                    nc.vector.tensor_copy(yr_h[:, 2 * i:2 * i + 2, :], ut[:]).then_inc(gr_hi, 1)
                    v.wait_ge(gr_hi, 2 * l + i + 1)
                    nc.vector.tensor_tensor(yr_l[:, 2 * i:2 * i + 2, :], ut[:], yr_h[:, 2 * i:2 * i + 2, :].bitcast(F32), ALU.subtract).then_inc(gr_done, 1)
                r = [u0 + n for n in BRANCH_USE]
                b0, m0 = 2 * 4 * l, 1 + 3 * 4 * l
                with v.Fori(0, 4) as j:
                    v.wait_ge(mg_done, 1 + 4 * l + j)
                    v.wait_ge(pm_free[0], r[0] + 2 + 3 * j)
                    v.wait_ge(branch_out, b0 + 1 + 2 * j)
                    nc.vector.tensor_tensor(mg[:], gates[:, 0], pm[1][:], ALU.mult).then_inc(pm_free[1], 1)
                    v.wait_ge(branch_out, b0 + 2 + 2 * j)
                    nc.vector.tensor_tensor(mt[:], gates[:, 1], pm[0][:], ALU.mult).then_inc(pm_free[0], 1)
                    v.wait_ge(pm_free[1], r[1] + 2 + 3 * j)
                    v.wait_ge(pm_free[0], r[0] + 3 + 3 * j)
                    nc.vector.tensor_tensor(mg[:], mg[:], mt[:], ALU.add).then_inc(mix_sum, 1)
                    v.wait_ge(mix_sum, m0 + 1 + 3 * j)
                    v.wait_ge(slab_used, s0 + 14 + 4 * j)
                    nc.vector.tensor_tensor(mt[:], gates[:, 2], pm[1][:], ALU.mult).then_inc(pm_free[1], 1)
                    v.wait_ge(pm_free[1], r[1] + 3 + 3 * j)
                    nc.vector.tensor_tensor(mg[:], mg[:], mt[:], ALU.add).then_inc(mix_sum, 1)
                    v.wait_ge(mix_sum, m0 + 2 + 3 * j)
                    v.sem_inc(vtick, 1)
                    nc.vector.tensor_copy(mg_h[:, bass.ds(2 * j, 2), :], mg[:]).then_inc(mix_sum, 1)
                    v.wait_ge(mix_sum, m0 + 3 + 3 * j)
                    nc.vector.tensor_tensor(mg_l[:, bass.ds(2 * j, 2), :], mg[:], mg_h[:, bass.ds(2 * j, 2), :].bitcast(F32), ALU.subtract).then_inc(mg_done, 1)
                for m in range(KD // 2):
                    v.wait_ge(slab_used, s0 + 27 + m)
                    xs = x[:, 2 * m:2 * m + 2, :]
                    nc.vector.tensor_tensor(xs, xs, pm[m % 2][:], ALU.add).then_inc(pm_free[m % 2], 1)
                    for k in (2 * m, 2 * m + 1):
                        dve_low(v, n + 1, k, ffn_gain(l, 1))
                    for k in (2 * m, 2 * m + 1):
                        dve_square(v, n + 1, k % 2, 8 * (n + 1) + k + 1, k == 0)
                v.sem_inc(hn_done, KD)
                v.wait_ge(pm_free[0], u0 + MIX_USES - 2)
                v.sem_inc(pm_free[0], 2)

            for l in range(LAYERS):
                ffn(l, 0)
                mix(l)
                ffn(l, 1)
            n = NORMS1 + 3 * LAYERS
            dve_norm(v, n, n - 1, gains(GAINS["final"]), out=uh_f)
            for k in range(KD):
                v.wait_ge(out_tr, k + 1)
                nc.vector.tensor_copy(x[:, k, :], pa[k % 4][:]).then_inc(out_copied, 1)

        def mm3(out, wh, wl, ah, al, start, stop):
            nc.tensor.matmul(out, wh, ah, start=start, stop=False)
            nc.tensor.matmul(out, wh, al, start=False, stop=False)
            return nc.tensor.matmul(out, wl, ah, start=False, stop=stop)

        @block.tensor
        def _(pe):
            pe.wait_ge(const_loaded, 16 * 4)
            pe.wait_ge(const_made, 2)

            def norm(n, W=T):
                if n:
                    pe.wait_ge(std_done, n)
                pe.wait_ge(sq_added, 8 * n + KD)
                nc.tensor.matmul(pa[0][:, 0:W], ones[:], (std if n else cstd)[:, 0:W], start=True, stop=True).then_inc(sq_summed, 1)

            def slab_first(b, use, nh):
                for k in range(KD):
                    pe.wait_ge(hl_done, 8 * nh + k + 1)
                    for i in range(2):
                        c = slice(P * i, P * i + P)
                        last = mm3(pm[use][:, i, :], whi[b][:, k, c], wlo[b][:, k, c], hh[:, k, :], hl[:, k, :], k == 0, k == KD - 1)
                return last

            def slab_t(b, ah, al, use, n):
                for i in range(2):
                    c = slice(P * i, P * i + P)
                    for k in range(KD):
                        last = mm3(pm[use][:, i, :], whi[b][:, k, c], wlo[b][:, k, c], ah[:, k, :], al[:, k, :], k == 0, k == KD - 1)
                return last

            def slab_tok(b, use):
                for t in range(TT):
                    c = slice(P * t, P * t + P)
                    o = pm[use][:, t // 2, SLAB * (t % 2):SLAB * (t % 2) + SLAB]
                    for k in range(KD):
                        nc.tensor.matmul(o, hh[:, k, c], whi[b][:, k, :], start=k == 0, stop=False)
                        nc.tensor.matmul(o, hl[:, k, c], whi[b][:, k, :], start=False, stop=False)
                        last = nc.tensor.matmul(o, hh[:, k, c], wlo[b][:, k, :], start=False, stop=k == KD - 1)
                return last

            def ffn_products(s0, u0, nh, hidden, after, own=None):
                pe.wait_ge(split_done, s0 + 1)
                pe.wait_ge(pm_free[0], u0)
                slab_first(0, 0, nh).then_inc(slab_used, 1)
                if own is not None:
                    norm(own)
                pe.wait_ge(split_done, s0 + 2)
                pe.wait_ge(pm_free[1], u0)
                slab_t(1, hh, hl, 1, KD).then_inc(slab_used, 1)
                with pe.Fori(1, UP_STEPS) as j:
                    for b in range(2):
                        pe.wait_ge(split_done, s0 + b + 1 + 2 * j)
                        pe.wait_ge(pm_free[b], u0 + j)
                        slab_t(b, hh, hl, b, KD).then_inc(slab_used, 1)
                s1, u1 = s0 + 2 * UP_STEPS, u0 + UP_STEPS

                def down(j, first):
                    for b in range(2):
                        for i in range(2):
                            pe.wait_ge(split_done, s1 + 2 * b + i + 1 + 4 * j)
                            if b == 0:
                                pe.wait_ge(pm_free[i], u1 + j)
                            h, o = (a[i][:].rearrange("p k n -> p (k n)") for a in (whi, wlo))
                            for k in range(DOWN_K):
                                if first and i == 0 and (k == 0 or b == 1 and k == DOWN_K - 2):
                                    pe.wait_ge(hidden_done, 1 + hidden - 2 * UP_STEPS + (DOWN_K + 1 if b == 0 else 2 * UP_STEPS - 2 * (k == 0)))
                                c = slice(P * k, P * k + P)
                                last = mm3(pm[i][:, 0, :], h[:, c], o[:, c], uh[:, DOWN_K * b + k, :], ul[:, DOWN_K * b + k, :],
                                           b == 0 and k == 0, b == 1 and k == DOWN_K - 1)
                            last.then_inc(slab_used, 1)

                down(0, True)
                with pe.Fori(1, KD // 2) as j:
                    down(j, False)
                if after is not None:
                    norm(after)

            def ffn(l, f):
                n = NORMS1 + 3 * l + 2 * f
                ffn_products(ffn_slab(l, f), ffn_use(l, f), n - 1, 2 * UP_STEPS * (2 + 2 * l + f), None if f and l + 1 < LAYERS else n + 1, n)

            def context_t(b, p):
                for i in range(2):
                    c = slice(P * i, P * i + P)
                    for k in range(KD):
                        last = mm3(pa[p][:, CT * i:CT * i + CT], whi[b][:, k, c], wlo[b][:, k, c], ch[:, k, :], cl[:, k, :], k == 0, k == KD - 1)
                return last

            def context_tok(b, p):
                for t in range(CTT):
                    c = slice(P * t, P * t + P)
                    o = pa[p][:, SLAB * t:SLAB * t + SLAB]
                    for k in range(KD):
                        nc.tensor.matmul(o, ch[:, k, c], whi[b][:, k, :], start=k == 0, stop=False)
                        nc.tensor.matmul(o, cl[:, k, c], whi[b][:, k, :], start=False, stop=False)
                        last = nc.tensor.matmul(o, ch[:, k, c], wlo[b][:, k, :], start=False, stop=k == KD - 1)
                return last

            def in1(i):
                name, b, p = IN1[i][0], i % 2, IN1_P[i]
                pe.wait_ge(split_done, 2 + i + 1)
                if IN1_USE[i]:
                    pe.wait_ge(pm_free[p], IN1_USE[i])
                if IN1_CTX[i]:
                    pe.wait_ge(ctx_free[p], IN1_CTX[i])
                if name == "gate":
                    h, o = (a[b][:].rearrange("p k n -> p (k n)") for a in (whi, wlo))
                    for out, yh, yl_ in ((pm[p][:, 0, :], hh, hl), (pa[p][:, 0:CT], ch, cl)):
                        for k in range(KD // 2):
                            kk, c = KD // 2 * (i - 6) + k, slice(P * k, P * k + P)
                            last = mm3(out, h[:, c], o[:, c], yh[:, kk, :], yl_[:, kk, :], kk == 0, kk == KD - 1)
                elif name in ("mv", "hv"):
                    slab_tok(b, p)
                    last = context_tok(b, p)
                else:
                    last = slab_first(b, p, 1) if i == 0 else slab_t(b, hh, hl, p, KD)
                    if name in ("mk", "zf", "zb"):
                        last = context_t(b, p)
                last.then_inc(slab_used, 1)

            def modulation(first_, end):
                for i in range(first_, end):
                    if i < MOD_FIRST:
                        b, loads, out = i % len(modraw), i // len(modraw) + 1, pm[i // 4][0:2, i % 4 // 2, :]
                    else:
                        b, loads, out = i % 2, MOD_FIRST // len(modraw) + 1 + (i - MOD_FIRST) // 2 + 1, pm[1][0:2, 0, :]
                        if i % 2 == 0 and i > MOD_FIRST:
                            pe.wait_ge(mod_row, 2 + (i - MOD_FIRST) // 2)
                    pe.wait_ge(mod_loaded[b], 16 * loads)
                    for k in range(KD):
                        last = nc.tensor.matmul(out[:, SLAB * (i % 2):SLAB * (i % 2) + SLAB], silc[:, k, :], modraw[b][:, k, :], start=k == 0, stop=k == KD - 1)
                        if k == KD - 1:
                            last.then_inc(mod_used, 1)
                        yield

            def mod_turn(row, bank, n):
                for t in range(n):
                    last = nc.tensor.transpose(bank[:, 2 * t:2 * t + 2], row[:, P * t:P * t + P], ident[0:2, 0:2])
                last.then_inc(mod_turned, 1)

            def head_sum(e, h, bank):
                pe.wait_ge(t_sq, 4 * e + h + 1)
                nc.tensor.matmul(bank, ones[:], head_sq(e, h), start=True, stop=True).then_inc(t_ss, 1)

            def mlstm():
                pe.wait_ge(pm_free[0], IN1_USE[6] + 1)
                pe.wait_ge(ctx_free[0], IN1_CTX[6] + 1)
                for g in range(4):
                    if g:
                        pe.wait_ge(gsel_copied, 2 * g - 1)
                    nc.tensor.matmul(pa[2][0:4, :], ident[0:16, 4 * g:4 * g + 4], gall[:, 0:T], start=True, stop=True).then_inc(gsel_ready, 1)
                    if g:
                        pe.wait_ge(gsel_copied, 2 * g)
                    nc.tensor.matmul(pa[3][0:4, 0:CT], ident[0:16, 4 * g:4 * g + 4], gall[:, T:TA], start=True, stop=True).then_inc(gsel_ready, 1)
                in1(8)
                in1(9)
                pe.wait_ge(gsel_copied, 8)
                for d in range(2):
                    pe.wait_ge(gstep, 6 * d + 3)
                    for t in range(TAT):
                        at = LATC[d].start + P * t if t < TT else CTXC[d].start + P * (t - TT)
                        o = (d * TAT + t) * ML_HEADS
                        last = nc.tensor.transpose(pa[2][:, o:o + ML_HEADS], GI[d][:, at:at + P], ident[0:4, 0:4])
                last.then_inc(gtr, 1)
                pe.wait_ge(gcol_done, 1)
                pe.wait_ge(gdn, 2)
                pe.wait_ge(conv_silu, 8)
                pe.wait_ge(ctx_free[0], IN1_CTX[6] + 1)
                pe.wait_ge(ctx_free[1], IN1_CTX[5] + 1)
                pe.wait_ge(pm_free[1], IN1_USE[5] + 1)

                def scores(s):
                    h, i = s // TAT, s % TAT
                    if s >= 2:
                        pe.wait_ge(a_made, 2 * s - 2)
                    at = T + P * i if i < 2 else P * (i - 2)
                    nc.tensor.matmul(pa[s % 2][:], mk[:, h, at:at + P], mq[:, h, :], start=True, stop=True).then_inc(ms_ready, 1)

                scores(0)
                for h in range(ML_HEADS):
                    for d in range(2):
                        n = 2 * h + d
                        if h:
                            pe.wait_ge(mb_copied, 2 * n - 2)
                        if h >= 2:
                            pe.wait_ge(t_std, h - 1)
                        nc.tensor.matmul(pa[2 + d][:], bsel[:, h, :], GT[d][:, LATC[d]], start=True, stop=True).then_inc(mb_ready, 1)
                        pe.wait_ge(mb_copied, 2 * n + 1)
                        nc.tensor.matmul(pa[2 + d][:], bsel[:, h, :], GF[d][:, LATC[d]], start=True, stop=True).then_inc(mb_ready, 1)
                    for i in range(TAT):
                        s = TAT * h + i
                        if s + 1 < TAT * ML_HEADS:
                            scores(s + 1)
                        for d in range(2):
                            r = 2 * s + d
                            if i == 0:
                                pe.wait_ge(pm_free[d], ML_USE + h)
                            if i < 2:
                                pe.wait_ge(a_made, r + 1)
                                c, st_ = slice(0, T), TT + i
                            else:
                                pe.wait_ge(a_masked, 8 * h + 2 * (i - 2) + d + 1)
                                c, st_ = live(d, i - 2), i - 2
                            a = aw[d][s % 2][:, c]
                            nc.tensor.matmul(pm[d][:, 0, c], mv[:, st_, P * h:P * h + P], a, start=i == 0, stop=i == TAT - 1).then_inc(nd_acc, 1)
                        if h and i == 3:
                            head_sum(0, h - 1, pa[2][:])
                    for d in range(2):
                        pe.wait_ge(a_added, 10 * h + 8 + d + 1)
                        nc.tensor.matmul(pm[d][:, 1, :], ones[:], asum[d][:], start=True, stop=True).then_inc(den_ready, 1)
                in1(10)
                head_sum(0, ML_HEADS - 1, pa[2][:])

            def hgrn():
                for p in range(2):
                    pe.wait_ge(pm_free[p], HG_USE)
                    pe.wait_ge(ctx_free[p], ctx_uses_[p])
                rest = modulation(MOD_FIRST, MOD_SLABS)
                pe.wait_ge(hg_step, 2 + 19 + 8)
                def diagonal(h):
                    if h:
                        pe.wait_ge(hd_copied, h)
                    for c in range(TT):
                        cs = slice(P * c, P * c + P)
                        for e in range(2):
                            last = nc.tensor.matmul(pm[1][:, 1, cs], hz[e][:, h, cs], hq[:, h, cs], start=e == 0, stop=e == 1)
                    last.then_inc(hd_ready, 1)

                def output(h):
                    n = 2 * h + 1
                    pe.wait_ge(hs_done, 5 * n + 5)
                    pe.wait_ge(ha_copied, LEVELS * (n + 1))
                    pe.wait_ge(hkq, 2 * n + 2)
                    if h:
                        pe.wait_ge(pm_free[0], HG_USE + h)
                        pe.wait_ge(t_std, 4 + h)
                    for c in range(TT):
                        cs = slice(P * c, P * c + P)
                        o = pm[0][:, 0, cs]
                        nc.tensor.matmul(o, hv[:, c, P * h:P * h + P], ah[h % 2][:, cs], start=True, stop=False)
                        nc.tensor.matmul(o, st[0][:, 1 + c, :], qt[0][:, cs], start=False, stop=False)
                        last = nc.tensor.matmul(o, st[1][:, 1 + TT - 1 - c, :], qt[1][:, cs], start=False, stop=True)
                    last.then_inc(ho_ready, 1)

                diagonal(0)
                for lev in range(LEVELS * HG_N):
                    n, m = lev // LEVELS, lev % LEVELS
                    h, d = n // 2, n % 2
                    pe.wait_ge(hx_up, lev + 1)
                    pe.wait_ge(hx_lo, lev + 1)
                    if lev >= 2:
                        pe.wait_ge(ha_copied, lev - 1)
                    half = 2 ** m
                    for c in range(TT):
                        last = nc.tensor.matmul(pa[lev % 2][:, P // 2 * c:P // 2 * c + P // 2].rearrange("p (b w) -> p b w", w=half),
                                                xl[lev % 2][:, P * c:P * c + P], chunk_blocks(xl[lev % 2][:], half)[:, c, :, query_part(d, half)],
                                                start=True, stop=True)
                    last.then_inc(ha_ready, 1)
                    if h and d == 0 and m == 1:
                        output(h - 1)
                    if m == 2:
                        pe.wait_ge(hkq, 2 * n + 1)
                        if n:
                            pe.wait_ge(ht_copied, 2 * n)
                            pe.wait_ge(hs_done, 5 * n)
                        for u, c in enumerate(HG_ORDER[d]):
                            o = pa[2][:, P * u:P * u + P] if u < 4 else pa[3][:, 0:P]
                            last = nc.tensor.transpose(o, kt[:, P * c:P * c + P], ident[:])
                            if u >= 3:
                                last.then_inc(ht_ready, 1)
                    if m == 4:
                        pe.wait_ge(ht_copied, 2 * n + 2)
                        for u, c in enumerate(HG_ORDER[d]):
                            o = pm[0][:, 1, P * u:P * u + P] if u < 4 else pa[3][:, P:2 * P]
                            last = nc.tensor.matmul(o, ktok[:, u, :], hv[:, c, P * h:P * h + P], start=True, stop=True)
                        last.then_inc(hkv_ready, 1)
                    if d == 1 and m == 5 and h + 1 < HG_HEADS:
                        diagonal(h + 1)
                    if h and d == 0 and m == 5:
                        head_sum(1, h - 1, pm[0][:, 0, :])
                    for _ in range(MOD_REST[m]):
                        next(rest)
                output(HG_HEADS - 1)
                pe.wait_ge(mod_row, 2 + HG_N)
                mod_turn(modrow[1], pm[1][:, 0, :], MOD_TILES - MOD_TILES1)
                head_sum(1, HG_HEADS - 1, pm[0][:, 0, :])

            def first():
                norm(0, CT)
                norm(1)
                pe.wait_ge(mod_in, 1)
                for _ in modulation(0, MOD_FIRST):
                    pass
                pe.wait_ge(mod_row, 2)
                mod_turn(modrow[0], pa[1], MOD_TILES1)
                for i in range(8):
                    in1(i)
                mlstm()
                for i in range(11, IN1_SLABS):
                    in1(i)
                hgrn()
                pe.wait_ge(t_done, 1)
                pe.wait_ge(t_std, 8)
                for i in range(OUT1_SLABS):
                    b = i % 2
                    pe.wait_ge(split_done, OUT1_AT + i + 1)
                    pe.wait_ge(pm_free[b], OUT1_USE + i // 2)
                    for k in range(KD):
                        if i == 0 and k >= 3:
                            pe.wait_ge(t_done, k - 2)
                        for t in range(2):
                            c = slice(P * t, P * t + P)
                            yh, yl_ = (ym_h[:, k], ym_l[:, k]) if k < 4 else (yh_h[:, k - 4, 0:T], yh_l[:, k - 4, 0:T])
                            last = mm3(pm[b][:, t, :], whi[b][:, k, c], wlo[b][:, k, c], yh, yl_, k == 0, k == KD - 1)
                    last.then_inc(slab_used, 1)
                norm(2)
                ffn_products(UP1_AT, UP1_USE, 2, 2 * UP_STEPS, 3)

            def mix(l):
                s0, u0 = mix_slab(l), mix_use(l)
                n = NORMS1 + 3 * l + 1
                def slab(i, p, use):
                    b = i % 2
                    pe.wait_ge(split_done, s0 + i + 1)
                    pe.wait_ge(pm_free[p], u0 + use)
                    last = slab_first(b, p, n - 1) if i == 0 else slab_tok(b, p) if i in (2, 5, 6) else slab_t(b, hh, hl, p, KD)
                    last.then_inc(slab_used, 1)

                slab(0, 0, 0)
                slab(1, 1, 0)
                slab(2, 0, 1)
                pe.wait_ge(mixc_loaded, 16 * 11 * (l + 1))
                pe.wait_ge(pm_free[0], u0 + 1)
                pe.wait_ge(pm_free[1], u0 + 1)
                for h in range(SB_HEADS):
                    hp = slice(64 * (h % 2), 64 * (h % 2) + 64)
                    m = TT * (SB_HEADS * l + h)

                    def scores(j, start):
                        return nc.tensor.matmul(pa[j][:, 0:LIVE[j]], k_sb[hp, h // 2, P * j:P * j + P], q_sb[hp, h // 2, P * j:],
                                                start=start, stop=True)

                    for j in range(TT):
                        if h:
                            pe.wait_ge(w_done, m - j)
                        scores(j, True).then_inc(z_ready, 1)
                    slab(3 + 2 * h, 1, FILL_USE + 2 * h)
                    for n_, j in enumerate(reversed(range(TT))):
                        if n_ == 0:
                            pe.wait_ge(sp_masked, m + TT)
                        for i in range(j, TT):
                            o = P * (i - j)
                            nc.tensor.matmul(pa[j][:, o:LIVE[j]], trineg[:] if i == j else onesneg[:],
                                             sp_[:, LIVE_AT[i]:LIVE_AT[i] + LIVE[i]], start=i == j, stop=False)
                        scores(j, False).then_inc(logw_ready, 1)
                    if h + 1 < SB_HEADS:
                        slab(4 + 2 * h, 1, FILL_USE + 2 * h + 1)
                    pe.wait_ge(pm_free[0], u0 + SB_USE + h)
                    pe.wait_ge(w_done, m + TT)
                    for j in range(TT):
                        last = nc.tensor.matmul(pm[0][hp, 0, P * j:], v_sb[:, j, 64 * h:64 * h + 64], w_[:, LIVE_AT[j]:LIVE_AT[j] + LIVE[j]],
                                                start=j == 0, stop=j == TT - 1)
                    last.then_inc(sb_out, 1)
                pe.wait_ge(pm_free[1], u0 + FILL_USE + 2)
                for i in range(2):
                    for g in range(2):
                        nc.tensor.matmul(pa[2 * i + g][:], perm[:], rraw[i][:, g, :], start=True, stop=True).then_inc(swapped, 1)
                slab(10, 0, GATE_USE[0])
                slab(11, 1, GATE_USE[1])
                pe.wait_ge(pd_done, 6 * l + 6)
                for g in range(2):
                    nc.tensor.matmul(pa[g][:], wpool[:, g, :], pd[:, g, :], start=True, stop=True).then_inc(pool_out, 1)
                for h in range(RET_HEADS):
                    hp = slice(64 * (h % 2), 64 * (h % 2) + 64)
                    m = RET_HEADS * l + h
                    p = h % 2
                    if h == 0:
                        pe.wait_ge(rot_done, 4 * l + 4)
                        pe.wait_ge(pool_scaled, 2 * l + 2)
                    for j in range(TT):
                        if h:
                            pe.wait_ge(a_done, TT * (m - 1) + j + 1)
                        nc.tensor.matmul(pa[j][:, 0:LIVE[j]], k_r[hp, h // 2, P * j:P * j + P], q_r[hp, h // 2, P * j:],
                                         start=True, stop=True).then_inc(s_ready, 1)
                    pe.wait_ge(pm_free[p], u0 + RET_USE[p] + h // 2)
                    for j in range(TT):
                        pe.wait_ge(a_done, TT * m + j + 1)
                        last = nc.tensor.matmul(pm[p][:, 0, P * j:], v_r[:, j, P * h:P * h + P], aret[p][:, LIVE_AT[j]:LIVE_AT[j] + LIVE[j]],
                                                start=j == 0, stop=j == TT - 1)
                    last.then_inc(ret_out, 1)
                    pe.wait_ge(ret_sq, m + 1)
                    nc.tensor.matmul(pm[p][:, 1, :], ones[:], ret_sqr[:], start=True, stop=True).then_inc(ret_ss, 1)
                slab(12, 0, BRANCH_USE[0] + 1)
                r = [u0 + n for n in BRANCH_USE]
                pe.wait_ge(gr_done, 2 * l + 2)

                def branches(j):
                    pe.wait_ge(split_done, s0 + 14 + 4 * j)
                    for p, n, k0, nk, yh, yl in ((1, 1, 0, 2, ysb_h, ysb_l), (0, 2, 2, 4, yr_h, yr_l), (1, 2, 6, 2, yp_h, yp_l)):
                        pe.wait_ge(pm_free[p], r[p] + n + 3 * j)
                        for i in range(2):
                            c = slice(P * i, P * i + P)
                            for k in range(nk):
                                last = mm3(pm[p][:, i, :], whi[1][:, k0 + k, c], wlo[1][:, k0 + k, c], yh[:, k, :], yl[:, k, :], k == 0, k == nk - 1)
                        last.then_inc(slab_used if k0 == 6 else branch_out, 1)

                branches(0)
                with pe.Fori(1, 4) as j:
                    for g in range(3):
                        pe.wait_ge(split_done, s0 + 11 + g + 4 * j)
                        pe.wait_ge(pm_free[g % 2], r[g % 2] + g // 2 + 3 * j)
                        slab_t(g % 2, hh, hl, g % 2, KD).then_inc(slab_used, 1)
                    branches(j)
                for m in range(KD // 2):
                    b = m % 2
                    pe.wait_ge(split_done, s0 + 27 + m)
                    pe.wait_ge(pm_free[b], r[b] + 12 + m // 2)
                    if m:
                        last = slab_t(b, mg_h, mg_l, b, KD)
                    else:
                        for k in range(KD):
                            pe.wait_ge(mg_done, 1 + 4 * l + k // 2 + 1)
                            for i in range(2):
                                c = slice(P * i, P * i + P)
                                last = mm3(pm[b][:, i, :], whi[b][:, k, c], wlo[b][:, k, c], mg_h[:, k, :], mg_l[:, k, :], k == 0, k == KD - 1)
                    last.then_inc(slab_used, 1)

            first()
            for l in range(LAYERS):
                ffn(l, 0)
                mix(l)
                ffn(l, 1)
            n = NORMS1 + 3 * LAYERS
            for k in range(KD):
                pe.wait_ge(hn_done, 8 * n + k + 1)
                if k >= 4:
                    pe.wait_ge(out_copied, k - 3)
                for t in range(TT):
                    last = nc.tensor.transpose(pa[k % 4][:, P * t:P * t + P], uh_f[:, k, P * t:P * t + P], ident[:])
                last.then_inc(out_tr, 1)


def constants():
    c = {}
    c["c_ident"] = np.eye(P, dtype=np.float32)
    j, i = np.meshgrid(np.arange(P), np.arange(P), indexing="xy")
    c["c_trineg"] = -(i >= j).astype(np.float32)
    c["c_onesneg"] = -np.ones((P, P), np.float32)
    c["c_dmask"] = (i >= j).astype(np.float32)
    f = np.float32
    half = RET_DIM // 2
    inv = f(10000.0) ** (-np.arange(half, dtype=f) / f(half))
    ang = np.arange(T, dtype=f)[:, None] * inv[None, :]
    cos, sin = np.cos(ang).T, np.sin(ang).T
    c["c_rope"] = np.ascontiguousarray(np.stack([np.tile(cos, (4, 1)), np.tile(sin, (4, 1))], 1).astype(f))
    perm = np.zeros((P, P), f)
    for h in range(2):
        for a in range(half):
            perm[64 * h + half + a, 64 * h + a] = -1.0
            perm[64 * h + a, 64 * h + half + a] = 1.0
    c["c_perm"] = perm
    lg = np.log(1.0 - 2.0 ** (-5.0 - np.arange(RET_HEADS, dtype=np.float64)))
    diff = (np.arange(T)[None, :] - np.arange(P)[:, None]).astype(np.float64)
    dec = np.where(diff[:, None, :] >= 0, np.exp(np.maximum(diff, 0)[:, None, :] * lg[None, :, None]), 0.0)
    c["c_decay"] = np.ascontiguousarray(dec.astype(f))
    c["c_bsel"] = np.ascontiguousarray(np.repeat(np.eye(ML_HEADS, dtype=f)[:, :, None], P, 2))
    c["c_mlmask"] = np.ascontiguousarray(np.stack([(i <= j), (i >= j)], 1).astype(f))
    levels = []
    for d in range(2):
        s, t = (i, j) if d == 0 else (j, i)
        for m in range(LEVELS):
            level = (s >> (m + 1) == t >> (m + 1)) & (s >> m & 1 == 0) & (t >> m & 1 == 1)
            queries = np.arange(P) >> m & 1 == 1 - d
            levels.append(level[:, queries])
    c["c_hgmask"] = np.ascontiguousarray(np.stack(levels, 1).astype(f))
    win = np.repeat(np.array(POOL_WINDOWS), 64).reshape(2, P)
    cnt = np.minimum(np.arange(PAD)[None, None, :] + 1, win.T[:, :, None])
    c["c_invcnt"] = np.ascontiguousarray((1.0 / cnt).astype(f))
    return c


def packed(g):
    gate = np.zeros((4, P), np.float32)
    gate[:, 0:ML_HEADS] = g["mlstm_gate_b"][0].reshape(4, ML_HEADS)
    rows = [g["g_ffn1_2"], g["g_mix_2"], g["g_ffn2_2"], g["g_final_2"], g["pool_scale_2"], g["norm1_w"], g["norm2_w"], g["final_norm_w"],
            np.stack([g["c"][0].reshape(KD, P), g["c_ctx"].reshape(KD, P)], 1), g["mlstm_norm_w"], g["hgrn_norm_w"], g["hgrn_lb_logits"],
            g["b_mod"], g["mlstm_conv_w"], g["ffn_conv_w"], gate]
    return np.ascontiguousarray(np.concatenate([r.reshape(-1, P) for r in rows]).T)


def kernel(**inputs):
    import concourse.bacc as bacc
    from concourse.bass_utils import run_bass_kernel_spmd as run

    nc = bacc.Bacc("TRN2", target_bir_lowering=False, num_devices=1)
    arrays, io = {}, {}
    given = {k: np.ascontiguousarray(v) for k, v in inputs.items()}
    given["cols"] = packed(given)
    given["xT"] = np.ascontiguousarray(given.pop("x")[0].T)
    given["ctxT"] = np.ascontiguousarray(given.pop("ctx")[0].T)
    given.update(constants())
    for name, a in given.items():
        arrays["in_" + name] = a
        io[name] = nc.dram_tensor("in_" + name, a.shape, mybir.dt.from_np(a.dtype), kind="ExternalInput").ap()
    io["out"] = nc.dram_tensor("out_0", (1, T, D), F32, kind="ExternalOutput").ap()
    build(nc, io)
    r = run(nc, [arrays], core_ids=[0])
    return r.results[0]["out_0"]
```
